# Optimizing a Trainium2 kernel written in Bass

```python
import math
import jax, jax.numpy as jnp
from jax import lax
import numpy as np

D_MODEL = 1024
BATCH = 1
SEQ = 512
DEPTH = 2
DEC_BATCH = 8
DEC_SEQ = 8
PAST_LEN = 1024
PAGE_SIZE = 128

N_META = 16
N_BRANCH = 4
BRANCH_W = 256
D_FF = 2816
CONV_C = 256
CONV_K = 31
RET_HEADS = 4
RET_DK = 64
RET_DV = 64
GLA_HEADS = 4
GLA_DK = 32
GLA_DV = 64
GLA_RANK = 16
GLA_TAU = 16.0
DIFF_HEADS = 4
DIFF_HD = 32
DIFF_VD = 2 * DIFF_HD
REL_BUCKETS = 32
REL_MAX_DIST = 128
CHUNK = 128
Q_BLOCK = 128
ROPE_BASE = 10000.0
EPS = 1e-6
IN_SIZES = (CONV_C, CONV_C,
            RET_HEADS * RET_DK, RET_HEADS * RET_DK, RET_HEADS * RET_DV, RET_HEADS * RET_DV,
            GLA_HEADS * GLA_DK, GLA_HEADS * GLA_DK, GLA_HEADS * GLA_DV, GLA_HEADS * GLA_DV, GLA_RANK,
            DIFF_HEADS * 2 * DIFF_HD, DIFF_HEADS * 2 * DIFF_HD, DIFF_HEADS * DIFF_VD,
            N_BRANCH * D_MODEL)
N_IN = sum(IN_SIZES)

kernel_name = "hybrid_gated_branch_decoder_step"

def rmsnorm(x, g):
    xf = x.astype(jnp.float32)
    y = xf * lax.rsqrt(jnp.mean(xf * xf, axis=-1, keepdims=True) + EPS)
    return (y * g.astype(jnp.float32)).astype(x.dtype)

def layernorm(x, g, b):
    xf = x.astype(jnp.float32)
    mu = jnp.mean(xf, axis=-1, keepdims=True)
    xc = xf - mu
    y = xc * lax.rsqrt(jnp.mean(xc * xc, axis=-1, keepdims=True) + EPS)
    return (y * g.astype(jnp.float32) + b.astype(jnp.float32)).astype(x.dtype)

def head_norm(o, g, center):
    of = o.astype(jnp.float32)
    if center:
        of = of - jnp.mean(of, axis=-1, keepdims=True)
    y = of * lax.rsqrt(jnp.mean(of * of, axis=-1, keepdims=True) + EPS) * g.astype(jnp.float32)
    return y.reshape(o.shape[0], o.shape[1], -1).astype(o.dtype)

def swiglu(x, wg, wu, wd):
    return (jax.nn.silu(x @ wg) * (x @ wu)) @ wd

def rope(x, pos):
    half = x.shape[-1] // 2
    inv = ROPE_BASE ** (-jnp.arange(half, dtype=jnp.float32) / half)
    ang = pos.astype(jnp.float32)[:, None] * inv[None, :]
    cos = jnp.cos(ang)[None, :, None, :]
    sin = jnp.sin(ang)[None, :, None, :]
    xf = x.astype(jnp.float32)
    x1, x2 = xf[..., :half], xf[..., half:]
    return jnp.concatenate([x1 * cos - x2 * sin, x1 * sin + x2 * cos], axis=-1).astype(x.dtype)

def decayed_linear_attention(q, k, v, log_decay, state0, front_pad):
    B, L, H, _ = q.shape
    DV = v.shape[-1]
    total = L + front_pad
    c = min(CHUNK, total)
    n = -(-total // c)
    back = n * c - total

    def to_chunks(a):
        a = jnp.pad(a.astype(jnp.float32), ((0, 0), (front_pad, back), (0, 0), (0, 0)))
        return a.reshape(B, n, c, H, a.shape[-1]).transpose(1, 0, 3, 2, 4)

    qc, kc, vc, gc = to_chunks(q), to_chunks(k), to_chunks(v), to_chunks(log_decay)
    causal = jnp.tril(jnp.ones((c, c), dtype=bool))[None, None, :, :, None]

    def step(S, inp):
        qb, kb, vb, gb = inp
        b = jnp.cumsum(gb, axis=2)
        rel = b[:, :, :, None, :] - b[:, :, None, :, :]
        decay = jnp.exp(jnp.where(causal, rel, -jnp.inf))
        scores = jnp.sum(qb[:, :, :, None, :] * kb[:, :, None, :, :] * decay, axis=-1)
        o = (jnp.einsum('bhts,bhsv->bhtv', scores, vb)
             + jnp.einsum('bhtk,bhkv->bhtv', qb * jnp.exp(b), S))
        b_last = b[:, :, -1:, :]
        S_new = (jnp.exp(b_last[:, :, 0, :])[..., None] * S
                 + jnp.einsum('bhsk,bhsv->bhkv', kb * jnp.exp(b_last - b), vb))
        return S_new, o

    S_fin, o = lax.scan(step, state0.astype(jnp.float32), (qc, kc, vc, gc))
    o = o.transpose(1, 0, 3, 2, 4).reshape(B, n * c, H, DV)[:, front_pad:front_pad + L]
    return o.astype(v.dtype), S_fin.astype(state0.dtype)

def t5_bucket(rel):
    n = jnp.maximum(rel, 0)
    max_exact = REL_BUCKETS // 2
    nf = jnp.maximum(n, 1).astype(jnp.float32)
    large = max_exact + (jnp.log(nf / max_exact) / math.log(REL_MAX_DIST / max_exact)
                         * (REL_BUCKETS - max_exact)).astype(jnp.int32)
    large = jnp.minimum(large, REL_BUCKETS - 1)
    return jnp.where(n < max_exact, n, large)

def diff_attention(q1, q2, k1, k2, v, q_pos, k_pos, rel_bias, lam):
    B, Lq, H, d = q1.shape
    qb = min(Q_BLOCK, Lq)
    nb = -(-Lq // qb)
    padq = nb * qb - Lq

    def prep(a):
        a = jnp.pad(a, ((0, 0), (0, padq), (0, 0), (0, 0)))
        return a.reshape(B, nb, qb, H, d).transpose(1, 0, 2, 3, 4)

    pos_blocks = jnp.pad(q_pos, (0, padq), mode='edge').reshape(nb, qb)
    scale = d ** -0.5
    lam32 = lam.astype(jnp.float32)

    def block(args):
        a1, a2, p = args
        rel = p[:, None] - k_pos[None, :]
        bias = rel_bias[t5_bucket(rel)].transpose(2, 0, 1).astype(jnp.float32)
        mask = rel >= 0

        def probs(a, kk):
            s = jnp.einsum('bqhd,bkhd->bhqk', a, kk).astype(jnp.float32) * scale + bias
            return jax.nn.softmax(jnp.where(mask, s, -jnp.inf), axis=-1)

        attn = probs(a1, k1) - lam32 * probs(a2, k2)
        return jnp.einsum('bhqk,bkhv->bqhv', attn.astype(v.dtype), v)

    o = lax.map(block, (prep(q1), prep(q2), pos_blocks))
    return o.transpose(1, 0, 2, 3, 4).reshape(B, nb * qb, H, v.shape[-1])[:, :Lq]

def trunk_layer(h, pos, k_pos, front_pad, conv_past, ret_s0, gla_s0, k_past, v_past,
                rel_bias, lam_init, w):
    B, L, _ = h.shape
    h = h + 0.5 * swiglu(rmsnorm(h, w['norm_ffn1']), w['ffn1_gate'], w['ffn1_up'], w['ffn1_down'])
    x = rmsnorm(h, w['norm_mix'])
    z = x @ w['w_in'] + w['b_in']
    split_at = [int(s) for s in np.cumsum(IN_SIZES)[:-1]]
    (c_a, c_g, r_q, r_k, r_v, r_g, g_q, g_k, g_v, g_r, g_low,
     d_q, d_k, d_v, gates) = jnp.split(z, split_at, axis=-1)

    u = c_a * jax.nn.sigmoid(c_g)
    u_ext = jnp.concatenate([conv_past.astype(u.dtype), u], axis=1)
    conv = lax.conv_general_dilated(u_ext, w['conv_w'][:, None, :], window_strides=(1,),
                                    padding='VALID', dimension_numbers=('NWC', 'WIO', 'NWC'),
                                    feature_group_count=CONV_C)
    br_conv = jax.nn.silu(layernorm(conv + w['conv_b'], w['conv_ln_g'], w['conv_ln_b']))
    conv_state = u_ext[:, u_ext.shape[1] - (CONV_K - 1):]

    rq = rope(r_q.reshape(B, L, RET_HEADS, RET_DK), pos)
    rk = rope(r_k.reshape(B, L, RET_HEADS, RET_DK), pos) * RET_DK ** -0.5
    rv = r_v.reshape(B, L, RET_HEADS, RET_DV)
    log_gamma = jnp.log1p(-jnp.exp2(-5.0 - jnp.arange(RET_HEADS, dtype=jnp.float32)))
    ret_decay = jnp.broadcast_to(log_gamma[:, None], (B, L, RET_HEADS, 1))
    r_o, ret_state = decayed_linear_attention(rq, rk, rv, ret_decay, ret_s0, front_pad)
    br_ret = jax.nn.silu(r_g) * head_norm(r_o, w['ret_gn'], center=True)

    gq = g_q.reshape(B, L, GLA_HEADS, GLA_DK) * GLA_DK ** -0.5
    gk = g_k.reshape(B, L, GLA_HEADS, GLA_DK)
    gv = g_v.reshape(B, L, GLA_HEADS, GLA_DV)
    g_pre = (g_low @ w['gla_alpha_w'] + w['gla_alpha_b']).astype(jnp.float32)
    gla_decay = (jax.nn.log_sigmoid(g_pre) / GLA_TAU).reshape(B, L, GLA_HEADS, GLA_DK)
    g_o, gla_state = decayed_linear_attention(gq, gk, gv, gla_decay, gla_s0, front_pad)
    br_gla = jax.nn.silu(g_r) * head_norm(g_o, w['gla_gn'], center=False)

    dq = rmsnorm(d_q.reshape(B, L, DIFF_HEADS, 2, DIFF_HD), w['q_norm'])
    dk = rmsnorm(d_k.reshape(B, L, DIFF_HEADS, 2, DIFF_HD), w['k_norm'])
    dv = d_v.reshape(B, L, DIFF_HEADS, DIFF_VD)
    k_rows = dk.reshape(B, L, DIFF_HEADS, 2 * DIFF_HD)
    if k_past is None:
        k_all, v_all = dk, dv
    else:
        k_all = jnp.concatenate([k_past.astype(dk.dtype).reshape(B, -1, DIFF_HEADS, 2, DIFF_HD), dk], axis=1)
        v_all = jnp.concatenate([v_past.astype(dv.dtype), dv], axis=1)
    lam = (jnp.exp(jnp.sum(w['lam_q1'].astype(jnp.float32) * w['lam_k1'].astype(jnp.float32)))
           - jnp.exp(jnp.sum(w['lam_q2'].astype(jnp.float32) * w['lam_k2'].astype(jnp.float32)))
           + lam_init)
    d_o = diff_attention(dq[..., 0, :], dq[..., 1, :], k_all[..., 0, :], k_all[..., 1, :], v_all,
                         pos, k_pos, rel_bias, lam)
    br_diff = head_norm(d_o, w['diff_subln'], center=False) * (1.0 - lam_init)

    branches = jnp.stack([br_conv, br_ret, br_gla, br_diff], axis=2)
    gate = jax.nn.sigmoid(gates.reshape(B, L, N_BRANCH, D_MODEL))
    merged = jnp.einsum('blnc,ncd,blnd->bld', branches, w['w_branch'], gate)
    h = h + merged @ w['w_out']
    h = h + 0.5 * swiglu(rmsnorm(h, w['norm_ffn2']), w['ffn2_gate'], w['ffn2_up'], w['ffn2_down'])
    return h, (k_rows, dv, ret_state, gla_state, conv_state)

def setup_inputs(seed: int = 0) -> dict:
    key = jax.random.key(seed)
    keys = iter(jax.random.split(key, 64))
    f32 = jnp.float32

    def nrm(shape, scale):
        return jax.random.normal(next(keys), shape, f32) * scale

    def gain(shape):
        return 1.0 + nrm(shape, 0.05)

    n_pages = PAST_LEN // PAGE_SIZE
    n_pool = (DEC_BATCH * n_pages * 5) // 4
    page_table = jax.random.permutation(next(keys), n_pool)[:DEC_BATCH * n_pages]
    page_table = page_table.reshape(DEC_BATCH, n_pages).astype(jnp.int32)
    return {
        'x_prompt': nrm((BATCH, SEQ, D_MODEL), 1.0),
        'x_sample': nrm((DEC_BATCH, DEC_SEQ, D_MODEL), 1.0),
        'cache_k': nrm((DEPTH, n_pool, PAGE_SIZE, DIFF_HEADS, 2 * DIFF_HD), 1.0),
        'cache_v': nrm((DEPTH, n_pool, PAGE_SIZE, DIFF_HEADS, DIFF_VD), 1.0),
        'page_table': page_table,
        'state_ret': nrm((DEPTH, DEC_BATCH, RET_HEADS, RET_DK, RET_DV), 0.3),
        'state_gla': nrm((DEPTH, DEC_BATCH, GLA_HEADS, GLA_DK, GLA_DV), 0.3),
        'state_conv': nrm((DEPTH, DEC_BATCH, CONV_K - 1, CONV_C), 0.5),
        'meta_tokens': nrm((N_META, D_MODEL), 1.0),
        'rel_bias': nrm((REL_BUCKETS, DIFF_HEADS), 0.5),
        'norm_ffn1': gain((DEPTH, D_MODEL)),
        'ffn1_gate': nrm((DEPTH, D_MODEL, D_FF), D_MODEL ** -0.5),
        'ffn1_up': nrm((DEPTH, D_MODEL, D_FF), D_MODEL ** -0.5),
        'ffn1_down': nrm((DEPTH, D_FF, D_MODEL), D_FF ** -0.5),
        'norm_mix': gain((DEPTH, D_MODEL)),
        'w_in': nrm((DEPTH, D_MODEL, N_IN), D_MODEL ** -0.5),
        'b_in': nrm((DEPTH, N_IN), 0.02),
        'conv_w': nrm((DEPTH, CONV_K, CONV_C), CONV_K ** -0.5),
        'conv_b': nrm((DEPTH, CONV_C), 0.02),
        'conv_ln_g': gain((DEPTH, CONV_C)),
        'conv_ln_b': nrm((DEPTH, CONV_C), 0.02),
        'ret_gn': gain((DEPTH, RET_HEADS, RET_DV)),
        'gla_alpha_w': nrm((DEPTH, GLA_RANK, GLA_HEADS * GLA_DK), GLA_RANK ** -0.5),
        'gla_alpha_b': nrm((DEPTH, GLA_HEADS * GLA_DK), 0.02),
        'gla_gn': gain((DEPTH, GLA_HEADS, GLA_DV)),
        'q_norm': gain((DEPTH, DIFF_HD)),
        'k_norm': gain((DEPTH, DIFF_HD)),
        'lam_q1': nrm((DEPTH, DIFF_HD), 0.1),
        'lam_k1': nrm((DEPTH, DIFF_HD), 0.1),
        'lam_q2': nrm((DEPTH, DIFF_HD), 0.1),
        'lam_k2': nrm((DEPTH, DIFF_HD), 0.1),
        'diff_subln': gain((DEPTH, DIFF_VD)),
        'w_branch': nrm((DEPTH, N_BRANCH, BRANCH_W, D_MODEL), BRANCH_W ** -0.5),
        'w_out': nrm((DEPTH, D_MODEL, D_MODEL), D_MODEL ** -0.5),
        'norm_ffn2': gain((DEPTH, D_MODEL)),
        'ffn2_gate': nrm((DEPTH, D_MODEL, D_FF), D_MODEL ** -0.5),
        'ffn2_up': nrm((DEPTH, D_MODEL, D_FF), D_MODEL ** -0.5),
        'ffn2_down': nrm((DEPTH, D_FF, D_MODEL), D_FF ** -0.5),
    }

def reference(x_prompt, x_sample, cache_k, cache_v, page_table, state_ret, state_gla, state_conv,
              meta_tokens, rel_bias, norm_ffn1, ffn1_gate, ffn1_up, ffn1_down, norm_mix, w_in, b_in,
              conv_w, conv_b, conv_ln_g, conv_ln_b, ret_gn, gla_alpha_w, gla_alpha_b, gla_gn,
              q_norm, k_norm, lam_q1, lam_k1, lam_q2, lam_k2, diff_subln, w_branch, w_out,
              norm_ffn2, ffn2_gate, ffn2_up, ffn2_down):
    B, S, _ = x_prompt.shape
    DB, DS, _ = x_sample.shape
    L = S + N_META
    meta = jnp.broadcast_to(meta_tokens[None].astype(x_prompt.dtype), (B, N_META, D_MODEL))
    h_p = jnp.concatenate([meta, x_prompt], axis=1)
    h_s = x_sample
    pos_p = jnp.arange(L, dtype=jnp.int32)
    pos_s = PAST_LEN + jnp.arange(DS, dtype=jnp.int32)
    kpos_s = jnp.arange(PAST_LEN + DS, dtype=jnp.int32)
    front_pad = (CHUNK - N_META % CHUNK) % CHUNK

    kp_l, vp_l, rp_l, gp_l, cp_l = [], [], [], [], []
    ks_l, vs_l, rs_l, gs_l, cs_l = [], [], [], [], []
    for l in range(DEPTH):
        w = dict(norm_ffn1=norm_ffn1[l], ffn1_gate=ffn1_gate[l], ffn1_up=ffn1_up[l],
                 ffn1_down=ffn1_down[l], norm_mix=norm_mix[l], w_in=w_in[l], b_in=b_in[l],
                 conv_w=conv_w[l], conv_b=conv_b[l], conv_ln_g=conv_ln_g[l], conv_ln_b=conv_ln_b[l],
                 ret_gn=ret_gn[l], gla_alpha_w=gla_alpha_w[l], gla_alpha_b=gla_alpha_b[l],
                 gla_gn=gla_gn[l], q_norm=q_norm[l], k_norm=k_norm[l], lam_q1=lam_q1[l],
                 lam_k1=lam_k1[l], lam_q2=lam_q2[l], lam_k2=lam_k2[l], diff_subln=diff_subln[l],
                 w_branch=w_branch[l], w_out=w_out[l], norm_ffn2=norm_ffn2[l],
                 ffn2_gate=ffn2_gate[l], ffn2_up=ffn2_up[l], ffn2_down=ffn2_down[l])
        lam_init = 0.8 - 0.6 * math.exp(-0.3 * l)
        h_p, (kp, vp, rp, gp, cp) = trunk_layer(
            h_p, pos_p, pos_p, front_pad,
            jnp.zeros((B, CONV_K - 1, CONV_C), h_p.dtype),
            jnp.zeros((B, RET_HEADS, RET_DK, RET_DV), state_ret.dtype),
            jnp.zeros((B, GLA_HEADS, GLA_DK, GLA_DV), state_gla.dtype),
            None, None, rel_bias, lam_init, w)
        k_past = jnp.take(cache_k[l], page_table, axis=0).reshape(DB, PAST_LEN, DIFF_HEADS, 2 * DIFF_HD)
        v_past = jnp.take(cache_v[l], page_table, axis=0).reshape(DB, PAST_LEN, DIFF_HEADS, DIFF_VD)
        h_s, (ks, vs, rs, gs, cs) = trunk_layer(
            h_s, pos_s, kpos_s, 0, state_conv[l], state_ret[l], state_gla[l],
            k_past, v_past, rel_bias, lam_init, w)
        kp_l.append(kp); vp_l.append(vp); rp_l.append(rp); gp_l.append(gp); cp_l.append(cp)
        ks_l.append(ks); vs_l.append(vs); rs_l.append(rs); gs_l.append(gs); cs_l.append(cs)

    y_prompt = h_p[:, N_META:]
    y_sample = h_s
    k_prompt = jnp.stack(kp_l, axis=0)
    v_prompt = jnp.stack(vp_l, axis=0)
    k_sample = jnp.stack(ks_l, axis=0)
    v_sample = jnp.stack(vs_l, axis=0)
    ret_prompt = jnp.stack(rp_l, axis=0)
    ret_sample = jnp.stack(rs_l, axis=0)
    gla_prompt = jnp.stack(gp_l, axis=0)
    gla_sample = jnp.stack(gs_l, axis=0)
    conv_prompt = jnp.stack(cp_l, axis=0)
    conv_sample = jnp.stack(cs_l, axis=0)
    return (y_prompt, y_sample, k_prompt, v_prompt, k_sample, v_sample,
            ret_prompt, ret_sample, gla_prompt, gla_sample, conv_prompt, conv_sample)


_drawn_inputs = setup_inputs


def setup_inputs(seed=0):
    import zlib

    import numpy as np

    out = dict(_drawn_inputs(seed))
    spreads = {}
    factors = {'conv_b': 3.496,
     'conv_ln_b': 6.642,
     'ret_gn': 2.915,
     'gla_alpha_b': 5.937,
     'gla_gn': 2.904,
     'conv_ln_g': 3.035,
     'lam_q2': 3.434,
     'lam_k2': 2.762,
     'diff_subln': 2.848,
     'norm_ffn2': 2.88}
    for name, (base, spread) in spreads.items():
        noise = np.random.default_rng([zlib.crc32(name.encode()), seed]).standard_normal(out[name].shape)
        drawn = base * np.exp(spread * noise) if base else spread * noise
        out[name] = __import__('jax').numpy.asarray(drawn.astype(out[name].dtype))
    for name, factor in factors.items():
        out[name] = (out[name] * factor).astype(out[name].dtype)
    return out
```

```python
from contextlib import ExitStack
import math

import numpy as np

import concourse.bass as bass
from concourse import mybir

F32 = mybir.dt.float32
F32R = mybir.dt.float32r
U32 = mybir.dt.uint32
I32 = mybir.dt.int32
ALU = mybir.AluOpType
ACT = mybir.ActivationFunctionType
AX_X = mybir.AxisListType.X
ds = bass.ds

P = 128
D, FF, DEPTH = 1024, 2816, 2
KD, KF = D // P, FF // P
NB, NT = 8, 8
META, SEQ = 16, 512
TS = NB * NT
T = TS + META + SEQ
HALF = T // 2
LP = META + SEQ
PAST, PAGE = 1024, 128
PAGES = PAST // PAGE
POOL = NB * PAGES * 5 // 4
H = 4
CK = 31
EPS = 1e-6
ATT_SCALE = 32 ** -0.5
NEG = -1e30
RING = 4
WINDOWS = 5

U_FFN1, U_DOWN1 = 0, 2 * KF
U_MIX = U_DOWN1 + 24
U_GATES = U_MIX + 24
U_OUT = U_GATES + 40
U_FFN2 = U_OUT + 8
U_DOWN2 = U_FFN2 + 2 * KF
UNITS = U_DOWN2 + 24
QUADS = UNITS // RING
DOWN_BLOCKS = (8, 8, KF - 16)

V_COLS = (1024, 1792, 2832)
Z_COLS = (2320, 2448, 2576, 2704, 512, 640, 768, 896, 1536, 1664, 1280, 1408, 2048, 2176,
          256, 384, 0, 128)
DQ, DK, RQ, RK, GQ, GK, RG, GR, CG, CA = 0, 2, 4, 6, 8, 9, 10, 12, 14, 16
NZ = len(Z_COLS)
LOW_COL, GATE_COL = 2304, 3088

P_GAIN = 0
P_ZB = P_GAIN + 24
P_GB = P_ZB + NZ + 1
P_CW = P_GB + 32
P_CB, P_LG, P_LB = P_CW + 2 * CK, P_CW + 2 * CK + 2, P_CW + 2 * CK + 4
P_RGN, P_GGN = P_LB + 2, P_LB + 4
P_AB, P_SUB, P_QN, P_KN = P_GGN + 2, P_GGN + 3, P_GGN + 4, P_GGN + 5
P_LI, P_LI1 = P_KN + 1, P_KN + 2
P_LAM = P_KN + 3
P_AW = P_LAM + 4
NP_ = P_AW + P

CONSTS = 6
REL = PAST + NT
RL = REL + 127
SKEW = P - 1 + LP
GAMMA = [1.0 - 2.0 ** (-5 - h) for h in range(H)]
LEVELS = (128, 64, 32, 16, 8, 4, 2)


def window(w):
    return (0, TS + META) if w == 0 else (TS + META + P * (w - 1), P)


def centered_before(i):
    return i // 2


level_items = [(n, w) for n in range(len(LEVELS) + 1) for w in range(WINDOWS)
               if w or n == 0 or LEVELS[n - 1] <= META]


def items_through(n):
    return sum(m <= n for m, _ in level_items)


def level_start(b):
    return 0 if b <= NT else TS if b <= META else TS + META


def split_cols(ap):
    return ap.rearrange("p (h t) -> p h t", h=2)


def build(nc, h_in, wstream, wlow, params, vbias, cache_k, cache_v, page_table, st_ret, st_gla,
          st_conv, rel_bias, c_bucket, c_ones, c_ident, c_newmask, c_coef, c_rope, c_perm, c_dec, c_dec0,
          c_gq, c_gk, c_seq, c_reset, c_lvl, c_lvl0,
          y_out, k_out, v_out, ret_out, rets_out, gla_out, glas_out, conv_out, convs_out):
    scratch = nc.dram_tensor("bias_rows", (16, RL), F32).ap()
    skewed = nc.dram_tensor("bias_skewed", (P * (H * SKEW + 1),), F32).ap()

    with ExitStack() as ctx:
        def sem(name):
            return ctx.enter_context(nc.semaphore(name))

        at = -(-nc.sbuf_base // 32) * 32

        def place(name, shape, dt, offset):
            return nc.alloc_sbuf_tensor_at(name, shape, dt, offset=offset)

        def keep(name, shape, dt=F32):
            nonlocal at
            t = place(name, shape, dt, at)
            at += -(-4 * int(np.prod(shape[1:])) // 32) * 32
            return t

        hT = keep("hT", [P, KD, T])
        x_hi = keep("x_hi", [P, KD, T], F32R)
        x_lo = keep("x_lo", [P, KD, T], F32R)
        w_raw = keep("w_raw", [P, RING, 8, P])
        w_hi = keep("w_hi", [P, RING, 8, P], F32R)
        w_lo = keep("w_lo", [P, RING, 8, P], F32R)
        arena = at
        hid_hi = keep("hid_hi", [P, KF, T], F32R)
        hid_lo = keep("hid_lo", [P, KF, T], F32R)
        tmp = keep("tmp", [P, 2, T])
        gu = keep("gu", [P, 2, T])
        arena_end = at
        fresh = (gu[:, 0, :], gu[:, 1, :], tmp[:, 1, :])
        ssum = keep("ssum", [P, T])
        prm = keep("prm", [P, NP_ - P])
        ones = keep("ones", [P, 3, P])
        ident = keep("ident", [P, P])
        coef = keep("coef", [P, 8])
        hb = keep("hb", [P, 32])
        small = keep("small", [P, 2, 6])
        pages = keep("pages", [1, NB * PAGES], I32)
        assert at <= nc.sbuf_usable_end, at

        TB = 4 * T
        Z = place("Z", [P, NZ, T], F32, arena)
        V = place("V", [P, WINDOWS, 768], F32, arena + NZ * TB)
        od = place("od", [P, 2, T], F32, arena + NZ * TB + 15360)
        work = arena + NZ * TB + 15360 + 2 * TB
        GL = V[96:112, 0, 0:T]

        def area(name, shape, offset, dt=F32):
            size = 4 * int(np.prod(shape[1:]))
            assert offset % 32 == 0 and work + offset + size <= arena_end, (name, offset, size)
            return place(name, shape, dt, work + offset)

        kpage = area("kpage", [P, 2, PAGES, 2, P], 0)
        vpage = area("vpage", [P, 2, PAGES, 256], 16384)
        low_raw = area("low_raw", [P, 8, P], 32768)
        low_hi = area("low_hi", [P, 8, P], 36864, F32R)
        low_lo = area("low_lo", [P, 8, P], 40960, F32R)
        vb = area("vb", [P, 768], 45056)
        s_bias = area("s_bias", [P, PAST + NT], 32768)
        new_bias = area("new_bias", [P, 4, TS], 36896)
        new_mask = area("new_mask", [P, 4, TS], 37920)
        qbd = area("qbd", [P, 2, NB, 32], 38944)
        n_sq = area("n_sq", [P, 2, T], 40992)
        n_root = area("n_root", [P, 2, T], 45728)
        s_prob = area("s_prob", [P, PAST + TS], 40992)
        s_turn = area("s_turn", [P, 9, P], 45344)
        s_out = area("s_out", [P, P], 49952)
        p_bias = area("p_bias", [P, H, LP], 0)
        p_prob = area("p_prob", [P, 2, 2, LP], 8448)
        p_turn = area("p_turn", [P, 2, 512], 16896)
        p_meta = area("p_meta", [P, 2, P], 20992)
        rope = area("rope", [P, 2, T], 22016)
        perm = area("perm", [P, P], 26752)
        dec = area("dec", [P, H, P], 27264)
        dec0 = area("dec0", [P, H, 80], 29312)
        gq = area("gq", [P, 2, 208], 30592)
        gk = area("gk", [P, 2, 208], 32256)
        seqs = area("seqs", [P, NB], 33920)
        ss = area("ss", [P, 2, NB, P], 33984)
        vm = area("vm", [P, 2, NB, P], 42176)
        rqh = area("rqh", [P, 2, T], 0)
        rkh = area("rkh", [P, 2, T], 4736)
        rtmp = area("rtmp", [P, 2, 2, T], 9472)
        rkt = area("rkt", [P, WINDOWS, 2, P], 9472)
        rsc = area("rsc", [P, 2, 512], 14592)
        rst = area("rst", [P, 2, P], 18688)
        g_e = area("g_e", [P, 2, T], 0)
        g_qh = area("g_qh", [P, T], 4736)
        g_kh = area("g_kh", [P, T], 7104)
        g_kt = area("g_kt", [P, WINDOWS, P], 9472)
        g_sc = area("g_sc", [P, WINDOWS, 512], 12032)
        g_vm = area("g_vm", [P, NB, 256], 22272)
        g_st = area("g_st", [P, 256], 30464)
        reset = area("reset", [P, T], 31488)
        lvl = area("lvl", [P, 8, P], 33856)
        lvl0 = area("lvl0", [P, 5, 80], 37952)
        g_ss = area("g_ss", [P, NB, 256], 39552)
        aw = area("aw", [P, P], 47744)
        g_seqs = area("g_seqs", [P, NB], 48256)
        g_ql = Z[:, 0:2, :]
        g_kl = Z[:, 2:4, :]
        g_b = Z[:, RK, :]
        g_eb = Z[:, RK + 1, :]
        UE_S = NB * 38
        ue = area("ue", [P, 2, UE_S + 30 + LP], 0)
        hn_sq = area("hn_sq", [P, 2, T], 40992)
        hn_root = area("hn_root", [P, 2, T], 36256)
        TG = 0
        branch_tiles = [Z[:, CG, :], Z[:, CG + 1, :], Z[:, RQ, :], Z[:, RQ + 1, :],
                        Z[:, GQ, :], Z[:, GQ + 1, :], od[:, 0, :], od[:, 1, :]]
        rb = place("rb", [33, 16], F32, arena)
        bucket = place("bucket", [33, RL], F32, arena + 64)
        brow = place("brow", [16, RL], F32, arena + 4736)
        br_hi = area("br_hi", [P, 8, T], 0, F32R)
        br_lo = area("br_lo", [P, 8, T], 18944, F32R)
        m_hi = place("m_hi", [P, KD, T], F32R, arena)
        m_lo = place("m_lo", [P, KD, T], F32R, arena + KD * TB)
        d_sg = place("d_sg", [P, 4, T], F32, arena + 2 * KD * TB)
        d_acc = place("d_acc", [P, 2, T], F32, arena + (2 * KD + 4) * TB)
        assert (2 * KD + 6) * TB <= NZ * TB + 15360

        ps = ctx.enter_context(nc.psum_tensor("ps", [P, 8, 512], F32))

        def pair(p):
            return ps[:, 2 * p:2 * p + 2, 0:HALF]

        h_loaded = sem("h_loaded")
        consts_loaded = sem("consts_loaded")
        bias_row_made = sem("bias_row_made")
        bias_row_stored = sem("bias_row_stored")
        params_loaded = sem("params_loaded")
        weights_loaded = [sem(f"weights_loaded_{s}") for s in range(RING)]
        weights_high = sem("weights_high")
        weights_low = sem("weights_low")
        units_multiplied = sem("units_multiplied")
        squared = sem("squared")
        squares_summed = sem("squares_summed")
        square_total = sem("square_total")
        root_ready = sem("root_ready")
        inverse_ready = sem("inverse_ready")
        normed = sem("normed")
        x_high = sem("x_high")
        x_ready = sem("x_ready")
        tanh_ready = sem("tanh_ready")
        gated = sem("gated")
        hidden_made = sem("hidden_made")
        hidden_high = sem("hidden_high")
        hidden_ready = sem("hidden_ready")
        residual_added = sem("residual_added")
        phases_entered = sem("phases_entered")
        mixers_left = sem("mixers_left")
        mixers_open = sem("mixers_open")
        y_stored = sem("y_stored")

        cleared = []

        def msem(name):
            cleared.append(sem(name))
            return cleared[-1]

        v_products, v_ready, z_ready = msem("v_products"), msem("v_ready"), msem("z_ready")
        low_loaded, low_high, low_split, low_product = (msem(n) for n in ("low_loaded", "low_high", "low_split", "low_product"))
        vector_chain, scalar_chain = msem("vector_chain"), msem("scalar_chain")
        vb_loaded, attn_tables_loaded, lam_ready = msem("vb_loaded"), msem("attn_tables_loaded"), msem("lam_ready")
        lam_products, lam_sums, lam_exps = msem("lam_products"), msem("lam_sums"), msem("lam_exps")
        keys_loaded = [msem(f"keys_loaded_{i}") for i in range(2)]
        values_loaded = [msem(f"values_loaded_{i}") for i in range(2)]
        qk_squared, qk_summed, qk_root, qk_normed = (msem(n) for n in ("qk_squared", "qk_summed", "qk_root", "qk_normed"))
        queries_placed = msem("queries_placed")
        sample_scores, sample_max, sample_exp, sample_scaled, sample_turned, sample_pt, sample_pv, sample_copied, sample_placed = (
            msem("sample_" + n) for n in ("scores", "max", "exp", "scaled", "turned", "pt", "pv", "copied", "placed"))
        prompt_bias_loaded = msem("prompt_bias_loaded")
        prompt_scores, prompt_max, prompt_exp, prompt_attn, prompt_turned, prompt_pt, prompt_pv, prompt_evac = (
            msem("prompt_" + n) for n in ("scores", "max", "exp", "attn", "turned", "pt", "pv", "evac"))
        ret_tables_loaded = msem("ret_tables_loaded")
        rope_swapped, rope_turned, ret_scaled, ret_blocks, ret_keys, ret_scores, ret_decayed, ret_mixed, ret_evac, ret_update, ret_state = (
            msem(n) for n in ("rope_swapped", "rope_turned", "ret_scaled", "ret_blocks", "ret_keys", "ret_scores",
                              "ret_decayed", "ret_mixed", "ret_evac", "ret_update", "ret_state"))
        ret_spread, ret_s_update, ret_s_state = msem("ret_spread"), msem("ret_s_update"), msem("ret_s_state")
        gla_tables_loaded = msem("gla_tables_loaded")
        alpha_product, alpha_log, gla_summed, gla_exp_b, gla_diff, gla_exp_last, gla_scaled, gla_blocks, gla_keys = (
            msem(n) for n in ("alpha_product", "alpha_log", "gla_summed", "gla_exp_b", "gla_diff", "gla_exp_last",
                              "gla_scaled", "gla_blocks", "gla_keys"))
        lvl_diff, lvl_exp, lvl_ready, lvl_scores, lvl_taken = (msem("level_" + n) for n in ("diff", "exp", "ready", "scores", "taken"))
        gla_mixed, gla_evac, gla_update, gla_state, gla_spread, gla_s_update, gla_s_state = (
            msem("gla_" + n) for n in ("mixed", "evac", "update", "state", "spread", "s_update", "s_state"))
        conv_loaded, conv_tanh, conv_gated, conv_rows, conv_done = (msem("conv_" + n) for n in ("loaded", "tanh", "gated", "rows", "done"))
        hn_summed, hn_centered, hn_squared, hn_totalled, hn_root_ready, hn_normed = (
            msem("head_norm_" + n) for n in ("mean", "centered", "squared", "totalled", "root", "normed"))
        act_tanh, br_ready, br_high, br_split = msem("branch_tanh"), msem("branch_ready"), msem("branch_high"), msem("branch_split")
        mixers_stored = msem("mixers_stored")
        gate_tanh, branch_products, branch_taken, merged_steps, merged_high, merged_ready = (
            msem(n) for n in ("gate_tanh", "branch_products", "branch_taken", "merged_steps", "merged_high", "merged_ready"))
        nums = [s.num for s in cleared]
        assert nums == list(range(nums[0], nums[0] + len(nums)))

        HEAD_NORMS = (
            (od, 0, None, 1, 64, False, False),
            (Z, RQ, P_RGN, 1, 64, True, False),
            (Z, GQ, P_GGN, 1, 64, False, False),
            (Z, CG, P_LG, 0, 256, True, True),
        )
        MIXER_STORES = 10
        POOL_LOADS = ((vb_loaded, 1), (low_loaded, 1), (attn_tables_loaded, 9), (prompt_bias_loaded, 1),
                      (ret_tables_loaded, 8), (gla_tables_loaded, 6), (conv_loaded, 2))

        block = ctx.enter_context(nc.Block())

        @block.sync
        def _(sp):
            def load_unit(quad, slot):
                sp.wait_ge(weights_low, 4 * quad + slot + 1)
                sp.dma_start(w_raw[:, slot, :, :], wstream[ds(4 * quad + slot, 1)].rearrange("a p (k m) -> (a p) k m", k=8)
                             ).then_inc(weights_loaded[slot], 16)

            def load_quads(l, first, count):
                with sp.Fori(0, count) as i:
                    for s in range(RING):
                        load_unit(l * QUADS + first + i, s)

            def load_pages(l, b):
                for pg in range(PAGES):
                    page = sp.value_load(pages[0:1, b * PAGES + pg:b * PAGES + pg + 1], min_val=0, max_val=POOL - 1)
                    sp.dma_start(kpage[:, b % 2, pg, :, :], cache_k[ds(l * POOL + page, 1)].rearrange("a p (j s) -> (a p) j s", j=2)
                                 ).then_inc(keys_loaded[b % 2], 16)
                    sp.dma_start(vpage[:, b % 2, pg, :], cache_v[ds(l * POOL + page, 1)].rearrange("a p n -> (a p) n")
                                 ).then_inc(values_loaded[b % 2], 16)

            sp.dma_start(hT[:, :, :], h_in).then_inc(h_loaded, 16)
            for s in range(RING):
                sp.dma_start(w_raw[:, s, :, :], wstream[s].rearrange("p (k m) -> p k m", k=8)).then_inc(weights_loaded[s], 16)
            sp.wait_ge(consts_loaded, 16 * CONSTS)
            with sp.Fori(0, DEPTH) as l:
                load_quads(l, 1, U_MIX // RING)
                sp.wait_ge(mixers_open, l + 1)
                sp.sem_inc(phases_entered, 1)
                sp.wait_ge(x_ready, l * 24 + 16)
                sp.sem_inc(phases_entered, 1)
                for b in range(2):
                    load_pages(l, b)
                load_quads(l, 1 + U_MIX // RING, (U_GATES - U_MIX) // RING)
                for b in range(2, NB):
                    sp.wait_ge(sample_pv, b // 2)
                    load_pages(l, b)
                sp.wait_ge(sample_pv, 4)
                sp.sem_inc(mixers_left, 1)
                load_quads(l, 1 + U_GATES // RING, (UNITS - U_GATES) // RING)
            sp.wait_ge(residual_added, 4 + 24 * DEPTH)
            sp.dma_start(y_out, hT[:, :, :]).then_inc(y_stored, 16)
            sp.wait_ge(y_stored, 16)
            for s in range(RING):
                sp.wait_ge(weights_loaded[s], 16 * (DEPTH * QUADS + 1))

        @block.gpsimd
        def _(pl):
            pl.dma_start(pages[:, :], page_table).then_inc(consts_loaded, 16)
            pl.dma_start(ones[:, :, :], c_ones).then_inc(consts_loaded, 16)
            pl.dma_start(ident[:, :], c_ident).then_inc(consts_loaded, 16)
            pl.dma_start(coef[:, 0:2], c_coef).then_inc(consts_loaded, 16)
            pl.dma_start(rb[0:33, :], rel_bias).then_inc(consts_loaded, 16)
            pl.dma_start(bucket[0:33, :], c_bucket).then_inc(consts_loaded, 16)
            pl.dma_start(prm[:, :], params[0][:, 0:NP_ - P]).then_inc(params_loaded, 16)
            pl.wait_ge(bias_row_made, 3)
            pl.dma_start(scratch, brow[:, :]).then_inc(bias_row_stored, 16)
            pl.wait_ge(bias_row_stored, 16)
            pl.dma_start(bass.AP(tensor=skewed.tensor, offset=skewed.offset, ap=[[H * SKEW + 1, P], [SKEW, H], [1, SKEW]]),
                         bass.AP(tensor=scratch.tensor, offset=scratch.offset + RL - SKEW, ap=[[0, P], [2 * RL, H], [1, SKEW]])
                         ).then_inc(bias_row_stored, 16)
            pl.wait_ge(bias_row_stored, 32)
            pl.sem_inc(mixers_open, 1)
            with pl.Fori(0, DEPTH) as l:
                pl.wait_ge(mixers_open, l + 1)
                pl.sem_inc(phases_entered, 1)
                pl.wait_ge(x_ready, l * 24 + 16)
                pl.sem_inc(phases_entered, 1)
                pl.dma_start(vb[:, :], vbias[ds(l, 1)].to_broadcast([P, 768])).then_inc(vb_loaded, 16)
                pl.dma_start(low_raw[:, :, :], wlow[ds(l, 1)].rearrange("a p (k m) -> (a p) k m", k=8)).then_inc(low_loaded, 16)
                pl.wait_ge(z_ready, NZ + 1)
                pl.wait_ge(v_ready, 15)
                for t in range(NT):
                    src = bass.AP(tensor=scratch.tensor, offset=scratch.offset + NT - 1 - t,
                                  ap=[[RL, 16], [1, PAST + NT]])
                    pl.dma_start(s_bias[t:P - NT + t + 1:NT, :], src).then_inc(attn_tables_loaded, 16)
                pl.dma_start(new_mask[:, :, :], c_newmask).then_inc(attn_tables_loaded, 16)
                pl.wait_ge(qk_normed, 4)
                pl.dma_start(k_out[ds(l, 1)].rearrange("a p j t -> (a p) j t"), Z[:, DK:DK + 2, :]).then_inc(mixers_stored, 16)
                pl.dma_start(v_out[ds(l, 1), 0:80, 0:1].rearrange("a p w n -> (a p) (w n)"), V[0:80, 0, 512:768]).then_inc(mixers_stored, 16)
                pl.dma_start(v_out[ds(l, 1), :, 1:WINDOWS].rearrange("a p w n -> (a p) w n"), V[:, 1:WINDOWS, 512:768]).then_inc(mixers_stored, 16)
                pl.wait_ge(sample_scores, 4)
                src = bass.AP(tensor=skewed.tensor, offset=skewed.offset + P - 1, ap=[[H * SKEW, P], [SKEW, H], [1, LP]])
                pl.dma_start(p_bias[:, :, :], src).then_inc(prompt_bias_loaded, 16)
                pl.wait_ge(sample_placed, 4)
                pl.dma_start(rope[:, :, :], c_rope).then_inc(ret_tables_loaded, 16)
                pl.dma_start(perm[:, :], c_perm).then_inc(ret_tables_loaded, 16)
                pl.dma_start(dec[:, :, :], c_dec).then_inc(ret_tables_loaded, 16)
                pl.dma_start(dec0[0:80, :, :], c_dec0).then_inc(ret_tables_loaded, 16)
                pl.dma_start(gq[:, :, :], c_gq).then_inc(ret_tables_loaded, 16)
                pl.dma_start(gk[:, :, :], c_gk).then_inc(ret_tables_loaded, 16)
                pl.dma_start(seqs[0:TS, :], c_seq).then_inc(ret_tables_loaded, 16)
                pl.dma_start(ss[:, :, :, :], st_ret[ds(l, 1)].rearrange("a p j b n -> (a p) j b n")).then_inc(ret_tables_loaded, 16)
                pl.wait_ge(ret_state, WINDOWS)
                pl.dma_start(ret_out[ds(l, 1)].rearrange("a p j n -> (a p) j n"), rst[:, :, :]).then_inc(mixers_stored, 16)
                pl.wait_ge(ret_s_state, 1)
                pl.dma_start(rets_out[ds(l, 1)].rearrange("a p j b n -> (a p) j b n"), ss[:, :, :, :]).then_inc(mixers_stored, 16)
                pl.wait_ge(mixers_stored, 16 * 5)
                pl.dma_start(reset[:, :], c_reset).then_inc(gla_tables_loaded, 16)
                pl.dma_start(lvl[:, :, :], c_lvl).then_inc(gla_tables_loaded, 16)
                pl.dma_start(lvl0[0:80, :, :], c_lvl0).then_inc(gla_tables_loaded, 16)
                pl.dma_start(g_ss[:, :, :], st_gla[ds(l, 1)].rearrange("a p b n -> (a p) b n")).then_inc(gla_tables_loaded, 16)
                pl.dma_start(g_seqs[0:TS, :], c_seq).then_inc(gla_tables_loaded, 16)
                pl.dma_start(aw[96:112, :], params[ds(l, 1), 0:16, P_AW:P_AW + P].rearrange("a p n -> (a p) n")).then_inc(gla_tables_loaded, 16)
                pl.wait_ge(gla_state, WINDOWS)
                pl.dma_start(gla_out[ds(l, 1)].rearrange("a p n -> (a p) n"), g_st[:, :]).then_inc(mixers_stored, 16)
                pl.wait_ge(gla_s_state, 1)
                pl.dma_start(glas_out[ds(l, 1)].rearrange("a p b n -> (a p) b n"), g_ss[:, :, :]).then_inc(mixers_stored, 16)
                pl.wait_ge(mixers_stored, 16 * 7)
                for j in range(2):
                    pl.dma_start(ue[:, j, 0:UE_S].rearrange("p (b r) -> p b r", r=38)[:, :, 0:30],
                                 st_conv[ds(l, 1), :, j:j + 1].rearrange("a p j b r -> (a p) (j b) r")).then_inc(conv_loaded, 16)
                pl.wait_ge(conv_rows, 4)
                pl.dma_start(conv_out[ds(l, 1)].rearrange("a p j r -> (a p) j r"), ue[:, :, UE_S + LP:UE_S + LP + 30]).then_inc(mixers_stored, 16)
                for j in range(2):
                    pl.dma_start(convs_out[ds(l, 1), :, j:j + 1].rearrange("a p j b r -> (a p) (j b) r"),
                                 ue[:, j, 0:UE_S].rearrange("p (b r) -> p b r", r=38)[:, :, 8:38]).then_inc(mixers_stored, 16)
                pl.wait_ge(mixers_stored, 16 * MIXER_STORES)
                for loaded, count in POOL_LOADS:
                    pl.wait_ge(loaded, 16 * count)
                pl.wait_ge(mixers_left, 4 * (l + 1))
                pl.sem_inc(phases_entered, 1)
                pl.dma_reset(range(nums[0], nums[-1] + 1))
                pl.sem_clear(range(nums[0], nums[-1] + 1))
                pl.sem_inc(mixers_open, 1)
                pl.wait_ge(x_ready, l * 24 + 24)
                pl.sem_inc(phases_entered, 1)
                pl.dma_start(prm[:, :], params[ds(l + 1, 1), :, 0:NP_ - P].rearrange("a p n -> (a p) n")).then_inc(params_loaded, 16)
            pl.wait_ge(params_loaded, 16 * (DEPTH + 1))

        @block.scalar
        def _(act):
            def split_high(quad, slot):
                act.wait_ge(weights_loaded[slot], 16 * quad + 16)
                act.wait_ge(units_multiplied, 4 * quad + slot + 1)
                act.activation(w_hi[:, slot, :, :], w_raw[:, slot, :, :], ACT.Copy).then_inc(weights_high, 1)

            def unit_done(quad, slot):
                act.wait_ge(units_multiplied, 4 * quad + slot + 1 + RING)

            def norm(l, i):
                w = l * 3 + i
                act.wait_ge(square_total, w + 1)
                act.activation(split_cols(tmp[:, 0, :]), pair(0), ACT.Sqrt, bias=EPS, scale=1.0 / D).then_inc(root_ready, 1)
                for k in range(KD):
                    act.wait_ge(normed, 8 * w + k + 1)
                    act.activation(x_hi[:, k, :], fresh[k % 3], ACT.Copy).then_inc(x_high, 1)

            def gate_up(l, f, first):
                with act.Fori(0, KF // 2) as i:
                    for j in range(2):
                        q = l * 2 * KF + f * KF + i * 2 + j
                        quad = l * QUADS + first // RING + i
                        act.wait_ge(hidden_made, q + 1)
                        unit_done(quad, 2 * j)
                        act.activation(split_cols(tmp[:, j, :]), pair(2 * j), ACT.Tanh, scale=0.5).then_inc(tanh_ready, 1)
                        split_high(quad + 1, 2 * j)
                        act.wait_ge(hidden_made, q + 3)
                        split_high(quad + 1, 2 * j + 1)
                        act.activation(hid_hi[:, ds(i * 2 + j, 1), :], gu[:, j:j + 1, :], ACT.Copy).then_inc(hidden_high, 1)

            def residual(l, r0, first, units):
                with act.Fori(0, 2) as i:
                    for j in range(4):
                        r = l * 24 + r0 + i * 4 + j
                        for u in range(units):
                            pos = j * units + u
                            quad = l * QUADS + first // RING + i * units + pos // RING
                            if u == units - 1:
                                act.wait_ge(residual_added, r + 1 + 4)
                                act.wait_ge(squares_summed, r + 7)
                            split_high(quad + 1, pos % RING)
                        act.activation(tmp[:, j % 2:j % 2 + 1, :], hT[:, ds(i * 4 + j, 1), :], ACT.Square).then_inc(squared, 1)

            chain = [0]

            def link(ins):
                chain[0] += 1
                ins.then_inc(scalar_chain, 1)
                act.wait_ge(scalar_chain, chain[0])

            def project(l):
                act.wait_ge(mixers_open, l + 1)
                act.sem_inc(phases_entered, 1)
                act.wait_ge(low_loaded, 16)
                act.activation(low_hi[:, :, :], low_raw[:, :, :], ACT.Copy).then_inc(low_high, 1)
                for c in range(-6, NZ):
                    pos = c + 6
                    quad, slot = l * QUADS + U_MIX // RING + pos // RING, pos % RING
                    if c >= 0:
                        unit_done(quad, slot)
                        act.activation(split_cols(Z[:, c, :]), pair(c % 4), ACT.Identity, bias=prm[:, P_ZB + c:P_ZB + c + 1]).then_inc(z_ready, 1)
                    split_high(quad + 1, slot)
                act.wait_ge(low_product, 1)
                act.activation(split_cols(GL), ps[0:16, 4:6, 0:HALF], ACT.Identity, bias=prm[0:16, P_ZB + NZ:P_ZB + NZ + 1]).then_inc(z_ready, 1)

            def attention_sample():
                for t in range(4 + 1):
                    if t < 4:
                        act.wait_ge(z_ready, NZ + 1)
                        if t >= 2:
                            act.wait_ge(qk_summed, t - 1)
                        act.activation(n_sq[:, t % 2, :], Z[:, t, :], ACT.Square).then_inc(qk_squared, 1)
                    if t >= 1:
                        act.wait_ge(qk_summed, t)
                        if t >= 3:
                            act.wait_ge(qk_normed, t - 2)
                        act.activation(split_cols(n_root[:, (t - 1) % 2, :]), pair((t - 1) % 2), ACT.Sqrt, bias=EPS, scale=1.0 / 32).then_inc(qk_root, 1)
                act.wait_ge(lam_sums, 1)
                act.activation(coef[:, 2:4], ps[:, 7, 0:2], ACT.Exp).then_inc(lam_exps, 1)
                for p in range(4):
                    act.wait_ge(sample_max, p + 1)
                    act.activation(s_prob[:, :], s_prob[:, :], ACT.Exp, bias=coef[:, 6:7], accum_out=coef[:, 7:8]).then_inc(sample_exp, 1)
                    act.wait_ge(sample_turned, p + 1)
                    act.activation(s_turn[:, 0:8, :], ps[:, 3:5, :].rearrange("p b (s r) -> p (b s) r", s=4), ACT.Copy).then_inc(sample_pt, 1)
                    act.activation(s_turn[0:TS, 8, :], ps[0:TS, 5, 0:P], ACT.Copy).then_inc(sample_pt, 1)
                    act.wait_ge(sample_pv, p + 1)
                    act.activation(s_out[:, :], ps[:, 6, 0:P], ACT.Copy).then_inc(sample_copied, 1)

            def prompt_steps():
                return [(j, h) for j in range(WINDOWS) for h in range(H)]

            def attention_prompt():
                def exps(x):
                    n = META if x < H else P
                    ns = META + P * (x // H)
                    act.wait_ge(prompt_max, x + 1)
                    for i in range(2):
                        act.activation(p_prob[0:n, x % 2, i, 0:ns], p_prob[0:n, x % 2, i, 0:ns], ACT.Exp,
                                       bias=small[0:n, x % 2, i:i + 1], accum_out=small[0:n, x % 2, 2 + i:3 + i]).then_inc(prompt_exp, 1)

                steps = prompt_steps()
                exps(0)
                for x, (j, h) in enumerate(steps):
                    if x + 1 < len(steps):
                        exps(x + 1)
                    n = META if j == 0 else P
                    act.wait_ge(prompt_turned, x + 1)
                    if x >= 2:
                        act.wait_ge(prompt_pv, x - 1)
                    if j:
                        link(act.activation(p_turn[:, x % 2, 0:j * P], ps[:, 4 + x % 2, 0:j * P], ACT.Copy))
                    act.activation(p_meta[64:64 + META, x % 2, 0:n], ps[0:META, 6, 0:n], ACT.Copy).then_inc(prompt_pt, 1)
                    if h % 2:
                        c0, n = (TS, META) if j == 0 else window(j)
                        act.wait_ge(prompt_pv, x + 1)
                        act.activation(od[:, h // 2, c0:c0 + n], ps[:, 7, 0:n], ACT.Copy).then_inc(prompt_evac, 1)

            def retention():
                for w in range(WINDOWS):
                    n = window(w)[1]
                    act.wait_ge(ret_blocks, w + 1)
                    act.activation(rkt[0:n, w, :, :], ps[0:n, w % 2, 0:256].rearrange("p (j c) -> p j c", j=2), ACT.Copy).then_inc(ret_keys, 1)
                for w in range(WINDOWS):
                    c0, n = window(w)
                    act.wait_ge(ret_mixed, w + 1)
                    act.activation(Z[:, RQ:RQ + 2, c0:c0 + n], ps[:, 4 + w % 2, 0:256].rearrange("p (j c) -> p j c", j=2)[:, :, 0:n],
                                   ACT.Copy).then_inc(ret_evac, 1)

            def gla():
                act.wait_ge(alpha_product, 1)
                link(act.activation(split_cols(g_e[:, 0, :]), pair(0), ACT.Identity, bias=prm[:, P_AB:P_AB + 1]))
                link(act.activation(g_e[:, 1, :], g_e[:, 0, :], ACT.Abs))
                link(act.activation(g_e[:, 1, :], g_e[:, 1, :], ACT.Exp, scale=-1.0))
                act.activation(g_e[:, 1, :], g_e[:, 1, :], ACT.Ln, bias=1.0).then_inc(alpha_log, 1)
                act.wait_ge(gla_summed, 1)
                act.activation(g_eb, g_b, ACT.Exp).then_inc(gla_exp_b, 1)
                act.wait_ge(gla_diff, 1)
                act.activation(g_e[:, 1, :], g_e[:, 1, :], ACT.Exp).then_inc(gla_exp_last, 1)
                for w in range(WINDOWS):
                    n = window(w)[1]
                    act.wait_ge(gla_blocks, w + 1)
                    act.activation(g_kt[0:n, w, :], ps[0:n, 4 + w % 2, 0:P], ACT.Copy).then_inc(gla_keys, 1)
                for n, b in enumerate(LEVELS):
                    act.wait_ge(lvl_diff, n + 1)
                    c0 = level_start(b)
                    view = g_e[:, n % 2, c0:T].rearrange("p (n b) -> p n b", b=b)
                    act.activation(view[:, :, 0:b // 2], view[:, :, 0:b // 2], ACT.Exp, scale=-1.0).then_inc(lvl_exp, 1)
                    act.activation(view[:, :, b // 2:b], view[:, :, b // 2:b], ACT.Exp).then_inc(lvl_exp, 1)
                for w in range(WINDOWS):
                    c0, n = window(w)
                    act.wait_ge(gla_mixed, w + 1)
                    act.activation(Z[:, GQ:GQ + 2, c0:c0 + n], ps[:, 6 + w % 2, 0:256].rearrange("p (j c) -> p j c", j=2)[:, :, 0:n],
                                   ACT.Copy).then_inc(gla_evac, 1)

            def conv():
                for j in range(2):
                    act.activation(Z[:, CG + j, :], Z[:, CG + j, :], ACT.Tanh, scale=0.5).then_inc(conv_tanh, 1)
                for j in range(2):
                    act.wait_ge(conv_loaded, 32)
                    act.wait_ge(conv_gated, j + 2)
                    act.activation(ue[:, j, 0:UE_S].rearrange("p (b r) -> p b r", r=38)[:, :, 30:38],
                                   Z[:, CA + j, 0:TS].rearrange("p (b t) -> p b t", b=NB), ACT.Copy, scale=0.5).then_inc(conv_rows, 1)
                    act.activation(ue[:, j, UE_S + 30:UE_S + 30 + LP], Z[:, CA + j, TS:T], ACT.Copy, scale=0.5).then_inc(conv_rows, 1)

            def head_norms():
                for i, (src, c, gain, o, width, center, shared) in enumerate(HEAD_NORMS):
                    for j in range(2):
                        act.wait_ge(hn_centered, 2 * i + j + 1)
                        if i:
                            act.wait_ge(hn_totalled, 2 * i)
                        act.activation(hn_sq[:, j, :], src[:, c + j, :], ACT.Square).then_inc(hn_squared, 1)
                    for j in range(2):
                        act.wait_ge(hn_totalled, 2 * i + j + 1)
                        if i:
                            act.wait_ge(hn_normed, 2 * i)
                        act.activation(split_cols(hn_root[:, j, :]), pair(2 + j), ACT.Sqrt, bias=EPS, scale=1.0 / width).then_inc(hn_root_ready, 1)

            def branches():
                act.wait_ge(hn_normed, 8)
                for n, c in enumerate((RG, RG + 1, GR, GR + 1)):
                    act.activation(Z[:, TG + n, :], Z[:, c, :], ACT.Tanh, scale=0.5).then_inc(act_tanh, 1)
                act.wait_ge(conv_done, 2)
                for n in range(2):
                    act.activation(hn_root[:, n, :], Z[:, CG + n, :], ACT.Tanh, scale=0.5).then_inc(act_tanh, 1)
                act.wait_ge(mixers_stored, 16 * MIXER_STORES)
                for n, t in enumerate(branch_tiles):
                    act.wait_ge(br_ready, 6)
                    act.activation(br_hi[:, n, :], t, ACT.Copy).then_inc(br_high, 1)

            def gates(l):
                act.wait_ge(br_split, 8)
                with act.Fori(0, 2) as i:
                    for mm in range(4):
                        m = i * 4 + mm
                        for n in range(5):
                            pos = mm * 5 + n
                            quad, slot = l * QUADS + U_GATES // RING + i * 5 + pos // RING, pos % RING
                            if n < 4:
                                act.wait_ge(branch_taken, m * 4 + n + 1)
                                unit_done(quad, slot)
                                split_high(quad + 1, slot)
                                act.activation(split_cols(d_sg[:, n, :]), pair(n), ACT.Tanh, scale=0.5, bias=hb[:, ds(m + 8 * n, 1)]).then_inc(gate_tanh, 1)
                            else:
                                act.wait_ge(merged_steps, m * 3 + 3)
                                split_high(quad + 1, slot)
                                act.activation(m_hi[:, ds(m, 1), :], d_acc[:, 0:1, :], ACT.Copy, scale=0.5).then_inc(merged_high, 1)
                act.drain().then_inc(mixers_left, 1)

            act.wait_ge(bias_row_stored, 16)
            act.wait_ge(h_loaded, 16)
            for s in range(RING):
                act.wait_ge(weights_loaded[s], 16)
                act.activation(w_hi[:, s, :, :], w_raw[:, s, :, :], ACT.Copy).then_inc(weights_high, 1)
            for m in range(KD):
                if m >= 2:
                    act.wait_ge(squares_summed, m - 1)
                act.activation(tmp[:, m % 2, :], hT[:, m, :], ACT.Square).then_inc(squared, 1)
            with act.Fori(0, DEPTH) as l:
                norm(l, 0)
                gate_up(l, 0, U_FFN1)
                residual(l, 0, U_DOWN1, 3)
                norm(l, 1)
                project(l)
                attention_sample()
                attention_prompt()
                retention()
                gla()
                conv()
                head_norms()
                branches()
                gates(l)
                residual(l, 8, U_OUT, 1)
                norm(l, 2)
                gate_up(l, 1, U_FFN2)
                residual(l, 16, U_DOWN2, 3)

        @block.tensor
        def _(pe):
            def products(p, slot, blocks, k0, xh, xl, start=True, stop=True, wh=None, wl=None):
                wh = w_hi[:, slot, :, :] if wh is None else wh
                wl = w_lo[:, slot, :, :] if wl is None else wl
                for k in range(blocks[0], blocks[1]):
                    for n, (wp, xp) in enumerate(((wh, xh), (wl, xh), (wh, xl))):
                        for half in range(2):
                            mm = pe.matmul(ps[:, 2 * p + half, 0:HALF], wp[:, k, :],
                                           xp[:, k0 + k - blocks[0], half * HALF:(half + 1) * HALF],
                                           start=start and k == blocks[0] and n == 0,
                                           stop=stop and k == blocks[1] - 1 and n == 2)
                return mm

            def unit_ready(quad, slot):
                pe.wait_ge(weights_low, 4 * quad + slot + 1 + RING)

            def sum_tile(p, mat, tile, start=True, stop=True):
                for half in range(2):
                    mm = pe.matmul(ps[:, 2 * p + half, 0:HALF], mat, tile[:, half * HALF:(half + 1) * HALF], start=start, stop=stop)
                return mm

            def norm(l, i):
                w = l * 3 + i
                pe.wait_ge(squares_summed, 8 * (w + 1))
                sum_tile(0, ones[:, 0, :], ssum[:, :]).then_inc(square_total, 1)

            def gate_up(l, f, first):
                pe.wait_ge(x_ready, l * 24 + 8 * (2 * f + 1))
                pe.sem_inc(phases_entered, 1)
                with pe.Fori(0, KF // 2) as i:
                    for j in range(2):
                        quad = l * QUADS + first // RING + i
                        pe.wait_ge(hidden_made, l * 2 * KF + f * KF + i * 2 + j + 1)
                        for part in range(2):
                            unit_ready(quad, 2 * j + part)
                            products(2 * j + part, 2 * j + part, (0, 8), 0, x_hi, x_lo).then_inc(units_multiplied, 1)

            def residual(l, r0, first, blocks, xh, xl):
                units = len(blocks)
                with pe.Fori(0, 2) as i:
                    for j in range(4):
                        pe.wait_ge(residual_added, l * 24 + r0 + i * 4 + j + 1)
                        for u in range(units):
                            pos = j * units + u
                            unit_ready(l * QUADS + first // RING + i * units + pos // RING, pos % RING)
                            products(j, pos % RING, (0, blocks[u]), 8 * u, xh, xl, start=u == 0,
                                     stop=u == units - 1).then_inc(units_multiplied, 1)

            def project(l):
                pe.wait_ge(mixers_open, l + 1)
                pe.sem_inc(phases_entered, 1)
                pe.wait_ge(x_ready, l * 24 + 16)
                for g in range(3):
                    s0 = 2 * g % RING
                    for w in range(WINDOWS):
                        c0, n = window(w)
                        idx = WINDOWS * g + w
                        if w == 0:
                            unit_ready(l * QUADS + U_MIX // RING + 2 * g // RING, s0 + 1)
                        if idx >= 8:
                            pe.wait_ge(v_ready, idx - 7)
                        for k in range(KD):
                            for m, (xp, wp) in enumerate(((x_hi, w_hi), (x_hi, w_lo), (x_lo, w_hi))):
                                mm = pe.matmul(ps[0:n, idx % 8, 0:256], xp[:, k, c0:c0 + n], wp[:, s0:s0 + 2, k, :],
                                               start=k == 0 and m == 0, stop=k == KD - 1 and m == 2)
                        mm.then_inc(*((v_products, 1) if w < WINDOWS - 1 else (units_multiplied, 2)))
                pe.wait_ge(v_ready, 15)
                for c in range(NZ):
                    pos = c + 6
                    unit_ready(l * QUADS + U_MIX // RING + pos // RING, pos % RING)
                    if c >= 4:
                        pe.wait_ge(z_ready, c - 3)
                    products(c % 4, pos % RING, (0, 8), 0, x_hi, x_lo).then_inc(units_multiplied, 1)
                pe.wait_ge(low_split, 1)
                pe.wait_ge(z_ready, NZ - 3)
                products(NZ % 4, 0, (0, 8), 0, x_hi, x_lo, wh=low_hi, wl=low_lo).then_inc(low_product, 1)

            def attention_sample():
                pe.wait_ge(z_ready, NZ + 1)
                for t in range(4):
                    pe.wait_ge(qk_squared, t + 1)
                    if t >= 2:
                        pe.wait_ge(qk_root, t - 1)
                    sum_tile(t % 2, ones[:, 2, :], n_sq[:, t % 2, :]).then_inc(qk_summed, 1)
                pe.wait_ge(lam_products, 1)
                pe.matmul(ps[:, 7, 0:2], ones[0:32, 0, :], coef[0:32, 2:4], start=True, stop=True).then_inc(lam_sums, 1)
                pe.wait_ge(queries_placed, 1)
                for p in range(4):
                    if p:
                        pe.wait_ge(sample_max, p)
                    for b2 in range(2):
                        pe.wait_ge(keys_loaded[b2], 16 * PAGES * (p + 1))
                        for j in range(2):
                            r0 = 64 * b2 + 32 * j
                            q = qbd[:, j, 2 * p + b2, :]
                            for half in range(2):
                                pe.matmul(ps[r0:r0 + 32, half, :], q, kpage[:, b2, 4 * half:4 * half + 4, j, :], start=True, stop=True)
                            mm = pe.matmul(ps[r0:r0 + 32, 2, 0:TS], q, Z[:, DK + j, 0:TS], start=True, stop=True)
                    mm.then_inc(sample_scores, 1)
                    pe.wait_ge(sample_scaled, p + 1)
                    for s in range(8):
                        pe.transpose(ps[:, 3 + s // 4, s % 4 * P:(s % 4 + 1) * P], s_prob[:, s * P:(s + 1) * P], ident[:, :])
                    pe.transpose(ps[0:TS, 5, 0:P], s_prob[:, PAST:PAST + TS], ident[:, :]).then_inc(sample_turned, 1)
                    pe.wait_ge(sample_pt, 2 * (p + 1))
                    for b2 in range(2):
                        pe.wait_ge(values_loaded[b2], 16 * PAGES * (p + 1))
                        for j in range(2):
                            r0 = 64 * b2 + 32 * j
                            for s in range(PAGES):
                                pe.matmul(ps[:, 6, r0:r0 + 32], vpage[:, b2, s, P * j:P * j + P], s_turn[:, s, r0:r0 + 32],
                                          start=s == 0, stop=False)
                            mm = pe.matmul(ps[:, 6, r0:r0 + 32], V[0:TS, 0, 512 + P * j:512 + P * j + P], s_turn[0:TS, 8, r0:r0 + 32],
                                           start=False, stop=True)
                    mm.then_inc(sample_pv, 1)

            def attention_prompt():
                steps = [(j, h) for j in range(WINDOWS) for h in range(H)]

                def scores(x):
                    j, h = steps[x]
                    c0, n = (TS, META) if j == 0 else window(j)
                    ns = META + P * j
                    if x:
                        pe.wait_ge(prompt_max, x)
                    for i in range(2):
                        r0 = 32 * (2 * (h % 2) + i)
                        q = Z[r0:r0 + 32, DQ + h // 2, c0:c0 + n]
                        k = Z[r0:r0 + 32, DK + h // 2, TS:TS + ns]
                        mm = pe.matmul(ps[0:n, 2 * i, 0:min(ns, 512)], q, k[:, 0:min(ns, 512)], start=True, stop=True)
                        if ns > 512:
                            mm = pe.matmul(ps[0:n, 2 * i + 1, 0:ns - 512], q, k[:, 512:ns], start=True, stop=True)
                    mm.then_inc(prompt_scores, 1)

                pe.wait_ge(sample_pt, 8)
                pe.wait_ge(sample_copied, 4)
                scores(0)
                for x, (j, h) in enumerate(steps):
                    n = META if j == 0 else P
                    if x + 1 < len(steps):
                        scores(x + 1)
                    pe.wait_ge(prompt_attn, x + 1)
                    if x:
                        pe.wait_ge(prompt_pt, x)
                    for s in range(j):
                        pe.transpose(ps[:, 4 + x % 2, s * P:(s + 1) * P], p_prob[0:n, x % 2, 0, META + s * P:META + (s + 1) * P], ident[0:n, 0:n])
                    pe.transpose(ps[0:META, 6, 0:n], p_prob[0:n, x % 2, 0, 0:META], ident[0:n, 0:n]).then_inc(prompt_turned, 1)
                    pe.wait_ge(prompt_pt, x + 1)
                    if h % 2 == 0 and x:
                        pe.wait_ge(prompt_evac, x // 2)
                    r0 = 64 * (h % 2)
                    vc = 512 + 64 * h
                    for s in range(j):
                        pe.matmul(ps[r0:r0 + 64, 7, 0:n], V[:, s + 1, vc:vc + 64], p_turn[:, x % 2, s * P:(s + 1) * P], start=s == 0, stop=False)
                    pe.matmul(ps[r0:r0 + 64, 7, 0:n], V[64:64 + META, 0, vc:vc + 64], p_meta[64:64 + META, x % 2, 0:n],
                              start=j == 0, stop=True).then_inc(prompt_pv, 1)

            def retention():
                pe.wait_ge(prompt_evac, 10)
                pe.wait_ge(ret_tables_loaded, 16 * 8)
                for t in range(4):
                    if t >= 2:
                        pe.wait_ge(rope_turned, t - 1)
                    sum_tile(t % 2, perm[:, :], Z[:, RQ + t, :]).then_inc(rope_swapped, 1)
                pe.wait_ge(ret_scaled, 1)
                for w in range(WINDOWS):
                    c0, n = window(w)
                    if w >= 2:
                        pe.wait_ge(ret_keys, w - 1)
                    pe.transpose(ps[0:n, w % 2, 0:P], rkh[:, 0, c0:c0 + n], ident[:, :])
                    pe.transpose(ps[0:n, w % 2, P:2 * P], rkh[:, 1, c0:c0 + n], ident[:, :]).then_inc(ret_blocks, 1)

                def scores(w):
                    c0, n = window(w)
                    if w >= 2:
                        pe.wait_ge(ret_decayed, w - 1)
                    for h in range(H):
                        r0 = 64 * (h % 2)
                        mm = pe.matmul(ps[0:n, 2 * (w % 2) + h % 2, h // 2 * n:(h // 2 + 1) * n], Z[r0:r0 + 64, RK + h // 2, c0:c0 + n],
                                       Z[r0:r0 + 64, RQ + h // 2, c0:c0 + n], start=True, stop=True)
                    mm.then_inc(ret_scores, 1)

                pe.wait_ge(ret_keys, WINDOWS)
                scores(0)
                for w in range(WINDOWS):
                    c0, n = window(w)
                    if w + 1 < WINDOWS:
                        scores(w + 1)
                    pe.wait_ge(ret_decayed, w + 1)
                    if w >= 2:
                        pe.wait_ge(ret_evac, w - 1)
                    if w:
                        pe.wait_ge(ret_state, w)
                    for j in range(2):
                        out = ps[:, 4 + w % 2, P * j:P * j + n]
                        for i in range(2):
                            h = 2 * j + i
                            pe.matmul(out[64 * i:64 * i + 64, :], V[0:n, w, 64 * h:64 * h + 64], rsc[0:n, w % 2, h * n:(h + 1) * n],
                                      start=True, stop=True)
                        if w:
                            mm = pe.matmul(out, rst[:, j, :], rqh[:, j, c0:c0 + n], start=False, stop=True, skip_group_check=True)
                        else:
                            for b in range(NB):
                                mm = pe.matmul(out[:, NT * b:NT * b + NT], ss[:, j, b, :], rqh[:, j, NT * b:NT * b + NT],
                                               start=False, stop=True, skip_group_check=True)
                    mm.then_inc(ret_mixed, 1)
                    r0, rows = (64, META) if w == 0 else (0, P)
                    for j in range(2):
                        mm = pe.matmul(ps[:, 6 + w % 2, P * j:P * j + P], rkt[r0:r0 + rows, w, j, :], V[r0:r0 + rows, w, P * j:P * j + P],
                                       start=True, stop=True)
                    mm.then_inc(ret_update, 1)
                pe.wait_ge(ret_spread, 1)
                pe.wait_ge(ret_decayed, WINDOWS)
                for j in range(2):
                    for half in range(2):
                        mm = pe.matmul(ps[:, 2 * j + half, :], rkt[0:TS, 0, j, :], vm[0:TS, j, 4 * half:4 * half + 4, :], start=True, stop=True)
                mm.then_inc(ret_s_update, 1)

            def gla():
                pe.wait_ge(ret_s_state, 1)
                pe.wait_ge(gla_tables_loaded, 16 * 6)
                for half in range(2):
                    mm = pe.matmul(ps[:, half, 0:HALF], aw[96:112, :], GL[:, half * HALF:(half + 1) * HALF], start=True, stop=True)
                mm.then_inc(alpha_product, 1)
                pe.wait_ge(gla_scaled, 1)
                for w in range(WINDOWS):
                    c0, n = window(w)
                    if w == 0:
                        pe.wait_ge(ret_evac, WINDOWS)
                    if w >= 2:
                        pe.wait_ge(gla_keys, w - 1)
                    pe.transpose(ps[0:n, 4 + w % 2, 0:P], g_kh[:, c0:c0 + n], ident[:, :]).then_inc(gla_blocks, 1)
                for idx, (n, w) in enumerate(level_items):
                    c0, cols = window(w)
                    pe.wait_ge(lvl_ready, n + 1)
                    if idx >= 2:
                        pe.wait_ge(lvl_taken, idx - 1)
                    if idx == 1:
                        pe.wait_ge(gla_keys, WINDOWS)
                    for h in range(H):
                        if n == 0:
                            k, q = Z[32 * h:32 * h + 32, GK, :], Z[32 * h:32 * h + 32, GQ, :]
                        else:
                            k, q = g_kl[32 * h:32 * h + 32, n % 2, :], g_ql[32 * h:32 * h + 32, n % 2, :]
                        mm = pe.matmul(ps[0:cols, 4 * (idx % 2) + h, 0:cols], k[:, c0:c0 + cols], q[:, c0:c0 + cols], start=True, stop=True)
                    mm.then_inc(lvl_scores, 1)
                pe.wait_ge(lvl_taken, len(level_items))
                for w in range(WINDOWS):
                    c0, n = window(w)
                    if w >= 2:
                        pe.wait_ge(gla_evac, w - 1)
                    if w:
                        pe.wait_ge(gla_state, w)
                    for j in range(2):
                        out = ps[:, 6 + w % 2, P * j:P * j + n]
                        for i in range(2):
                            h = 2 * j + i
                            pe.matmul(out[64 * i:64 * i + 64, :], V[0:n, w, 256 + 64 * h:320 + 64 * h], g_sc[0:n, w, h * n:(h + 1) * n],
                                      start=True, stop=True)
                        if w:
                            mm = pe.matmul(out, g_st[:, P * j:P * j + P], g_qh[:, c0:c0 + n], start=False, stop=True, skip_group_check=True)
                        else:
                            for b in range(NB):
                                mm = pe.matmul(out[:, NT * b:NT * b + NT], g_ss[:, b, P * j:P * j + P], g_qh[:, NT * b:NT * b + NT],
                                               start=False, stop=True, skip_group_check=True)
                    mm.then_inc(gla_mixed, 1)
                    r0, rows = (64, META) if w == 0 else (0, P)
                    pe.matmul(ps[:, 4 + w % 2, 0:256], g_kt[r0:r0 + rows, w, :], V[r0:r0 + rows, w, 256:512], start=True, stop=True).then_inc(gla_update, 1)
                pe.wait_ge(gla_spread, 1)
                for q in range(4):
                    mm = pe.matmul(ps[:, q, :], g_kt[0:TS, 0, :], g_vm[0:TS, 2 * q:2 * q + 2, :], start=True, stop=True)
                mm.then_inc(gla_s_update, 1)

            def head_norms():
                pe.wait_ge(gla_s_state, 1)
                for i, (src, c, gain, o, width, center, shared) in enumerate(HEAD_NORMS):
                    if center:
                        if i == 3:
                            pe.wait_ge(conv_done, 1)
                        pe.wait_ge(hn_normed, 2 * i)
                        for j in range(2):
                            for n, t in enumerate((0, 1) if shared else (j,)):
                                mm = sum_tile(j, ones[:, o, :], src[:, c + t, :], start=n == 0, stop=n == shared)
                        mm.then_inc(hn_summed, 1)
                    pe.wait_ge(hn_squared, 2 * i + 2)
                    if i:
                        pe.wait_ge(hn_root_ready, 2 * i)
                    for j in range(2):
                        for n, t in enumerate((0, 1) if shared else (j,)):
                            mm = sum_tile(2 + j, ones[:, o, :], hn_sq[:, t, :], start=n == 0, stop=n == shared)
                        mm.then_inc(hn_totalled, 1)

            def gates(l):
                pe.wait_ge(br_split, 8)
                with pe.Fori(0, 2) as i:
                    for mm_ in range(4):
                        m = i * 4 + mm_
                        for n in range(5):
                            pos = mm_ * 5 + n
                            quad, slot = l * QUADS + U_GATES // RING + i * 5 + pos // RING, pos % RING
                            unit_ready(quad, slot)
                            if n < 4:
                                pe.wait_ge(branch_taken, m * 4 + n + 1)
                                products(n, slot, (0, 8), 0, x_hi, x_lo).then_inc(units_multiplied, 1)
                            else:
                                for b in range(4):
                                    pe.wait_ge(gate_tanh, m * 4 + b + 1)
                                    last = products(b, slot, (2 * b, 2 * b + 2), 2 * b, br_hi, br_lo)
                                    last.then_inc(*((branch_products, 1) if b < 3 else (units_multiplied, 1)))
                pe.wait_ge(merged_ready, KD)
                pe.drain().then_inc(mixers_left, 1)

            pe.sem_inc(units_multiplied, RING)
            pe.wait_ge(consts_loaded, 16 * CONSTS)
            pe.wait_ge(bias_row_made, 1)
            for n, c in enumerate(range(0, RL, 512)):
                mm = pe.matmul(ps[0:16, 4 + n, 0:min(512, RL - c)], rb[0:33, :], bucket[0:33, c:min(c + 512, RL)], start=True, stop=True)
            mm.then_inc(bias_row_made, 1)
            with pe.Fori(0, DEPTH) as l:
                norm(l, 0)
                gate_up(l, 0, U_FFN1)
                pe.wait_ge(hidden_ready, l * 2 * KF + KF)
                pe.sem_inc(phases_entered, 1)
                residual(l, 0, U_DOWN1, DOWN_BLOCKS, hid_hi, hid_lo)
                norm(l, 1)
                project(l)
                attention_sample()
                attention_prompt()
                retention()
                gla()
                head_norms()
                gates(l)
                residual(l, 8, U_OUT, (8,), m_hi, m_lo)
                norm(l, 2)
                gate_up(l, 1, U_FFN2)
                pe.wait_ge(hidden_ready, l * 2 * KF + 2 * KF)
                pe.sem_inc(phases_entered, 1)
                residual(l, 16, U_DOWN2, DOWN_BLOCKS, hid_hi, hid_lo)

        @block.vector
        def _(v):
            def split_low(quad, slot):
                v.wait_ge(weights_high, 4 * quad + slot + 1)
                v.tensor_tensor(w_lo[:, slot, :, :], w_raw[:, slot, :, :], w_hi[:, slot, :, :].bitcast(F32), ALU.subtract).then_inc(weights_low, 1)

            def unit_done(quad, slot):
                v.wait_ge(units_multiplied, 4 * quad + slot + 1 + RING)

            def norm(l, i):
                w = l * 3 + i
                v.wait_ge(root_ready, w + 1)
                if i == 0:
                    v.wait_ge(params_loaded, 16 * (l + 1))
                v.memset(ssum[:, :], 0.0)
                v.reciprocal(tmp[:, 0, :], tmp[:, 0, :]).then_inc(inverse_ready, 1)
                v.wait_ge(inverse_ready, w + 1)

                def low(k):
                    v.wait_ge(x_high, 8 * w + k + 1)
                    v.wait_ge(normed, 8 * w + k + 1)
                    v.tensor_tensor(x_lo[:, k, :], fresh[k % 3], x_hi[:, k, :].bitcast(F32), ALU.subtract).then_inc(x_ready, 1)

                for k in range(KD):
                    c = P_GAIN + 8 * i + k
                    if k >= 3:
                        v.wait_ge(x_ready, 8 * w + k - 2)
                    v.scalar_tensor_tensor(fresh[k % 3], hT[:, k, :], prm[:, c:c + 1], tmp[:, 0, :], ALU.mult, ALU.mult).then_inc(normed, 1)
                    if k:
                        low(k - 1)
                low(KD - 1)

            def gate_up(l, f, first):
                with v.Fori(0, KF // 2) as i:
                    for j in range(2):
                        q = l * 2 * KF + f * KF + i * 2 + j
                        quad = l * QUADS + first // RING + i
                        v.wait_ge(tanh_ready, q + 1)
                        v.scalar_tensor_tensor(split_cols(gu[:, j, :]), split_cols(tmp[:, j, :]), 1.0, pair(2 * j), ALU.add, ALU.mult).then_inc(gated, 1)
                        split_low(quad + 1, 2 * j)
                        unit_done(quad, 2 * j + 1)
                        v.wait_ge(gated, q + 1)
                        v.tensor_tensor(split_cols(gu[:, j, :]), split_cols(gu[:, j, :]), pair(2 * j + 1), ALU.mult).then_inc(hidden_made, 1)
                        split_low(quad + 1, 2 * j + 1)
                        v.wait_ge(hidden_made, q + 3)
                        v.wait_ge(hidden_high, q + 1)
                        v.tensor_tensor(hid_lo[:, ds(i * 2 + j, 1), :], gu[:, j:j + 1, :], hid_hi[:, ds(i * 2 + j, 1), :].bitcast(F32), ALU.subtract).then_inc(hidden_ready, 1)

            def residual(l, r0, first, units, scale):
                with v.Fori(0, 2) as i:
                    for j in range(4):
                        r = l * 24 + r0 + i * 4 + j
                        for u in range(units):
                            pos = j * units + u
                            quad, slot = l * QUADS + first // RING + i * units + pos // RING, pos % RING
                            if u == units - 1:
                                unit_done(quad, slot)
                                tile = hT[:, ds(i * 4 + j, 1), :].rearrange("p a (h t) -> p (a h) t", h=2)
                                v.scalar_tensor_tensor(tile, pair(j), scale, tile, ALU.mult, ALU.add).then_inc(residual_added, 1)
                            split_low(quad + 1, slot)
                        v.wait_ge(squared, 9 + r)
                        v.wait_ge(squares_summed, 8 + r)
                        v.tensor_tensor(ssum[:, :], ssum[:, :], tmp[:, j % 2, :], ALU.add).then_inc(squares_summed, 1)

            chain = [0]

            def link(ins):
                chain[0] += 1
                ins.then_inc(vector_chain, 1)
                v.wait_ge(vector_chain, chain[0])

            def project(l):
                v.wait_ge(mixers_open, l + 1)
                v.sem_inc(phases_entered, 1)
                v.wait_ge(vb_loaded, 16)
                for g in range(3):
                    for w in range(WINDOWS):
                        n = window(w)[1]
                        idx = WINDOWS * g + w
                        quad = l * QUADS + U_MIX // RING + 2 * g // RING
                        if w < WINDOWS - 1:
                            v.wait_ge(v_products, 4 * g + w + 1)
                        else:
                            unit_done(quad, 2 * g % RING + 1)
                        v.tensor_tensor(V[0:n, w, 256 * g:256 * g + 256], ps[0:n, idx % 8, 0:256], vb[0:n, 256 * g:256 * g + 256], ALU.add).then_inc(v_ready, 1)
                    for s in range(2):
                        split_low(quad + 1, 2 * g % RING + s)
                v.wait_ge(low_high, 1)
                v.tensor_tensor(low_lo[:, :, :], low_raw[:, :, :], low_hi[:, :, :].bitcast(F32), ALU.subtract).then_inc(low_split, 1)
                for c in range(NZ):
                    pos = c + 6
                    split_low(l * QUADS + U_MIX // RING + pos // RING + 1, pos % RING)

            def attention_sample():
                v.tensor_tensor(coef[0:32, 2:4], prm[0:32, P_LAM:P_LAM + 2], prm[0:32, P_LAM + 2:P_LAM + 4], ALU.mult).then_inc(lam_products, 1)
                v.tensor_scalar(hb[:, :], prm[:, P_GB:P_GB + 32], 0.5, None, ALU.mult)
                for t in range(4):
                    v.wait_ge(qk_root, t + 1)
                    link(v.reciprocal(n_root[:, t % 2, :], n_root[:, t % 2, :]))
                    c = P_QN if t < 2 else P_KN
                    v.scalar_tensor_tensor(Z[:, t, :], Z[:, t, :], prm[:, c:c + 1], n_root[:, t % 2, :], ALU.mult, ALU.mult).then_inc(qk_normed, 1)
                v.wait_ge(lam_exps, 1)
                link(v.tensor_tensor(coef[:, 4:5], coef[:, 3:4], coef[:, 2:3], ALU.subtract))
                link(v.tensor_tensor(coef[:, 4:5], coef[:, 4:5], prm[:, P_LI:P_LI + 1], ALU.subtract))
                v.scalar_tensor_tensor(coef[:, 5:6], coef[:, 1:2], coef[:, 4:5], coef[:, 0:1], ALU.mult, ALU.add)
                link(v.memset(qbd[:, :, :, :], 0.0))
                v.wait_ge(qk_normed, 4)
                for j in range(2):
                    for g in range(4):
                        ins = v.tensor_copy(qbd[32 * g:32 * g + 32, j, :, 8 * g:8 * g + 8],
                                            Z[32 * g:32 * g + 32, DQ + j, 0:TS].rearrange("p (b t) -> p b t", b=NB))
                ins.then_inc(queries_placed, 1)
                v.wait_ge(attn_tables_loaded, 16 * 9)
                link(v.tensor_tensor(new_bias[:, :, :].rearrange("p a (b s) -> p a b s", s=NT),
                                     new_mask[:, :, :].rearrange("p a (b s) -> p a b s", s=NT),
                                     s_bias[:, None, None, PAST:PAST + NT].to_broadcast([P, 4, NB, NT]), ALU.add))
                for p in range(4):
                    v.wait_ge(sample_scores, p + 1)
                    if p:
                        v.wait_ge(sample_turned, p)
                    link(v.tensor_tensor_reduce(out=s_prob[:, 0:PAST], in0=ps[:, 0:2, :].rearrange("p b c -> p (b c)"), in1=s_bias[:, 0:PAST],
                                                scale=ATT_SCALE, scalar=-3e38, op0=ALU.add, op1=ALU.max, accum_out=coef[:, 7:8]))
                    link(v.tensor_tensor_reduce(out=s_prob[:, PAST:PAST + TS], in0=ps[:, 2, 0:TS], in1=new_bias[:, p, :],
                                                scale=ATT_SCALE, scalar=coef[:, 7:8], op0=ALU.add, op1=ALU.max, accum_out=coef[:, 6:7]))
                    v.tensor_scalar(coef[:, 6:7], coef[:, 6:7], -1.0, None, ALU.mult).then_inc(sample_max, 1)
                    v.wait_ge(sample_exp, p + 1)
                    link(v.reciprocal(coef[:, 7:8], coef[:, 7:8]))
                    link(v.tensor_tensor(coef[:, 7:8], coef[:, 7:8], coef[:, 5:6], ALU.mult))
                    v.tensor_scalar(s_prob[:, :], s_prob[:, :], coef[:, 7:8], None, ALU.mult).then_inc(sample_scaled, 1)
                    v.wait_ge(sample_copied, p + 1)
                    for h2 in range(2):
                        rows = s_out[64 * h2:64 * h2 + 64, :].rearrange("p (b j r) -> p b j r", b=2, j=2)
                        for j in range(2):
                            ins = v.tensor_tensor(od[64 * h2:64 * h2 + 64, j, 2 * NT * p:2 * NT * (p + 1)].rearrange("p (b t) -> p b t", b=2),
                                                  rows[:, :, j, 16 * h2:16 * h2 + 8], rows[:, :, j, 16 * h2 + 8:16 * h2 + 16], ALU.add)
                    ins.then_inc(sample_placed, 1)

            def attention_prompt():
                steps = [(j, h) for j in range(WINDOWS) for h in range(H)]

                def biased(x):
                    j, h = steps[x]
                    n = META if j == 0 else P
                    ns = META + P * j
                    t0 = 0 if j == 0 else META + P * (j - 1)
                    v.wait_ge(prompt_scores, x + 1)
                    if x >= 2:
                        v.wait_ge(prompt_turned, x - 1)
                    for i in range(2):
                        src = ps[0:n, 2 * i:2 * i + 2, :].rearrange("p b c -> p (b c)")[:, 0:ns]
                        ins = v.tensor_tensor_reduce(out=p_prob[0:n, x % 2, i, 0:ns], in0=src, in1=p_bias[0:n, h, LP - P - t0:LP - P - t0 + ns],
                                                     scale=ATT_SCALE, scalar=-3e38, op0=ALU.add, op1=ALU.max, accum_out=small[0:n, x % 2, 4 + i:5 + i])
                    link(ins)
                    v.tensor_scalar(small[0:n, x % 2, 0:2], small[0:n, x % 2, 4:6], -1.0, None, ALU.mult).then_inc(prompt_max, 1)

                v.wait_ge(prompt_bias_loaded, 16)
                v.wait_ge(sample_turned, 4)
                biased(0)
                for x, (j, h) in enumerate(steps):
                    n = META if j == 0 else P
                    ns = META + P * j
                    if x + 1 < len(steps):
                        biased(x + 1)
                    v.wait_ge(prompt_exp, 2 * (x + 1))
                    sums = small[0:n, x % 2, 2:4]
                    link(v.reciprocal(sums, sums))
                    link(v.tensor_tensor(sums[:, 1:2], sums[:, 1:2], coef[0:n, 4:5], ALU.mult))
                    one, two = p_prob[0:n, x % 2, 0, 0:ns], p_prob[0:n, x % 2, 1, 0:ns]
                    link(v.tensor_scalar(one, one, sums[:, 0:1], None, ALU.mult))
                    v.scalar_tensor_tensor(one, two, sums[:, 1:2], one, ALU.mult, ALU.add).then_inc(prompt_attn, 1)

            def by_window(ap, j=None):
                return ap[:, TS + META:T].rearrange("p (w t) -> p w t", t=P)

            def retention():
                v.wait_ge(ret_tables_loaded, 16 * 8)
                v.wait_ge(prompt_pt, 20)
                v.wait_ge(prompt_pv, 20)
                for t in range(4):
                    a, b = rtmp[:, t % 2, 0, :], rtmp[:, t % 2, 1, :]
                    scale = 1.0 if t < 2 else 64 ** -0.5
                    v.scalar_tensor_tensor(a, Z[:, RQ + t, :], scale, rope[:, 0, :], ALU.mult, ALU.mult)
                    v.wait_ge(rope_swapped, t + 1)
                    link(v.scalar_tensor_tensor(split_cols(b), pair(t % 2), scale, split_cols(rope[:, 1, :]), ALU.mult, ALU.mult))
                    v.tensor_tensor(Z[:, RQ + t, :], a, b, ALU.add).then_inc(rope_turned, 1)
                v.wait_ge(rope_turned, 4)
                v.memset(rst[:, :, :], 0.0)
                for src, table, dst in ((RQ, gq, rqh), (RK, gk, rkh)):
                    for j in range(2):
                        v.tensor_tensor(dst[:, j, 0:80], Z[:, src + j, 0:80], table[:, j, 0:80], ALU.mult)
                        ins = v.tensor_tensor(by_window(dst[:, j, :]), by_window(Z[:, src + j, :]),
                                              table[:, j:j + 1, 80:208].to_broadcast([P, 4, P]), ALU.mult)
                ins.then_inc(ret_scaled, 1)

                def decayed(w):
                    n = window(w)[1]
                    v.wait_ge(ret_scores, w + 1)
                    if w >= 2:
                        v.wait_ge(ret_mixed, w - 1)
                    table = dec[:, :, :] if w else dec0[0:80, :, :]
                    src = ps[0:n, 2 * (w % 2):2 * (w % 2) + 2, 0:2 * n].rearrange("p i (j t) -> p i j t", j=2)
                    v.tensor_tensor(rsc[0:n, w % 2, 0:H * n].rearrange("p (j i t) -> p i j t", j=2, i=2), src,
                                    table.rearrange("p (j i) t -> p i j t", j=2), ALU.mult).then_inc(ret_decayed, 1)

                decayed(0)
                for w in range(WINDOWS):
                    if w + 1 < WINDOWS:
                        decayed(w + 1)
                    v.wait_ge(ret_mixed, w + 1)
                    v.wait_ge(ret_update, w + 1)
                    if w:
                        v.wait_ge(ret_state, w)
                    for h in range(H):
                        j, r = h // 2, 64 * (h % 2)
                        block_ = rst[r:r + 64, j, r:r + 64]
                        ins = v.scalar_tensor_tensor(block_, block_, float(GAMMA[h] ** P), ps[r:r + 64, 6 + w % 2, P * j + r:P * j + r + 64], ALU.mult, ALU.add)
                    ins.then_inc(ret_state, 1)
                for j in range(2):
                    ins = v.tensor_tensor(vm[0:TS, j, :, :], V[0:TS, 0:1, P * j:P * j + P].to_broadcast([TS, NB, P]),
                                          seqs[0:TS, :, None].to_broadcast([TS, NB, P]), ALU.mult)
                ins.then_inc(ret_spread, 1)
                v.wait_ge(ret_s_update, 1)
                for h in range(H):
                    j, r = h // 2, 64 * (h % 2)
                    block_ = ss[r:r + 64, j, :, r:r + 64]
                    new = ps[r:r + 64, 2 * j:2 * j + 2, :].rearrange("p q (b n) -> p (q b) n", b=4)[:, :, r:r + 64]
                    ins = v.scalar_tensor_tensor(block_, block_, float(GAMMA[h] ** NT), new, ALU.mult, ALU.add)
                ins.then_inc(ret_s_state, 1)

            def gla():
                v.wait_ge(gla_tables_loaded, 16 * 6)
                v.wait_ge(alpha_log, 1)
                a, b = g_e[:, 0, :], g_e[:, 1, :]
                link(v.scalar_tensor_tensor(a, a, 0.0, b, ALU.min, ALU.subtract))
                link(v.tensor_scalar(a, a, 1.0 / 16, None, ALU.mult))
                v.tensor_tensor_scan(g_b, reset[:, :], a, 0.0, ALU.mult, ALU.add).then_inc(gla_summed, 1)
                v.wait_ge(gla_summed, 1)
                for c0, n, size in ((0, NB, NT), (TS, 1, META), (TS + META, 4, P)):
                    src = g_b[:, c0:c0 + n * size].rearrange("p (n t) -> p n t", n=n)
                    ins = v.tensor_tensor(b[:, c0:c0 + n * size].rearrange("p (n t) -> p n t", n=n),
                                          src[:, :, size - 1:size].to_broadcast([P, n, size]), src, ALU.subtract)
                ins.then_inc(gla_diff, 1)
                link(v.tensor_scalar(Z[:, GQ, :], Z[:, GQ, :], 32 ** -0.5, None, ALU.mult))
                v.wait_ge(gla_exp_b, 1)
                v.tensor_tensor(g_qh[:, :], Z[:, GQ, :], g_eb, ALU.mult)
                v.wait_ge(gla_exp_last, 1)
                v.tensor_tensor(g_kh[:, :], Z[:, GK, :], b, ALU.mult).then_inc(gla_scaled, 1)
                link(v.memset(g_st[:, :], 0.0))
                v.memset(Z[:, 0:4, :], 0.0).then_inc(lvl_ready, 1)

                def difference(n):
                    size = LEVELS[n]
                    c0 = level_start(size)
                    src = g_b[:, c0:T].rearrange("p (n b) -> p n b", b=size)
                    if n == 1:
                        v.wait_ge(gla_scaled, 1)
                    if n >= 2:
                        v.wait_ge(lvl_ready, n)
                    v.tensor_tensor(g_e[:, n % 2, c0:T].rearrange("p (n b) -> p n b", b=size), src,
                                    src[:, :, size // 2 - 1:size // 2].to_broadcast([P, (T - c0) // size, size]), ALU.subtract).then_inc(lvl_diff, 1)

                def take(n):
                    for idx, (m, w) in enumerate(level_items):
                        if m != n:
                            continue
                        cols = window(w)[1]
                        v.wait_ge(lvl_scores, idx + 1)
                        src = ps[0:cols, 4 * (idx % 2):4 * (idx % 2) + 4, 0:cols]
                        dst = g_sc[0:cols, w, 0:H * cols].rearrange("p (h t) -> p h t", h=H)
                        m0 = max(n - 3, 0)
                        mask = (lvl[:, n:n + 1, :] if w else lvl0[0:80, m0:m0 + 1, :]).to_broadcast([cols, H, cols])
                        if n == 0:
                            v.tensor_tensor(dst, src, mask, ALU.mult).then_inc(lvl_taken, 1)
                        else:
                            v.copy_predicated(dst, mask.bitcast(U32), src).then_inc(lvl_taken, 1)

                difference(0)
                for n, size in enumerate(LEVELS):
                    c0 = level_start(size)

                    def half(ap, part):
                        view = ap[:, c0:T].rearrange("p (n b) -> p n b", b=size)
                        return view[:, :, size // 2:size] if part else view[:, :, 0:size // 2]

                    if n + 1 < len(LEVELS):
                        difference(n + 1)
                    v.wait_ge(lvl_exp, 2 * (n + 1))
                    if n >= 2:
                        v.wait_ge(lvl_scores, items_through(n - 1))
                    v.tensor_tensor(half(g_kl[:, (n + 1) % 2, :], 0), half(Z[:, GK, :], 0), half(g_e[:, n % 2, :], 0), ALU.mult)
                    v.tensor_tensor(half(g_ql[:, (n + 1) % 2, :], 1), half(Z[:, GQ, :], 1), half(g_e[:, n % 2, :], 1), ALU.mult).then_inc(lvl_ready, 1)
                    if n:
                        v.wait_ge(lvl_taken, items_through(n - 1))
                    take(n)
                v.wait_ge(lvl_taken, items_through(len(LEVELS) - 1))
                take(len(LEVELS))
                for w in range(WINDOWS):
                    v.wait_ge(gla_mixed, w + 1)
                    v.wait_ge(gla_update, w + 1)
                    if w:
                        v.wait_ge(gla_state, w)
                    last = window(w)[0] + window(w)[1] - 1
                    for h in range(H):
                        block_ = g_st[32 * h:32 * h + 32, 64 * h:64 * h + 64]
                        ins = v.scalar_tensor_tensor(block_, block_, g_eb[32 * h:32 * h + 32, last:last + 1],
                                                     ps[32 * h:32 * h + 32, 4 + w % 2, 64 * h:64 * h + 64], ALU.mult, ALU.add)
                    ins.then_inc(gla_state, 1)
                v.tensor_tensor(g_vm[0:TS, :, :], V[0:TS, 0:1, 256:512].to_broadcast([TS, NB, 256]),
                                g_seqs[0:TS, :, None].to_broadcast([TS, NB, 256]), ALU.mult).then_inc(gla_spread, 1)
                for h in range(H):
                    block_ = g_ss[32 * h:32 * h + 32, :, 64 * h:64 * h + 64]
                    decay = g_eb[32 * h:32 * h + 32, 0:TS].rearrange("p (b t) -> p b t", b=NB)[:, :, NT - 1:NT].to_broadcast([32, NB, 64])
                    ins = v.tensor_tensor(block_, block_, decay, ALU.mult)
                link(ins)
                v.wait_ge(gla_s_update, 1)
                for h in range(H):
                    block_ = g_ss[32 * h:32 * h + 32, :, 64 * h:64 * h + 64]
                    new = ps[32 * h:32 * h + 32, 0:4, :].rearrange("p q (b n) -> p (q b) n", b=2)[:, :, 64 * h:64 * h + 64]
                    ins = v.tensor_tensor(block_, block_, new, ALU.add)
                ins.then_inc(gla_s_state, 1)

            def conv():
                v.wait_ge(mixers_stored, 16 * 7)
                for j in range(2):
                    ins = v.memset(ue[:, j, UE_S:UE_S + 30], 0.0)
                ins.then_inc(conv_gated, 1)
                for j in range(2):
                    v.wait_ge(conv_tanh, j + 1)
                    v.scalar_tensor_tensor(Z[:, CA + j, :], Z[:, CG + j, :], 1.0, Z[:, CA + j, :], ALU.add, ALU.mult).then_inc(conv_gated, 1)
                v.wait_ge(conv_rows, 4)
                for k in range(CK):
                    for j in range(2):
                        tap = prm[:, P_CW + CK * j + k:P_CW + CK * j + k + 1]
                        for part in range(2):
                            if part:
                                src = ue[:, j, UE_S + k:UE_S + k + LP]
                                dst = Z[:, CG + j, TS:T]
                            else:
                                src = ue[:, j, 0:UE_S].rearrange("p (b r) -> p b r", r=38)[:, :, k:k + NT]
                                dst = Z[:, CG + j, 0:TS].rearrange("p (b t) -> p b t", b=NB)
                            if k == 0:
                                ins = v.tensor_scalar(dst, src, tap, prm[:, P_CB + j:P_CB + j + 1], ALU.mult, ALU.add)
                            else:
                                v.wait_ge(vector_chain, chain[0] - 3)
                                ins = v.scalar_tensor_tensor(dst, src, tap, dst, ALU.mult, ALU.add)
                            ins.then_inc(vector_chain, 1)
                            chain[0] += 1
                v.wait_ge(vector_chain, chain[0])
                v.sem_inc(conv_done, 1)

            def head_norms():
                for i, (src, c, gain, o, width, center, shared) in enumerate(HEAD_NORMS):
                    if center:
                        v.wait_ge(hn_summed, centered_before(i) + 1)
                        for j in range(2):
                            v.scalar_tensor_tensor(split_cols(src[:, c + j, :]), pair(j), -1.0 / width, split_cols(src[:, c + j, :]),
                                                   ALU.mult, ALU.add).then_inc(hn_centered, 1)
                        v.wait_ge(hn_centered, 2 * i + 2)
                    else:
                        v.wait_ge((prompt_evac, None, gla_evac)[i], (10, None, WINDOWS)[i])
                        v.sem_inc(hn_centered, 2)
                    if i == 0:
                        link(v.tensor_tensor(coef[:, 6:7], prm[:, P_SUB:P_SUB + 1], prm[:, P_LI1:P_LI1 + 1], ALU.mult))
                    for j in range(2):
                        v.wait_ge(hn_root_ready, 2 * i + j + 1)
                        link(v.reciprocal(hn_root[:, j, :], hn_root[:, j, :]))
                        g = coef[:, 6:7] if gain is None else prm[:, gain + j:gain + j + 1]
                        v.scalar_tensor_tensor(src[:, c + j, :], src[:, c + j, :], g, hn_root[:, j, :], ALU.mult, ALU.mult).then_inc(hn_normed, 1)

            def branches():
                v.wait_ge(hn_normed, 8)
                for j in range(2):
                    ins = v.tensor_scalar(Z[:, CG + j, :], Z[:, CG + j, :], prm[:, P_LB + j:P_LB + j + 1], None, ALU.add)
                ins.then_inc(conv_done, 1)
                for n, c in enumerate((RG, RG + 1, GR, GR + 1)):
                    v.wait_ge(act_tanh, n + 1)
                    link(v.scalar_tensor_tensor(Z[:, c, :], Z[:, TG + n, :], 1.0, Z[:, c, :], ALU.add, ALU.mult))
                    out = branch_tiles[2 + n]
                    v.scalar_tensor_tensor(out, Z[:, c, :], 0.5, out, ALU.mult, ALU.mult).then_inc(br_ready, 1)
                v.wait_ge(conv_done, 2)
                for n in range(2):
                    v.wait_ge(act_tanh, 5 + n)
                    link(v.tensor_scalar(hn_root[:, n, :], hn_root[:, n, :], 1.0, 0.5, ALU.add, ALU.mult))
                    v.tensor_tensor(branch_tiles[n], branch_tiles[n], hn_root[:, n, :], ALU.mult).then_inc(br_ready, 1)
                v.wait_ge(br_ready, 6)
                for n, t in enumerate(branch_tiles):
                    v.wait_ge(br_high, n + 1)
                    v.tensor_tensor(br_lo[:, n, :], t, br_hi[:, n, :].bitcast(F32), ALU.subtract).then_inc(br_split, 1)

            def gates(l):
                v.sem_inc(branch_taken, 4)
                with v.Fori(0, 2) as i:
                    for mm in range(4):
                        m = i * 4 + mm
                        for n in range(4):
                            pos = mm * 5 + n
                            split_low(l * QUADS + U_GATES // RING + i * 5 + pos // RING + 1, pos % RING)
                        pos = mm * 5 + 4
                        quad, slot = l * QUADS + U_GATES // RING + i * 5 + pos // RING, pos % RING
                        for b in range(4):
                            if b < 3:
                                v.wait_ge(branch_products, m * 3 + b + 1)
                            else:
                                unit_done(quad, slot)
                            if b > 1:
                                v.wait_ge(merged_steps, m * 3 + b - 1)
                            v.scalar_tensor_tensor(split_cols(d_acc[:, min(b, 1), :]), split_cols(d_sg[:, b, :]), 1.0, pair(b), ALU.add, ALU.mult
                                                   ).then_inc(branch_taken, 1)
                            if b:
                                v.wait_ge(branch_taken, m * 4 + b + 1 + 4)
                                v.tensor_tensor(d_acc[:, 0, :], d_acc[:, 0, :], d_acc[:, 1, :], ALU.add).then_inc(merged_steps, 1)
                        split_low(quad + 1, slot)
                        v.wait_ge(merged_steps, m * 3 + 3)
                        v.wait_ge(merged_high, m + 1)
                        v.scalar_tensor_tensor(m_lo[:, ds(m, 1), :], d_acc[:, 0:1, :], 0.5, m_hi[:, ds(m, 1), :].bitcast(F32),
                                               ALU.mult, ALU.subtract).then_inc(merged_ready, 1)
                v.drain().then_inc(mixers_left, 1)

            v.sem_inc(weights_low, RING)
            v.sem_inc(hidden_made, 2)
            v.sem_inc(residual_added, 4)
            v.memset(ssum[:, :], 0.0)
            v.wait_ge(consts_loaded, 16 * CONSTS)
            v.tensor_scalar(rb[0:32, :], rb[0:32, :], 1.0 / ATT_SCALE, None, ALU.mult).then_inc(bias_row_made, 1)
            v.wait_ge(bias_row_made, 2)
            v.tensor_copy(brow[:, :], ps[0:16, 4:7, :].rearrange("p b c -> p (b c)")[:, 0:RL]).then_inc(bias_row_made, 1)
            for s in range(RING):
                v.wait_ge(weights_high, s + 1)
                v.tensor_tensor(w_lo[:, s, :, :], w_raw[:, s, :, :], w_hi[:, s, :, :].bitcast(F32), ALU.subtract).then_inc(weights_low, 1)
            for m in range(KD):
                v.wait_ge(squared, m + 1)
                if m:
                    v.wait_ge(squares_summed, m)
                v.tensor_tensor(ssum[:, :], ssum[:, :], tmp[:, m % 2, :], ALU.add).then_inc(squares_summed, 1)
            with v.Fori(0, DEPTH) as l:
                norm(l, 0)
                gate_up(l, 0, U_FFN1)
                residual(l, 0, U_DOWN1, 3, 0.25)
                norm(l, 1)
                project(l)
                attention_sample()
                attention_prompt()
                retention()
                gla()
                conv()
                head_norms()
                branches()
                gates(l)
                residual(l, 8, U_OUT, 1, 1.0)
                norm(l, 2)
                gate_up(l, 1, U_FFN2)
                residual(l, 16, U_DOWN2, 3, 0.25)


def constants():
    f = np.float32
    col = np.arange(T)
    pos = np.where(col < TS, PAST + col % NT, col - TS).astype(np.int32)
    inv = f(10000.0) ** (-np.arange(32, dtype=f) / f(32))
    ang = (pos.astype(f)[None, :] * inv[np.arange(P) % 32][:, None]).astype(f)
    rope = np.stack([np.cos(ang), np.sin(ang)], axis=1).astype(f)
    perm = np.zeros((P, P), f)
    for m in range(P):
        if m % 64 < 32:
            perm[m + 32, m] = -1
        else:
            perm[m - 32, m] = 1
    gam = np.array(GAMMA, np.float64)
    a = np.arange(P)
    d = a[None, :] - a[:, None]
    dec = np.where(d[:, None, :] >= 0, gam[None, :, None] ** np.maximum(d, 0)[:, None, :], 0).astype(f)
    a = np.arange(80)
    d = a[None, :] - a[:, None]
    chunk = np.where(a < TS, a // NT, NB)
    ok = (d >= 0) & (chunk[:, None] == chunk[None, :])
    dec0 = np.where(ok[:, None, :], gam[None, :, None] ** np.maximum(d, 0)[:, None, :], 0).astype(f)
    c = np.arange(208)
    step = np.where(c < TS, c % NT, np.where(c < 80, c - TS, c - 80))
    size = np.where(c < TS, NT, np.where(c < 80, META, P))
    head = 2 * np.arange(2)[None, :] + np.arange(P)[:, None] // 64
    gq = (gam[head][:, :, None] ** (step + 1)).astype(f)
    gk = (gam[head][:, :, None] ** (size - 1 - step)).astype(f)
    seq = (np.arange(TS)[:, None] // NT == np.arange(NB)[None, :]).astype(f)
    starts = (col < TS) & (col % NT == 0) | (col == TS) | (col >= 80) & ((col - 80) % P == 0)
    reset = np.broadcast_to(np.where(starts, 0, 1).astype(f), (P, T)).copy()

    def level(n, b, rows):
        s, t = np.arange(rows)[:, None], np.arange(rows)[None, :]
        if n == 0:
            return s == t
        m = (s // b == t // b) & (s % b < b // 2) & (t % b >= b // 2)
        return m & (s >= TS) if b == META and rows == 80 else m

    lvl = np.stack([level(n, LEVELS[n - 1], P) for n in range(8)], axis=1).astype(f)
    lvl0 = np.stack([level(n, LEVELS[n - 1], 80) for n in (0, 4, 5, 6, 7)], axis=1).astype(f)
    rel = REL - 1 - np.arange(RL)
    n = np.maximum(rel, 0)
    nf = np.maximum(n, 1).astype(f)
    large = 16 + (np.log(nf / f(16)) / f(math.log(8)) * f(16)).astype(np.int32)
    bucket = np.where(n < 16, n, np.minimum(large, 31))
    bucket = np.where(rel < 0, 32, bucket)
    onehot = (np.arange(33)[:, None] == bucket[None, :]).astype(f)
    block_of = [np.arange(P) // b for b in (128, 64, 32)]
    ones = np.stack([(b[:, None] == b[None, :]) for b in block_of], axis=1).astype(f)
    row = np.arange(P)
    seq_of = 2 * np.arange(4)[None, :] + row[:, None] // 64
    newmask = np.where(seq_of[:, :, None] == (np.arange(TS) // NT)[None, None, :], 0, NEG).astype(f)
    part = row // 8 % 2
    coef = np.stack([part == 0, part == 1], axis=1).astype(f)
    return dict(c_bucket=onehot, c_ones=ones, c_ident=np.eye(P, dtype=f), c_newmask=newmask, c_coef=coef,
                c_rope=rope, c_perm=perm, c_dec=dec, c_dec0=dec0, c_gq=gq, c_gk=gk, c_seq=seq,
                c_reset=reset, c_lvl=lvl, c_lvl0=lvl0)


def tiles_of(w, c0=0, n=None):
    n = w.shape[1] if n is None else n
    w = w[:, c0:c0 + n]
    return w.reshape(w.shape[0] // P, P, n // P, P).transpose(2, 1, 0, 3)


def down_units(w):
    t = tiles_of(w)
    out = np.zeros((KD, 3, P, 8, P), w.dtype)
    for u, k in enumerate(DOWN_BLOCKS):
        out[:, u, :, 0:k, :] = t[:, :, 8 * u:8 * u + k, :]
    return out.reshape(KD * 3, P, 8, P)


def per_tile(v):
    return v.reshape(-1, P).T


def layouts(a):
    f = np.float32
    out = {}
    h = np.concatenate([a["x_sample"].reshape(TS, D), a["meta_tokens"], a["x_prompt"].reshape(SEQ, D)], axis=0)
    out["h_in"] = h.T.reshape(KD, P, T).transpose(1, 0, 2)
    units = []
    low = np.zeros((DEPTH, P, 8, P), f)
    prm = np.zeros((DEPTH + 1, P, NP_), f)
    vb = np.zeros((DEPTH, 768), f)
    for l in range(DEPTH):
        w_in = a["w_in"][l]
        for f_ in (1, 2):
            pair_ = np.stack([tiles_of(a[f"ffn{f_}_gate"][l]), tiles_of(a[f"ffn{f_}_up"][l])], axis=1)
            ffn = [pair_.reshape(2 * KF, P, 8, P), down_units(a[f"ffn{f_}_down"][l])]
            if f_ == 1:
                units += ffn
                units += [tiles_of(w_in, c, 256) for c in V_COLS]
                units += [tiles_of(w_in, c, P) for c in Z_COLS]
                branch = a["w_branch"][l].reshape(8, P, KD, P).transpose(2, 1, 0, 3)
                gate = tiles_of(w_in, GATE_COL, 4 * D).reshape(4, KD, P, 8, P)
                units.append(np.concatenate([gate, branch[None]], axis=0).transpose(1, 0, 2, 3, 4).reshape(40, P, 8, P))
                units.append(tiles_of(a["w_out"][l]))
            else:
                units += ffn
        low[l, :, :, 0:16] = w_in[:, LOW_COL:LOW_COL + 16].reshape(8, P, 16).transpose(1, 0, 2)
        b = a["b_in"][l]
        vb[l] = np.concatenate([b[c:c + 256] for c in V_COLS])
        p = prm[l]
        for i, name in enumerate(("norm_ffn1", "norm_mix", "norm_ffn2")):
            p[:, P_GAIN + 8 * i:P_GAIN + 8 * i + 8] = per_tile(a[name][l])
        for i, c in enumerate(Z_COLS):
            p[:, P_ZB + i] = b[c:c + P]
        p[0:16, P_ZB + NZ] = b[LOW_COL:LOW_COL + 16]
        p[:, P_GB:P_GB + 32] = per_tile(b[GATE_COL:])
        for j in range(2):
            p[:, P_CW + CK * j:P_CW + CK * j + CK] = a["conv_w"][l][:, P * j:P * j + P].T
        for c, name in ((P_CB, "conv_b"), (P_LG, "conv_ln_g"), (P_LB, "conv_ln_b"), (P_RGN, "ret_gn"), (P_GGN, "gla_gn")):
            p[:, c:c + 2] = per_tile(a[name][l].reshape(-1))
        p[:, P_AB] = a["gla_alpha_b"][l]
        p[:, P_SUB] = np.tile(a["diff_subln"][l], 2)
        p[:, P_QN] = np.tile(a["q_norm"][l], 4)
        p[:, P_KN] = np.tile(a["k_norm"][l], 4)
        lam_init = 0.8 - 0.6 * math.exp(-0.3 * l)
        p[:, P_LI] = lam_init
        p[:, P_LI1] = 1.0 - lam_init
        for i, name in enumerate(("lam_q1", "lam_q2", "lam_k1", "lam_k2")):
            p[0:32, P_LAM + i] = a[name][l]
        p[0:16, P_AW:P_AW + P] = a["gla_alpha_w"][l]
    units.append(np.zeros((RING, P, 8, P), f))
    out["wstream"] = np.concatenate(units, axis=0).reshape(DEPTH * UNITS + RING, P, 8 * P)
    out["wlow"] = low.reshape(DEPTH, P, 8 * P)
    out["params"] = prm
    out["vbias"] = vb
    out["cache_k"] = a["cache_k"].reshape(DEPTH * POOL, PAGE, 2, P).transpose(0, 3, 2, 1).reshape(DEPTH * POOL, P, 2 * PAGE)
    out["cache_v"] = a["cache_v"].reshape(DEPTH * POOL, PAGE, 256)
    out["page_table"] = a["page_table"].reshape(1, NB * PAGES)
    sr = np.zeros((DEPTH, P, 2, NB, P), f)
    sg = np.zeros((DEPTH, P, NB, 256), f)
    for h in range(H):
        j, r = h // 2, 64 * (h % 2)
        sr[:, r:r + 64, j, :, r:r + 64] = a["state_ret"][:, :, h].transpose(0, 2, 1, 3)
        sg[:, 32 * h:32 * h + 32, :, 64 * h:64 * h + 64] = a["state_gla"][:, :, h].transpose(0, 2, 1, 3)
    out["st_ret"], out["st_gla"] = sr, sg
    out["st_conv"] = a["state_conv"].reshape(DEPTH, NB, CK - 1, 2, P).transpose(0, 4, 3, 1, 2)
    out["rel_bias"] = np.tile(np.repeat(np.concatenate([a["rel_bias"], np.full((1, H), NEG, f)], axis=0), 2, axis=1), (1, 2))
    return out


_ORDER = ["h_in", "wstream", "wlow", "params", "vbias", "cache_k", "cache_v", "page_table", "st_ret", "st_gla",
          "st_conv", "rel_bias", "c_bucket", "c_ones", "c_ident", "c_newmask", "c_coef", "c_rope", "c_perm",
          "c_dec", "c_dec0", "c_gq", "c_gk", "c_seq", "c_reset", "c_lvl", "c_lvl0"]
_OUTS = [("y_out", (P, KD, T)), ("k_out", (DEPTH, P, 2, T)), ("v_out", (DEPTH, P, WINDOWS, 256)),
         ("ret_out", (DEPTH, P, 2, P)), ("rets_out", (DEPTH, P, 2, NB, P)), ("gla_out", (DEPTH, P, 256)),
         ("glas_out", (DEPTH, P, NB, 256)), ("conv_out", (DEPTH, P, 2, CK - 1)), ("convs_out", (DEPTH, P, 2, NB, CK - 1))]


def kernel(**inputs):
    import concourse.bacc as _bacc
    from concourse.bass_utils import run_bass_kernel_spmd as _run

    nc = _bacc.Bacc("TRN2", target_bir_lowering=False, num_devices=1, dynamic_dma_scratch_size=2048)
    arrays = layouts({k: np.asarray(v) for k, v in inputs.items()})
    arrays.update(constants())
    arrays = {k: np.ascontiguousarray(v) for k, v in arrays.items()}
    args = [nc.dram_tensor(k, arrays[k].shape, mybir.dt.from_np(arrays[k].dtype), kind="ExternalInput").ap() for k in _ORDER]
    args += [nc.dram_tensor(k, shape, F32, kind="ExternalOutput").ap() for k, shape in _OUTS]
    build(nc, *args)
    r = _run(nc, [arrays], core_ids=[0]).results[0]

    y = r["y_out"].transpose(2, 1, 0).reshape(T, D)
    k = r["k_out"].transpose(0, 3, 2, 1).reshape(DEPTH, T, H, 64)
    v = r["v_out"]
    v_prompt = np.concatenate([v[:, TS:TS + META, 0], v[:, :, 1:].transpose(0, 2, 1, 3).reshape(DEPTH, SEQ, 256)], axis=1)
    ret_p = np.stack([r["ret_out"][:, 64 * (h % 2):64 * (h % 2) + 64, h // 2, 64 * (h % 2):64 * (h % 2) + 64] for h in range(H)], axis=1)
    ret_s = np.stack([r["rets_out"][:, 64 * (h % 2):64 * (h % 2) + 64, h // 2, :, 64 * (h % 2):64 * (h % 2) + 64].transpose(0, 2, 1, 3)
                      for h in range(H)], axis=2)
    gla_p = np.stack([r["gla_out"][:, 32 * h:32 * h + 32, 64 * h:64 * h + 64] for h in range(H)], axis=1)
    gla_s = np.stack([r["glas_out"][:, 32 * h:32 * h + 32, :, 64 * h:64 * h + 64].transpose(0, 2, 1, 3) for h in range(H)], axis=2)
    return (y[TS + META:].reshape(1, SEQ, D), y[:TS].reshape(NB, NT, D),
            k[:, TS:].reshape(DEPTH, 1, LP, H, 64), v_prompt.reshape(DEPTH, 1, LP, H, 64),
            k[:, :TS].reshape(DEPTH, NB, NT, H, 64), v[:, :TS, 0].reshape(DEPTH, NB, NT, H, 64),
            ret_p[:, None], ret_s, gla_p[:, None], gla_s,
            r["conv_out"].transpose(0, 3, 2, 1).reshape(DEPTH, 1, CK - 1, 256),
            r["convs_out"].transpose(0, 3, 4, 2, 1).reshape(DEPTH, NB, CK - 1, 256))
```

```python
from contextlib import ExitStack
import math

import numpy as np

import concourse.bass as bass
from concourse import mybir

F32 = mybir.dt.float32
F32R = mybir.dt.float32r
U32 = mybir.dt.uint32
I32 = mybir.dt.int32
ALU = mybir.AluOpType
ACT = mybir.ActivationFunctionType
AX_X = mybir.AxisListType.X
ds = bass.ds

P = 128
D, FF, DEPTH = 1024, 2816, 2
KD, KF = D // P, FF // P
NB, NT = 8, 8
META, SEQ = 16, 512
TS = NB * NT
T = TS + META + SEQ
HALF = T // 2
LP = META + SEQ
PAST, PAGE = 1024, 128
PAGES = PAST // PAGE
POOL = NB * PAGES * 5 // 4
H = 4
CK = 31
EPS = 1e-6
ATT_SCALE = 32 ** -0.5
NEG = -1e30
RING = 4
WINDOWS = 5

U_FFN1, U_DOWN1 = 0, 2 * KF
U_MIX = U_DOWN1 + 24
U_GATES = U_MIX + 24
U_OUT = U_GATES + 40
U_FFN2 = U_OUT + 8
U_DOWN2 = U_FFN2 + 2 * KF
UNITS = U_DOWN2 + 24
QUADS = UNITS // RING
DOWN_BLOCKS = (8, 8, KF - 16)

V_COLS = (1024, 1792, 2832)
Z_COLS = (2320, 2448, 2576, 2704, 512, 640, 768, 896, 1536, 1664, 1280, 1408, 2048, 2176,
          256, 384, 0, 128)
DQ, DK, RQ, RK, GQ, GK, RG, GR, CG, CA = 0, 2, 4, 6, 8, 9, 10, 12, 14, 16
NZ = len(Z_COLS)
Z_ORDER = (DQ, DQ + 1, DK, DK + 1, CG, CG + 1, CA, CA + 1, RQ, RQ + 1, RK, RK + 1, GQ, GK, RG, RG + 1, GR, GR + 1)
Z_FIRST, Z_BEFORE = 4, 6
LOW_COL, GATE_COL = 2304, 3088

P_GAIN = 0
P_ZB = P_GAIN + 24
P_GB = P_ZB + NZ + 1
P_CW = P_GB + 32
P_CB, P_LG, P_LB = P_CW + 2 * CK, P_CW + 2 * CK + 2, P_CW + 2 * CK + 4
P_RGN, P_GGN = P_LB + 2, P_LB + 4
P_AB, P_SUB, P_QN, P_KN = P_GGN + 2, P_GGN + 3, P_GGN + 4, P_GGN + 5
P_LI, P_LI1 = P_KN + 1, P_KN + 2
P_LAM = P_KN + 3
P_AW = P_LAM + 4
NP_ = P_AW + P

CONSTS = 6
REL = PAST + NT
RL = REL + 127
SKEW = P - 1 + LP
GAMMA = [1.0 - 2.0 ** (-5 - h) for h in range(H)]
LEVELS = (128, 64, 32, 16, 8, 4, 2)


def window(w):
    return (0, TS + META) if w == 0 else (TS + META + P * (w - 1), P)


level_items = [(n, w) for n in range(len(LEVELS) + 1) for w in range(WINDOWS)
               if w or n == 0 or LEVELS[n - 1] <= META]


def items_through(n):
    return sum(m <= n for m, _ in level_items)


def level_start(b):
    return 0 if b <= NT else TS if b <= META else TS + META


def split_cols(ap):
    return ap.rearrange("p (h t) -> p h t", h=2)


def build(nc, h_in, wstream, wlow, params, vbias, cache_k, cache_v, page_table, st_ret, st_gla,
          st_conv, rel_bias, c_bucket, c_ones, c_ident, c_newmask, c_coef, c_rope, c_perm, c_dec, c_dec0,
          c_gq, c_gk, c_seq, c_reset, c_lvl, c_lvl0,
          y_out, k_out, v_out, ret_out, rets_out, gla_out, glas_out, conv_out, convs_out):
    scratch = nc.dram_tensor("bias_rows", (16, RL), F32).ap()
    skewed = nc.dram_tensor("bias_skewed", (P * (H * SKEW + 1),), F32).ap()

    with ExitStack() as ctx:
        def sem(name):
            return ctx.enter_context(nc.semaphore(name))

        at = -(-nc.sbuf_base // 32) * 32

        def place(name, shape, dt, offset):
            return nc.alloc_sbuf_tensor_at(name, shape, dt, offset=offset)

        def keep(name, shape, dt=F32):
            nonlocal at
            t = place(name, shape, dt, at)
            at += -(-4 * int(np.prod(shape[1:])) // 32) * 32
            return t

        hT = keep("hT", [P, KD, T])
        x_hi = keep("x_hi", [P, KD, T], F32R)
        x_lo = keep("x_lo", [P, KD, T], F32R)
        w_raw = keep("w_raw", [P, RING, 8, P])
        w_hi = keep("w_hi", [P, RING, 8, P], F32R)
        w_lo = keep("w_lo", [P, RING, 8, P], F32R)
        arena = at
        hid_hi = keep("hid_hi", [P, KF, T], F32R)
        hid_lo = keep("hid_lo", [P, KF, T], F32R)
        tmp = keep("tmp", [P, 2, T])
        gu = keep("gu", [P, 2, T])
        arena_end = at
        fresh = (gu[:, 0, :], gu[:, 1, :], tmp[:, 1, :])
        sum_room = at
        ssum = keep("ssum", [P, 2 * NB * (CK - 1 + NT)])[:, 0:T]
        prm = keep("prm", [P, NP_ - P])
        ones = keep("ones", [P, 3, P])
        ident = keep("ident", [P, P])
        coef = keep("coef", [P, 8])
        hb = keep("hb", [P, 32])
        small = keep("small", [P, 2, 6])
        pages = keep("pages", [1, NB * PAGES], I32)
        assert at <= nc.sbuf_usable_end, at

        TB = 4 * T
        Z = place("Z", [P, NZ, T], F32, arena)
        V = place("V", [P, WINDOWS, 768], F32, arena + NZ * TB)
        od = place("od", [P, 2, T], F32, arena + NZ * TB + 15360)
        work = arena + NZ * TB + 15360 + 2 * TB
        GL = V[96:112, 0, 0:T]

        def area(name, shape, offset, dt=F32):
            size = 4 * int(np.prod(shape[1:]))
            assert offset % 32 == 0 and work + offset + size <= arena_end, (name, offset, size)
            return place(name, shape, dt, work + offset)

        kpage = area("kpage", [P, 2, PAGES, 2 * P], 0)
        vpage = area("vpage", [P, 2, PAGES, 256], 16384)
        low_raw = area("low_raw", [P, 8, P], 32768)
        low_hi = area("low_hi", [P, 8, P], 36864, F32R)
        low_lo = area("low_lo", [P, 8, P], 40960, F32R)
        vb = area("vb", [P, 768], 45056)
        s_bias = area("s_bias", [P, PAST + NT], 32768)
        new_bias = area("new_bias", [P, 4, TS], 36896)
        new_mask = area("new_mask", [P, 4, TS], 37920)
        qbd = area("qbd", [P, 2, NB, 32], 38944)
        n_room = area("n_room", [P, 4, T], 40992)
        s_prob = area("s_prob", [P, PAST + TS], 40992)
        s_turn = area("s_turn", [P, 9, P], 45344)
        s_out = s_turn[:, 0:2, :]
        s_half = area("s_half", [P, 2, 2 * NT], 49952)
        p_bias = area("p_bias", [P, H, LP], 0)
        p_prob = area("p_prob", [P, 2, 2, LP], 8448)
        p_turn = area("p_turn", [P, 2, 512], 16896)
        p_meta = area("p_meta", [P, 2, P], 20992)
        rope = area("rope", [P, 2, T], 22016)
        perm = area("perm", [P, P], 26752)
        dec = area("dec", [P, H, P], 27264)
        dec0 = area("dec0", [P, H, 80], 29312)
        gq = area("gq", [P, 2, 208], 30592)
        gk = area("gk", [P, 2, 208], 32256)
        seqs = area("seqs", [P, NB], 33920)
        ss = area("ss", [P, 2, NB, P], 33984)
        vm = area("vm", [P, 2, NB, P], 42176)
        rqh = area("rqh", [P, 2, T], 0)
        rkh = area("rkh", [P, 2, T], 4736)
        rtmp = area("rtmp", [P, 2, 2, T], 9472)
        rkt = area("rkt", [P, WINDOWS, 2, P], 9472)
        rsc = area("rsc", [P, 2, 512], 14592)
        rst = area("rst", [P, 2, P], 18688)
        g_e = area("g_e", [P, 2, T], 0)
        g_qh = area("g_qh", [P, T], 4736)
        g_kh = area("g_kh", [P, T], 7104)
        g_kt = area("g_kt", [P, WINDOWS, P], 9472)
        g_sc = area("g_sc", [P, WINDOWS, 512], 12032)
        g_vm = area("g_vm", [P, NB, 256], 22272)
        g_st = area("g_st", [P, 256], 30464)
        lvl = area("lvl", [P, 8, P], 22016)
        lvl0 = area("lvl0", [P, 5, 80], 31520)
        g_ss = area("g_ss", [P, NB, 256], 39552)
        aw = area("aw", [P, P], 50368)
        g_seqs = area("g_seqs", [P, NB], 31488)
        g_ql = Z[:, 0:2, :]
        g_kl = Z[:, 2:4, :]
        g_b = Z[:, CA + 1, :]
        g_eb = Z[:, CA, :]
        reset = Z[:, DQ, :]
        g_rest = Z[:, DQ + 1, :]
        ue_s = place("ue_s", [P, 2, NB, CK - 1 + NT], F32, sum_room)
        ue_p = Z[:, CA:CA + 2, 0:CK - 1 + LP]
        glu = Z[:, GR:GR + 2, :]
        hn_root = area("hn_root", [P, 4, T], 0)
        hn_sq = area("hn_sq", [P, 4, T], 12032)
        TG = 0
        branch_tiles = [Z[:, CG, :], Z[:, CG + 1, :], Z[:, RQ, :], Z[:, RQ + 1, :],
                        Z[:, GQ, :], Z[:, GQ + 1, :], od[:, 0, :], od[:, 1, :]]
        rb = place("rb", [33, 16], F32, arena)
        bucket = place("bucket", [33, RL], F32, arena + 64)
        brow = place("brow", [16, RL], F32, arena + 4736)
        br_hi = area("br_hi", [P, 8, T], 12032, F32R)
        br_lo = area("br_lo", [P, 8, T], 30976, F32R)
        m_hi = place("m_hi", [P, KD, T], F32R, arena)
        m_lo = place("m_lo", [P, KD, T], F32R, arena + KD * TB)
        d_sg = place("d_sg", [P, 4, T], F32, arena + 2 * KD * TB)
        d_acc = place("d_acc", [P, 2, T], F32, arena + (2 * KD + 4) * TB)
        assert (2 * KD + 6) * TB <= NZ * TB + 15360

        ps = ctx.enter_context(nc.psum_tensor("ps", [P, 8, 512], F32))

        def pair(p):
            return ps[:, 2 * p:2 * p + 2, 0:HALF]

        h_loaded = [sem(f"h_loaded_{i}") for i in range(4)]
        consts_loaded = sem("consts_loaded")
        bias_row_made = sem("bias_row_made")
        bias_row_stored = sem("bias_row_stored")
        params_loaded = sem("params_loaded")
        weights_loaded = [sem(f"weights_loaded_{s}") for s in range(RING)]
        weights_high = sem("weights_high")
        weights_low = sem("weights_low")
        units_multiplied = sem("units_multiplied")
        sum_cleared = sem("sum_cleared")
        squared = sem("squared")
        squares_summed = sem("squares_summed")
        square_total = sem("square_total")
        log_ready = sem("log_ready")
        inverse_ready = sem("inverse_ready")
        normed = sem("normed")
        x_high = sem("x_high")
        x_ready = sem("x_ready")
        gate_scaled = sem("gate_scaled")
        tanh_ready = sem("tanh_ready")
        gated = sem("gated")
        hidden_made = sem("hidden_made")
        hidden_high = sem("hidden_high")
        hidden_ready = sem("hidden_ready")
        residual_added = sem("residual_added")
        merged_ready = sem("merged_ready")
        phases_entered = sem("phases_entered")
        mixers_left = sem("mixers_left")
        mixers_open = sem("mixers_open")
        y_stored = sem("y_stored")

        cleared = []

        def msem(name):
            cleared.append(sem(name))
            return cleared[-1]

        v_products, v_ready, z_ready = msem("v_products"), msem("v_ready"), msem("z_ready")
        low_loaded, low_high, low_split, low_product = (msem(n) for n in ("low_loaded", "low_high", "low_split", "low_product"))
        vector_chain, scalar_chain = msem("vector_chain"), msem("scalar_chain")
        vb_loaded, attn_tables_loaded, lam_ready = msem("vb_loaded"), msem("attn_tables_loaded"), msem("lam_ready")
        lam_products, lam_sums, lam_exps = msem("lam_products"), msem("lam_sums"), msem("lam_exps")
        keys_loaded = [msem(f"keys_loaded_{i}") for i in range(2)]
        values_loaded = [msem(f"values_loaded_{i}") for i in range(2)]
        qk_squared, qk_summed, qk_root, qk_normed = (msem(n) for n in ("qk_squared", "qk_summed", "qk_root", "qk_normed"))
        queries_placed = msem("queries_placed")
        sample_scores, sample_max, sample_exp, sample_scaled, sample_turned, sample_pt, sample_pv, sample_copied, sample_placed = (
            msem("sample_" + n) for n in ("scores", "max", "exp", "scaled", "turned", "pt", "pv", "copied", "placed"))
        sample_back = msem("sample_back")
        prompt_bias_loaded = msem("prompt_bias_loaded")
        prompt_scores, prompt_max, prompt_exp, prompt_attn, prompt_turned, prompt_pt, prompt_pv, prompt_evac = (
            msem("prompt_" + n) for n in ("scores", "max", "exp", "attn", "turned", "pt", "pv", "evac"))
        ret_tables_loaded = msem("ret_tables_loaded")
        rope_swapped, rope_turned, ret_scaled, ret_blocks, ret_keys, ret_scores, ret_decayed, ret_mixed, ret_evac, ret_update, ret_state = (
            msem(n) for n in ("rope_swapped", "rope_turned", "ret_scaled", "ret_blocks", "ret_keys", "ret_scores",
                              "ret_decayed", "ret_mixed", "ret_evac", "ret_update", "ret_state"))
        ret_spread, ret_s_update, ret_s_state = msem("ret_spread"), msem("ret_s_update"), msem("ret_s_state")
        decay_tables_loaded, gla_tables_loaded = msem("decay_tables_loaded"), msem("gla_tables_loaded")
        alpha_taken, masks_loaded = msem("alpha_taken"), msem("level_masks_loaded")
        alpha_product, alpha_log, gla_summed, gla_exp_b, gla_diff, gla_exp_last, gla_scaled, gla_blocks, gla_keys = (
            msem(n) for n in ("alpha_product", "alpha_log", "gla_summed", "gla_exp_b", "gla_diff", "gla_exp_last",
                              "gla_scaled", "gla_blocks", "gla_keys"))
        lvl_diff, lvl_exp, lvl_ready, lvl_scores, lvl_taken = (msem("level_" + n) for n in ("diff", "exp", "ready", "scores", "taken"))
        gla_mixed, gla_evac, gla_update, gla_state, gla_spread, gla_s_update, gla_s_state = (
            msem("gla_" + n) for n in ("mixed", "evac", "update", "state", "spread", "s_update", "s_state"))
        conv_loaded, conv_tanh, conv_gated, conv_rows, conv_done = (msem("conv_" + n) for n in ("loaded", "tanh", "gated", "rows", "done"))
        hn_summed, hn_centered, hn_squared, hn_totalled, hn_root_ready, hn_normed = (
            msem("head_norm_" + n) for n in ("mean", "centered", "squared", "totalled", "root", "normed"))
        qk_log = msem("qk_log")
        conv_steps, silu_ready = msem("conv_steps"), msem("silu_ready")
        hn_log_ready = msem("head_norm_log")
        act_tanh, br_ready, br_high, br_split = msem("branch_tanh"), msem("branch_ready"), msem("branch_high"), msem("branch_split")
        mixers_stored = msem("mixers_stored")
        gate_tanh, branch_products, branch_taken, merged_steps, merged_high = (
            msem(n) for n in ("gate_tanh", "branch_products", "branch_taken", "merged_steps", "merged_high"))
        nums = [s.num for s in cleared]
        assert nums == list(range(nums[0], nums[0] + len(nums)))

        od_tiles, gla_tiles, ret_tiles, conv_tiles = ([(branch_tiles[n + i], c + i) for i in range(2)]
                                                      for n, c in ((6, 0), (4, P_GGN), (2, P_RGN), (0, P_LG)))
        QK_BANKS = (1, 2, 0, 1)
        HEAD_NORMS = ((3, 64, od_tiles[0:1]), (0, 64, od_tiles[1:2]), (1, 64, gla_tiles[0:1]), (2, 64, gla_tiles[1:2]),
                      (3, 64, ret_tiles[0:1]), (0, 64, ret_tiles[1:2]), (1, 256, conv_tiles))
        FINISHED = (6, 7, 4, 5, 2, 3, 0, 1)
        MIXER_STORES = 10
        POOL_LOADS = ((vb_loaded, 1), (low_loaded, 1), (attn_tables_loaded, 9), (prompt_bias_loaded, 1),
                      (ret_tables_loaded, 8), (decay_tables_loaded, 2), (masks_loaded, 2), (gla_tables_loaded, 2), (conv_loaded, 2))

        block = ctx.enter_context(nc.Block())

        @block.sync
        def _(sp):
            def load_unit(quad, slot):
                sp.wait_ge(weights_low, 4 * quad + slot + 1)
                sp.dma_start(w_raw[:, slot, :, :], wstream[ds(4 * quad + slot, 1)].rearrange("a p (k m) -> (a p) k m", k=8)
                             ).then_inc(weights_loaded[slot], 16)

            def load_quads(l, first, count):
                with sp.Fori(0, count) as i:
                    for s in range(RING):
                        load_unit(l * QUADS + first + i, s)

            def load_pages(l, b, cache, room, loaded):
                for pg in range(PAGES):
                    page = sp.value_load(pages[0:1, b * PAGES + pg:b * PAGES + pg + 1], min_val=0, max_val=POOL - 1)
                    sp.dma_start(room[:, b % 2, pg, :], cache[ds(l * POOL + page, 1)].rearrange("a p n -> (a p) n")).then_inc(loaded[b % 2], 16)

            for s in range(RING):
                sp.dma_start(hT[:, 2 * s:2 * s + 2, :], h_in[:, 2 * s:2 * s + 2, :]).then_inc(h_loaded[s], 16)
                sp.dma_start(w_raw[:, s, :, :], wstream[s].rearrange("p (k m) -> p k m", k=8)).then_inc(weights_loaded[s], 16)
            sp.wait_ge(consts_loaded, 16 * CONSTS)
            with sp.Fori(0, DEPTH) as l:
                load_quads(l, 1, U_MIX // RING)
                sp.wait_ge(mixers_open, l + 1)
                sp.sem_inc(phases_entered, 1)
                sp.wait_ge(x_ready, l * 24 + 16)
                sp.sem_inc(phases_entered, 1)
                def load_mix(i, slots=range(RING)):
                    for s in slots:
                        load_unit(l * QUADS + 1 + U_MIX // RING + i, s)

                def load_pair(p, cache, room, loaded):
                    for b in (2 * p, 2 * p + 1):
                        load_pages(l, b, cache, room, loaded)

                load_mix(0)
                load_pages(l, 0, cache_k, kpage, keys_loaded)
                load_mix(1)
                load_pages(l, 1, cache_k, kpage, keys_loaded)
                load_mix(2)
                load_pages(l, 0, cache_v, vpage, values_loaded)
                load_mix(3)
                load_pages(l, 1, cache_v, vpage, values_loaded)
                between = {1: ((), ((4, 0), (4, 1), (4, 2))), 2: (((4, 3),), ((5, 0), (5, 1))), 3: (((5, 2),), ((5, 3),))}
                for p in range(1, 4):
                    before, after = between[p]
                    for i, slot in before:
                        load_mix(i, (slot,))
                    sp.wait_ge(sample_scores, p)
                    load_pair(p, cache_k, kpage, keys_loaded)
                    for i, slot in after:
                        load_mix(i, (slot,))
                    sp.wait_ge(sample_pv, p)
                    load_pair(p, cache_v, vpage, values_loaded)
                sp.wait_ge(sample_pv, 4)
                sp.sem_inc(mixers_left, 1)
                load_quads(l, 1 + U_GATES // RING, (UNITS - U_GATES) // RING)
            sp.wait_ge(residual_added, 4 + 24 * DEPTH)
            sp.dma_start(y_out, hT[:, :, :]).then_inc(y_stored, 16)
            sp.wait_ge(y_stored, 16)
            for s in range(RING):
                sp.wait_ge(weights_loaded[s], 16 * (DEPTH * QUADS + 1))

        @block.gpsimd
        def _(pl):
            pl.dma_start(prm[:, :], params[0][:, 0:NP_ - P]).then_inc(params_loaded, 16)
            pl.dma_start(pages[:, :], page_table).then_inc(consts_loaded, 16)
            pl.dma_start(ones[:, :, :], c_ones).then_inc(consts_loaded, 16)
            pl.dma_start(ident[:, :], c_ident).then_inc(consts_loaded, 16)
            pl.dma_start(coef[:, 0:2], c_coef).then_inc(consts_loaded, 16)
            pl.dma_start(rb[0:33, :], rel_bias).then_inc(consts_loaded, 16)
            pl.dma_start(bucket[0:33, :], c_bucket).then_inc(consts_loaded, 16)
            pl.wait_ge(bias_row_made, 3)
            pl.dma_start(scratch, brow[:, :]).then_inc(bias_row_stored, 16)
            pl.wait_ge(bias_row_stored, 16)
            pl.dma_start(bass.AP(tensor=skewed.tensor, offset=skewed.offset, ap=[[H * SKEW + 1, P], [SKEW, H], [1, SKEW]]),
                         bass.AP(tensor=scratch.tensor, offset=scratch.offset + RL - SKEW, ap=[[0, P], [2 * RL, H], [1, SKEW]])
                         ).then_inc(bias_row_stored, 16)
            pl.wait_ge(bias_row_stored, 32)
            pl.sem_inc(mixers_open, 1)
            with pl.Fori(0, DEPTH) as l:
                pl.wait_ge(mixers_open, l + 1)
                pl.sem_inc(phases_entered, 1)
                pl.wait_ge(x_ready, l * 24 + 16)
                pl.sem_inc(phases_entered, 1)
                pl.dma_start(vb[:, :], vbias[ds(l, 1)].to_broadcast([P, 768])).then_inc(vb_loaded, 16)
                pl.dma_start(low_raw[:, :, :], wlow[ds(l, 1)].rearrange("a p (k m) -> (a p) k m", k=8)).then_inc(low_loaded, 16)
                for j in range(2):
                    pl.dma_start(ue_s[:, j, :, 0:CK - 1],
                                 st_conv[ds(l, 1), :, j:j + 1].rearrange("a p j b r -> (a p) (j b) r")).then_inc(conv_loaded, 16)
                pl.wait_ge(z_ready, Z_FIRST + 1)
                pl.wait_ge(v_ready, 15)
                for t in range(NT):
                    src = bass.AP(tensor=scratch.tensor, offset=scratch.offset + NT - 1 - t,
                                  ap=[[RL, 16], [1, PAST + NT]])
                    pl.dma_start(s_bias[t:P - NT + t + 1:NT, :], src).then_inc(attn_tables_loaded, 16)
                pl.dma_start(new_mask[:, :, :], c_newmask).then_inc(attn_tables_loaded, 16)
                pl.wait_ge(qk_normed, 4)
                pl.dma_start(k_out[ds(l, 1)].rearrange("a p j t -> (a p) j t"), Z[:, DK:DK + 2, :]).then_inc(mixers_stored, 16)
                pl.dma_start(v_out[ds(l, 1), 0:80, 0:1].rearrange("a p w n -> (a p) (w n)"), V[0:80, 0, 512:768]).then_inc(mixers_stored, 16)
                pl.dma_start(v_out[ds(l, 1), :, 1:WINDOWS].rearrange("a p w n -> (a p) w n"), V[:, 1:WINDOWS, 512:768]).then_inc(mixers_stored, 16)
                pl.wait_ge(conv_rows, 4)
                pl.wait_ge(conv_gated, 3)
                pl.dma_start(conv_out[ds(l, 1)].rearrange("a p j r -> (a p) j r"), ue_p[:, :, LP:LP + CK - 1]).then_inc(mixers_stored, 16)
                for j in range(2):
                    pl.dma_start(convs_out[ds(l, 1), :, j:j + 1].rearrange("a p j b r -> (a p) (j b) r"),
                                 ue_s[:, j, :, NT:NT + CK - 1]).then_inc(mixers_stored, 16)
                pl.wait_ge(sample_scores, 4)
                src = bass.AP(tensor=skewed.tensor, offset=skewed.offset + P - 1, ap=[[H * SKEW, P], [SKEW, H], [1, LP]])
                pl.dma_start(p_bias[:, :, :], src).then_inc(prompt_bias_loaded, 16)
                pl.wait_ge(sample_placed, 4)
                pl.dma_start(rope[:, :, :], c_rope).then_inc(ret_tables_loaded, 16)
                pl.dma_start(perm[:, :], c_perm).then_inc(ret_tables_loaded, 16)
                pl.dma_start(dec[:, :, :], c_dec).then_inc(ret_tables_loaded, 16)
                pl.dma_start(dec0[0:80, :, :], c_dec0).then_inc(ret_tables_loaded, 16)
                pl.dma_start(gq[:, :, :], c_gq).then_inc(ret_tables_loaded, 16)
                pl.dma_start(gk[:, :, :], c_gk).then_inc(ret_tables_loaded, 16)
                pl.dma_start(seqs[0:TS, :], c_seq).then_inc(ret_tables_loaded, 16)
                pl.dma_start(ss[:, :, :, :], st_ret[ds(l, 1)].rearrange("a p j b n -> (a p) j b n")).then_inc(ret_tables_loaded, 16)
                pl.dma_start(aw[96:112, :], params[ds(l, 1), 0:16, P_AW:P_AW + P].rearrange("a p n -> (a p) n")).then_inc(decay_tables_loaded, 16)
                pl.wait_ge(prompt_scores, WINDOWS * H)
                pl.dma_start(reset, c_reset).then_inc(decay_tables_loaded, 16)
                pl.wait_ge(ret_scaled, 1)
                pl.dma_start(lvl[:, :, :], c_lvl).then_inc(masks_loaded, 16)
                pl.dma_start(lvl0[0:80, :, :], c_lvl0).then_inc(masks_loaded, 16)
                pl.wait_ge(ret_state, WINDOWS)
                pl.dma_start(ret_out[ds(l, 1)].rearrange("a p j n -> (a p) j n"), rst[:, :, :]).then_inc(mixers_stored, 16)
                pl.wait_ge(ret_s_state, 1)
                pl.dma_start(rets_out[ds(l, 1)].rearrange("a p j b n -> (a p) j b n"), ss[:, :, :, :]).then_inc(mixers_stored, 16)
                pl.wait_ge(mixers_stored, 16 * (MIXER_STORES - 2))
                pl.dma_start(g_ss[:, :, :], st_gla[ds(l, 1)].rearrange("a p b n -> (a p) b n")).then_inc(gla_tables_loaded, 16)
                pl.dma_start(g_seqs[0:TS, :], c_seq).then_inc(gla_tables_loaded, 16)
                pl.wait_ge(gla_state, WINDOWS)
                pl.dma_start(gla_out[ds(l, 1)].rearrange("a p n -> (a p) n"), g_st[:, :]).then_inc(mixers_stored, 16)
                pl.wait_ge(gla_s_state, 1)
                pl.dma_start(glas_out[ds(l, 1)].rearrange("a p b n -> (a p) b n"), g_ss[:, :, :]).then_inc(mixers_stored, 16)
                pl.wait_ge(mixers_stored, 16 * MIXER_STORES)
                for loaded, count in POOL_LOADS:
                    pl.wait_ge(loaded, 16 * count)
                pl.wait_ge(mixers_left, 4 * (l + 1))
                pl.sem_inc(phases_entered, 1)
                pl.dma_reset(range(nums[0], nums[-1] + 1))
                pl.sem_clear(range(nums[0], nums[-1] + 1))
                pl.sem_inc(mixers_open, 1)
                pl.wait_ge(x_ready, l * 24 + 24)
                pl.sem_inc(phases_entered, 1)
                pl.dma_start(prm[:, :], params[ds(l + 1, 1), :, 0:NP_ - P].rearrange("a p n -> (a p) n")).then_inc(params_loaded, 16)
            pl.wait_ge(params_loaded, 16 * (DEPTH + 1))

        @block.scalar
        def _(act):
            def split_high(quad, slot):
                act.wait_ge(weights_loaded[slot], 16 * quad + 16)
                act.wait_ge(units_multiplied, 4 * quad + slot + 1)
                act.activation(w_hi[:, slot, :, :], w_raw[:, slot, :, :], ACT.Copy).then_inc(weights_high, 1)

            def unit_done(quad, slot):
                act.wait_ge(units_multiplied, 4 * quad + slot + 1 + RING)

            def inverse_root(room, sums, width, done):
                link(act.activation(split_cols(room), sums, ACT.Ln, bias=EPS, scale=1.0 / width))
                act.activation(room, room, ACT.Exp, scale=-0.5).then_inc(done, 1)

            def norm(l, i):
                w = l * 3 + i
                act.wait_ge(square_total, w + 1)
                room = tmp[:, 0, :] if i == 1 else ssum
                act.activation(split_cols(room), pair(3), ACT.Ln, bias=EPS, scale=1.0 / D).then_inc(log_ready, 1)
                act.wait_ge(log_ready, w + 1)
                act.activation(room, room, ACT.Exp, scale=-0.5).then_inc(inverse_ready, 1)
                if i == 1:
                    for k in range(KD):
                        act.wait_ge(normed, 8 * l + k + 1)
                        act.activation(x_hi[:, k, :], fresh[k % 3], ACT.Copy).then_inc(x_high, 1)

            def gate_up(l, f, first):
                with act.Fori(0, KF // 2) as i:
                    for j in range(2):
                        q = l * 2 * KF + f * KF + i * 2 + j
                        quad = l * QUADS + first // RING + i
                        act.wait_ge(weights_loaded[2 * j], 16 * quad + 32)
                        act.wait_ge(gate_scaled, q + 1)
                        act.activation(w_hi[:, 2 * j, :, :], w_raw[:, 2 * j, :, :], ACT.Copy).then_inc(weights_high, 1)
                        act.activation(gu[:, j, :], tmp[:, j, :], ACT.Tanh, scale=0.5).then_inc(tanh_ready, 1)
                        act.wait_ge(hidden_made, q + 3)
                        split_high(quad + 1, 2 * j + 1)
                        act.activation(hid_hi[:, ds(i * 2 + j, 1), :], gu[:, j:j + 1, :], ACT.Copy).then_inc(hidden_high, 1)

            def square_and_split(tile, room, gain, out):
                act.activation(room, tile, ACT.Square).then_inc(squared, 1)
                if gain is not None:
                    act.activation(out, tile, ACT.Copy, scale=gain).then_inc(x_high, 1)

            def residual(l, r0, first, units, gain):
                with act.Fori(0, 2) as i:
                    for j in range(4):
                        r = l * 24 + r0 + i * 4 + j
                        for u in range(units):
                            pos = j * units + u
                            quad = l * QUADS + first // RING + i * units + pos // RING
                            if u == units - 1:
                                act.wait_ge(residual_added, r + 1 + 4)
                                act.wait_ge(squares_summed, r + 7)
                            split_high(quad + 1, pos % RING)
                        m = i * 4 + j
                        square_and_split(hT[:, ds(m, 1), :], tmp[:, j % 2:j % 2 + 1, :],
                                         None if gain is None else prm[:, ds(m + gain, 1)], x_hi[:, ds(m, 1), :])

            chain = [0]

            def link(ins):
                chain[0] += 1
                ins.then_inc(scalar_chain, 1)
                act.wait_ge(scalar_chain, chain[0])

            def tile(l, c):
                pos = c + 6
                quad, slot = l * QUADS + U_MIX // RING + pos // RING, pos % RING
                if c >= 0:
                    z = Z_ORDER[c]
                    unit_done(quad, slot)
                    act.activation(split_cols(Z[:, z, :]), pair(min(c, 3)), ACT.Identity, bias=prm[:, P_ZB + z:P_ZB + z + 1]).then_inc(z_ready, 1)
                split_high(quad + 1, slot)

            def project(l):
                act.wait_ge(mixers_open, l + 1)
                act.sem_inc(phases_entered, 1)
                act.wait_ge(low_loaded, 16)
                act.activation(low_hi[:, :, :], low_raw[:, :, :], ACT.Copy).then_inc(low_high, 1)
                for c in range(-6, Z_FIRST):
                    tile(l, c)
                act.wait_ge(low_product, 1)
                act.activation(split_cols(GL), ps[0:16, 0:2, 0:HALF], ACT.Identity, bias=prm[0:16, P_ZB + NZ:P_ZB + NZ + 1]).then_inc(z_ready, 1)

            def attention_sample(l):
                act.wait_ge(v_ready, 15)
                act.wait_ge(z_ready, Z_FIRST + 1)
                for t in range(4):
                    act.activation(n_room[:, t, :], Z[:, t, :], ACT.Square).then_inc(qk_squared, 1)
                for t in range(4):
                    act.wait_ge(qk_summed, t + 1)
                    act.activation(split_cols(n_room[:, t, :]), pair(QK_BANKS[t]), ACT.Ln, bias=EPS, scale=1.0 / 32).then_inc(qk_log, 1)
                for t in range(4):
                    act.wait_ge(qk_log, t + 1)
                    act.activation(n_room[:, t, :], n_room[:, t, :], ACT.Exp, scale=-0.5).then_inc(qk_root, 1)
                act.wait_ge(lam_sums, 1)
                act.activation(coef[:, 2:4], ps[:, 4, 0:2], ACT.Exp).then_inc(lam_exps, 1)
                for c in range(Z_FIRST, Z_BEFORE):
                    tile(l, c)
                for p in range(4):
                    tile(l, Z_BEFORE + 3 * p)
                    act.wait_ge(sample_max, p + 1)
                    act.activation(s_prob[:, :], s_prob[:, :], ACT.Exp, bias=coef[:, 6:7], accum_out=coef[:, 7:8]).then_inc(sample_exp, 1)
                    tile(l, Z_BEFORE + 3 * p + 1)
                    act.wait_ge(sample_turned, p + 1)
                    act.activation(s_turn[:, 0:8, :], ps[:, 3:5, :].rearrange("p b (s r) -> p (b s) r", s=4), ACT.Copy).then_inc(sample_pt, 1)
                    act.activation(s_turn[0:TS, 8, :], ps[0:TS, 5, 0:P], ACT.Copy).then_inc(sample_pt, 1)
                    tile(l, Z_BEFORE + 3 * p + 2)
                    act.wait_ge(sample_pv, p + 1)
                    act.activation(s_out, ps[:, 5, 0:256].rearrange("p (j v) -> p j v", j=2), ACT.Copy).then_inc(sample_copied, 1)
                    if p == 0:
                        act.wait_ge(z_ready, 9)
                        for j in range(2):
                            act.activation(Z[:, CG + j, :], Z[:, CG + j, :], ACT.Tanh, scale=0.5).then_inc(conv_tanh, 1)
                        for j in range(2):
                            act.wait_ge(conv_loaded, 32)
                            act.wait_ge(conv_gated, j + 1)
                            act.activation(ue_s[:, j, :, CK - 1:CK - 1 + NT], glu[:, j, 0:TS].rearrange("p (b t) -> p b t", b=NB),
                                           ACT.Copy, scale=0.5).then_inc(conv_rows, 1)
                            act.activation(ue_p[:, j, CK - 1:CK - 1 + LP], glu[:, j, TS:T], ACT.Copy, scale=0.5).then_inc(conv_rows, 1)

            def prompt_steps():
                return [(j, h) for j in range(WINDOWS) for h in range(H)]

            def attention_prompt():
                def exps(x):
                    n = META if x < H else P
                    ns = META + P * (x // H)
                    act.wait_ge(prompt_max, x + 1)
                    for i in range(2):
                        act.activation(p_prob[0:n, x % 2, i, 0:ns], p_prob[0:n, x % 2, i, 0:ns], ACT.Exp,
                                       bias=small[0:n, x % 2, i:i + 1], accum_out=small[0:n, x % 2, 2 + i:3 + i]).then_inc(prompt_exp, 1)

                act.wait_ge(z_ready, NZ + 1)
                steps = prompt_steps()
                def placed(x):
                    j, h = steps[x]
                    if h % 2:
                        c0, n = (TS, META) if j == 0 else window(j)
                        act.wait_ge(prompt_pv, x + 1)
                        act.activation(od[:, h // 2, c0:c0 + n], ps[:, 7, 0:n], ACT.Copy).then_inc(prompt_evac, 1)

                exps(0)
                for x, (j, h) in enumerate(steps):
                    n = META if j == 0 else P
                    act.wait_ge(prompt_turned, x + 1)
                    if x >= 2:
                        act.wait_ge(prompt_pv, x - 1)
                    if j:
                        link(act.activation(p_turn[:, x % 2, 0:j * P], ps[:, 4 + x % 2, 0:j * P], ACT.Copy))
                    act.activation(p_meta[64:64 + META, x % 2, 0:n], ps[0:META, 6, 0:n], ACT.Copy).then_inc(prompt_pt, 1)
                    if x + 1 < len(steps):
                        exps(x + 1)
                    if x:
                        placed(x - 1)
                placed(len(steps) - 1)

            def retention():
                act.wait_ge(conv_done, 1)
                act.wait_ge(mixers_stored, 16 * 6)
                act.wait_ge(alpha_product, 1)
                act.activation(split_cols(g_eb), pair(2), ACT.Identity, bias=prm[:, P_AB:P_AB + 1]).then_inc(alpha_taken, 1)
                act.wait_ge(alpha_taken, 1)
                link(act.activation(g_b, g_eb, ACT.Abs))
                link(act.activation(g_b, g_b, ACT.Exp, scale=-1.0))
                act.activation(g_b, g_b, ACT.Ln, bias=1.0).then_inc(alpha_log, 1)
                for w in range(WINDOWS):
                    n = window(w)[1]
                    act.wait_ge(ret_blocks, w + 1)
                    act.activation(rkt[0:n, w, :, :], ps[0:n, w % 2, 0:256].rearrange("p (j c) -> p j c", j=2), ACT.Copy).then_inc(ret_keys, 1)
                act.wait_ge(gla_summed, 1)
                act.activation(g_eb, g_b, ACT.Exp).then_inc(gla_exp_b, 1)
                act.wait_ge(gla_diff, 1)
                act.activation(g_rest, g_rest, ACT.Exp).then_inc(gla_exp_last, 1)
                for w in range(WINDOWS):
                    c0, n = window(w)
                    act.wait_ge(ret_mixed, w + 1)
                    act.activation(Z[:, RQ:RQ + 2, c0:c0 + n], ps[:, 4 + w % 2, 0:256].rearrange("p (j c) -> p j c", j=2)[:, :, 0:n],
                                   ACT.Copy).then_inc(ret_evac, 1)

            def gla():
                for w in range(WINDOWS):
                    n = window(w)[1]
                    act.wait_ge(gla_blocks, w + 1)
                    act.activation(g_kt[0:n, w, :], ps[0:n, 4 + w % 2, 0:P], ACT.Copy).then_inc(gla_keys, 1)
                for n, b in enumerate(LEVELS):
                    act.wait_ge(lvl_diff, n + 1)
                    c0 = level_start(b)
                    view = g_e[:, n % 2, c0:T].rearrange("p (n b) -> p n b", b=b)
                    act.activation(view[:, :, 0:b // 2], view[:, :, 0:b // 2], ACT.Exp, scale=-1.0).then_inc(lvl_exp, 1)
                    act.activation(view[:, :, b // 2:b], view[:, :, b // 2:b], ACT.Exp).then_inc(lvl_exp, 1)
                for w in range(WINDOWS):
                    c0, n = window(w)
                    act.wait_ge(gla_mixed, w + 1)
                    act.activation(Z[:, GQ:GQ + 2, c0:c0 + n], ps[:, 6 + w % 2, 0:256].rearrange("p (j c) -> p j c", j=2)[:, :, 0:n],
                                   ACT.Copy).then_inc(gla_evac, 1)

            def head_norms():
                act.wait_ge(lvl_scores, len(level_items))
                for n, c in enumerate((RG, RG + 1, GR, GR + 1)):
                    act.activation(Z[:, TG + n, :], Z[:, c, :], ACT.Tanh, scale=0.5).then_inc(act_tanh, 1)

                def square(i, tile):
                    act.activation(hn_sq[:, i % 4, :], tile, ACT.Square).then_inc(hn_squared, 1)

                def root(i):
                    banks, width, tiles = HEAD_NORMS[i]
                    act.wait_ge(hn_totalled, i + 1)
                    act.activation(split_cols(hn_root[:, i % 4, :]), pair(banks), ACT.Ln, bias=EPS, scale=1.0 / width).then_inc(hn_log_ready, 1)

                def inverse(i):
                    act.wait_ge(hn_log_ready, i + 1)
                    act.activation(hn_root[:, i % 4, :], hn_root[:, i % 4, :], ACT.Exp, scale=-0.5).then_inc(hn_root_ready, 1)

                act.wait_ge(prompt_evac, 10)
                act.wait_ge(gla_evac, WINDOWS)
                for i in range(4):
                    square(i, HEAD_NORMS[i][2][0][0])
                for i in range(4):
                    root(i)
                for i in range(4):
                    inverse(i)
                for i, tile in enumerate((2, 3, 0, 1)):
                    act.wait_ge(hn_centered, i + 1)
                    square(4 + i, branch_tiles[tile])
                for i in range(4, 7):
                    act.wait_ge(hn_normed, i - 3)
                    root(i)
                for i in range(4, 7):
                    inverse(i)

            def branches():
                act.wait_ge(mixers_stored, 16 * MIXER_STORES)
                for n, b in enumerate(FINISHED):
                    if n == 4:
                        act.wait_ge(conv_done, 2)
                        for i in range(2):
                            act.activation(hn_root[:, i, :], Z[:, CG + i, :], ACT.Tanh, scale=0.5).then_inc(act_tanh, 1)
                    act.wait_ge(hn_normed, 7)
                    act.wait_ge(br_ready, n + 1)
                    act.activation(br_hi[:, b, :], branch_tiles[b], ACT.Copy).then_inc(br_high, 1)

            def gates(l):
                with act.Fori(0, 2) as i:
                    for mm in range(4):
                        m = i * 4 + mm
                        for n in range(5):
                            pos = mm * 5 + n
                            quad, slot = l * QUADS + U_GATES // RING + i * 5 + pos // RING, pos % RING
                            if n < 4:
                                act.wait_ge(branch_taken, m * 4 + n + 1)
                                unit_done(quad, slot)
                                split_high(quad + 1, slot)
                                act.activation(split_cols(d_sg[:, n, :]), pair(n), ACT.Tanh, scale=0.5, bias=hb[:, ds(m + 8 * n, 1)]).then_inc(gate_tanh, 1)
                            else:
                                act.wait_ge(merged_steps, m * 3 + 3)
                                split_high(quad + 1, slot)
                                act.activation(m_hi[:, ds(m, 1), :], d_acc[:, 0:1, :], ACT.Copy, scale=0.5).then_inc(merged_high, 1)
                act.drain().then_inc(mixers_left, 1)

            act.wait_ge(params_loaded, 16)
            for m in range(KD):
                if m % 2 == 0:
                    act.wait_ge(h_loaded[m // 2], 16)
                if m >= 2:
                    act.wait_ge(squares_summed, m - 1)
                square_and_split(hT[:, m, :], tmp[:, m % 2, :], prm[:, P_GAIN + m:P_GAIN + m + 1], x_hi[:, m, :])
                if m % 2:
                    act.wait_ge(weights_loaded[m // 2], 16)
                    act.activation(w_hi[:, m // 2, :, :], w_raw[:, m // 2, :, :], ACT.Copy).then_inc(weights_high, 1)
            act.wait_ge(bias_row_stored, 16)
            with act.Fori(0, DEPTH) as l:
                norm(l, 0)
                gate_up(l, 0, U_FFN1)
                residual(l, 0, U_DOWN1, 3, None)
                norm(l, 1)
                project(l)
                attention_sample(l)
                attention_prompt()
                retention()
                gla()
                head_norms()
                branches()
                gates(l)
                residual(l, 8, U_OUT, 1, P_GAIN + 16)
                norm(l, 2)
                gate_up(l, 1, U_FFN2)
                act.wait_ge(params_loaded, 16 * (l + 2))
                act.sem_inc(phases_entered, 1)
                residual(l, 16, U_DOWN2, 3, P_GAIN)

        @block.tensor
        def _(pe):
            def products(p, slot, blocks, k0, xh, xl, start=True, stop=True, wh=None, wl=None):
                wh = w_hi[:, slot, :, :] if wh is None else wh
                wl = w_lo[:, slot, :, :] if wl is None else wl
                for k in range(blocks[0], blocks[1]):
                    for n, (wp, xp) in enumerate(((wh, xh), (wl, xh), (wh, xl))):
                        for half in range(2):
                            mm = pe.matmul(ps[:, 2 * p + half, 0:HALF], wp[:, k, :],
                                           xp[:, k0 + k - blocks[0], half * HALF:(half + 1) * HALF],
                                           start=start and k == blocks[0] and n == 0,
                                           stop=stop and k == blocks[1] - 1 and n == 2)
                return mm

            def unit_ready(quad, slot):
                pe.wait_ge(weights_low, 4 * quad + slot + 1 + RING)

            def sum_tile(p, mat, tile, start=True, stop=True):
                for half in range(2):
                    mm = pe.matmul(ps[:, 2 * p + half, 0:HALF], mat, tile[:, half * HALF:(half + 1) * HALF], start=start, stop=stop)
                return mm

            def norm(l, i):
                w = l * 3 + i
                pe.wait_ge(squares_summed, 8 * (w + 1))
                sum_tile(3, ones[:, 0, :], ssum).then_inc(square_total, 1)

            def gate_up(l, f, first):
                quad0 = l * QUADS + first // RING

                def unit(i, slot):
                    quad, q = quad0 + i, l * 2 * KF + f * KF + i * 2 + slot // 2
                    if slot % 2 == 0:
                        pe.wait_ge(hidden_made, q + 1)
                    unit_ready(quad, slot)
                    if slot == 3:
                        pe.wait_ge(log_ready, l * 3 + 2 * f + 1)
                    products(slot, slot, (0, 8), 0, x_hi, x_lo).then_inc(units_multiplied, 1)

                pe.wait_ge(hidden_made, l * 2 * KF + f * KF + 1)
                pe.wait_ge(x_ready, l * 24 + 16 * f + 7)
                unit_ready(quad0, 0)
                products(0, 0, (0, 7), 0, x_hi, x_lo, stop=False)
                pe.wait_ge(x_ready, l * 24 + 16 * f + 8)
                products(0, 0, (7, 8), 7, x_hi, x_lo, start=False).then_inc(units_multiplied, 1)
                norm(l, 2 * f)
                with pe.Fori(0, KF // 2 - 1) as i:
                    for slot in (1, 2, 3):
                        unit(i, slot)
                    unit(i + 1, 0)
                for slot in (1, 2, 3):
                    unit(KF // 2 - 1, slot)

            def residual(l, r0, first, blocks, xh, xl, hidden=None):
                units = len(blocks)
                with pe.Fori(0, 2) as i:
                    for j in range(4):
                        pe.wait_ge(residual_added, l * 24 + r0 + i * 4 + j + 1)
                        for u in range(units):
                            pos = j * units + u
                            if hidden is not None and j == 0:
                                pe.wait_ge(hidden_ready, hidden + min(8 * u + 8, KF))
                            unit_ready(l * QUADS + first // RING + i * units + pos // RING, pos % RING)
                            if hidden is None and j == 0:
                                pe.wait_ge(merged_ready, l * KD + KD - 1)
                                products(j, pos % RING, (0, KD - 1), 0, xh, xl, stop=False)
                                pe.wait_ge(merged_ready, l * KD + KD)
                                products(j, pos % RING, (KD - 1, KD), KD - 1, xh, xl, start=False).then_inc(units_multiplied, 1)
                            else:
                                products(j, pos % RING, (0, blocks[u]), 8 * u, xh, xl, start=u == 0,
                                         stop=u == units - 1).then_inc(units_multiplied, 1)

            def tile(l, c):
                pos = c + 6
                unit_ready(l * QUADS + U_MIX // RING + pos // RING, pos % RING)
                if c >= Z_FIRST:
                    pe.wait_ge(z_ready, c + 1)
                products(min(c, 3), pos % RING, (0, 8), 0, x_hi, x_lo).then_inc(units_multiplied, 1)

            def project(l):
                pe.wait_ge(mixers_open, l + 1)
                pe.sem_inc(phases_entered, 1)
                pe.wait_ge(x_ready, l * 24 + 16)
                for g in range(3):
                    s0 = 2 * g % RING
                    for w in range(WINDOWS):
                        c0, n = window(w)
                        idx = WINDOWS * g + w
                        if w == 0:
                            unit_ready(l * QUADS + U_MIX // RING + 2 * g // RING, s0 + 1)
                        if idx >= 8:
                            pe.wait_ge(v_ready, idx - 7)
                        for k in range(KD):
                            for m, (xp, wp) in enumerate(((x_hi, w_hi), (x_hi, w_lo), (x_lo, w_hi))):
                                mm = pe.matmul(ps[0:n, idx % 8, 0:256], xp[:, k, c0:c0 + n], wp[:, s0:s0 + 2, k, :],
                                               start=k == 0 and m == 0, stop=k == KD - 1 and m == 2)
                        mm.then_inc(*((v_products, 1) if w < WINDOWS - 1 else (units_multiplied, 2)))
                pe.wait_ge(v_ready, 15)
                for c in range(Z_FIRST):
                    tile(l, c)
                pe.wait_ge(low_split, 1)
                pe.wait_ge(z_ready, 1)
                products(0, 0, (0, 8), 0, x_hi, x_lo, wh=low_hi, wl=low_lo).then_inc(low_product, 1)

            def attention_sample(l):
                pe.wait_ge(z_ready, Z_FIRST + 1)
                for t in range(4):
                    pe.wait_ge(qk_squared, t + 1)
                    if t == 3:
                        pe.wait_ge(qk_log, 1)
                    sum_tile(QK_BANKS[t], ones[:, 2, :], n_room[:, t, :]).then_inc(qk_summed, 1)
                tile(l, Z_FIRST)
                pe.wait_ge(lam_products, 1)
                pe.wait_ge(qk_log, 4)
                pe.matmul(ps[:, 4, 0:2], ones[0:32, 0, :], coef[0:32, 2:4], start=True, stop=True).then_inc(lam_sums, 1)
                for c in range(Z_FIRST + 1, Z_BEFORE):
                    tile(l, c)
                pe.wait_ge(queries_placed, 1)
                for p in range(4):
                    if p:
                        pe.wait_ge(sample_max, p)
                    for b2 in range(2):
                        pe.wait_ge(keys_loaded[b2], 16 * PAGES * (p + 1))
                        for j in range(2):
                            r0 = 64 * b2 + 32 * j
                            q = qbd[:, j, 2 * p + b2, :]
                            for half in range(2):
                                pe.matmul(ps[r0:r0 + 32, half, :], q, kpage[:, b2, 4 * half:4 * half + 4, P * j:P * j + P], start=True, stop=True)
                            mm = pe.matmul(ps[r0:r0 + 32, 2, 0:TS], q, Z[:, DK + j, 0:TS], start=True, stop=True)
                        if b2 == 0:
                            tile(l, Z_BEFORE + 3 * p)
                    mm.then_inc(sample_scores, 1)
                    tile(l, Z_BEFORE + 3 * p + 1)
                    pe.wait_ge(sample_scaled, p + 1)
                    if p:
                        pe.wait_ge(sample_placed, p)
                    for s in range(8):
                        pe.transpose(ps[:, 3 + s // 4, s % 4 * P:(s % 4 + 1) * P], s_prob[:, s * P:(s + 1) * P], ident[:, :])
                    pe.transpose(ps[0:TS, 5, 0:P], s_prob[:, PAST:PAST + TS], ident[:, :]).then_inc(sample_turned, 1)
                    tile(l, Z_BEFORE + 3 * p + 2)
                    pe.wait_ge(sample_pt, 2 * (p + 1))
                    for b2 in range(2):
                        pe.wait_ge(values_loaded[b2], 16 * PAGES * (p + 1))
                        r0 = 64 * b2
                        for s in range(PAGES):
                            pe.matmul(ps[r0:r0 + 64, 5, 0:256], s_turn[:, s, r0:r0 + 64], vpage[:, b2, s, :], start=s == 0, stop=False)
                        mm = pe.matmul(ps[r0:r0 + 64, 5, 0:256], s_turn[0:TS, 8, r0:r0 + 64], V[0:TS, 0, 512:768], start=False, stop=True)
                    mm.then_inc(sample_pv, 1)
                    pe.wait_ge(sample_copied, p + 1)
                    for j in range(2):
                        mm = pe.transpose(ps[:, 5, P * j:P * j + P], s_out[:, j, :], ident[:, :])
                    mm.then_inc(sample_back, 1)

            def attention_prompt():
                steps = [(j, h) for j in range(WINDOWS) for h in range(H)]

                def scores(x):
                    j, h = steps[x]
                    c0, n = (TS, META) if j == 0 else window(j)
                    ns = META + P * j
                    if x:
                        pe.wait_ge(prompt_max, x)
                    for i in range(2):
                        r0 = 32 * (2 * (h % 2) + i)
                        q = Z[r0:r0 + 32, DQ + h // 2, c0:c0 + n]
                        k = Z[r0:r0 + 32, DK + h // 2, TS:TS + ns]
                        mm = pe.matmul(ps[0:n, 2 * i, 0:min(ns, 512)], q, k[:, 0:min(ns, 512)], start=True, stop=True)
                        if ns > 512:
                            mm = pe.matmul(ps[0:n, 2 * i + 1, 0:ns - 512], q, k[:, 512:ns], start=True, stop=True)
                    mm.then_inc(prompt_scores, 1)

                pe.wait_ge(z_ready, NZ + 1)
                def outputs(x):
                    j, h = steps[x]
                    n = META if j == 0 else P
                    pe.wait_ge(prompt_pt, x + 1)
                    if h % 2 == 0 and x:
                        pe.wait_ge(prompt_evac, x // 2)
                    r0 = 64 * (h % 2)
                    vc = 512 + 64 * h
                    for s in range(j):
                        pe.matmul(ps[r0:r0 + 64, 7, 0:n], V[:, s + 1, vc:vc + 64], p_turn[:, x % 2, s * P:(s + 1) * P], start=s == 0, stop=False)
                    pe.matmul(ps[r0:r0 + 64, 7, 0:n], V[64:64 + META, 0, vc:vc + 64], p_meta[64:64 + META, x % 2, 0:n],
                              start=j == 0, stop=True).then_inc(prompt_pv, 1)

                pe.wait_ge(sample_pt, 8)
                pe.wait_ge(sample_placed, 4)
                scores(0)
                for x, (j, h) in enumerate(steps):
                    n = META if j == 0 else P
                    if x + 1 < len(steps):
                        scores(x + 1)
                    pe.wait_ge(prompt_attn, x + 1)
                    if x:
                        pe.wait_ge(prompt_pt, x)
                    for s in range(j):
                        pe.transpose(ps[:, 4 + x % 2, s * P:(s + 1) * P], p_prob[0:n, x % 2, 0, META + s * P:META + (s + 1) * P], ident[0:n, 0:n])
                    pe.transpose(ps[0:META, 6, 0:n], p_prob[0:n, x % 2, 0, 0:META], ident[0:n, 0:n]).then_inc(prompt_turned, 1)
                    if x:
                        outputs(x - 1)
                outputs(len(steps) - 1)

            def retention():
                pe.wait_ge(prompt_evac, 10)
                pe.wait_ge(decay_tables_loaded, 16 * 2)
                for half in range(2):
                    mm = pe.matmul(ps[:, 4 + half, 0:HALF], aw[96:112, :], GL[:, half * HALF:(half + 1) * HALF], start=True, stop=True)
                mm.then_inc(alpha_product, 1)
                pe.wait_ge(ret_tables_loaded, 16 * 8)
                for t in range(4):
                    if t >= 2:
                        pe.wait_ge(rope_turned, t - 1)
                    sum_tile(t % 2, perm[:, :], Z[:, RQ + t, :]).then_inc(rope_swapped, 1)
                pe.wait_ge(ret_scaled, 1)
                for w in range(WINDOWS):
                    c0, n = window(w)
                    if w >= 2:
                        pe.wait_ge(ret_keys, w - 1)
                    pe.transpose(ps[0:n, w % 2, 0:P], rkh[:, 0, c0:c0 + n], ident[:, :])
                    pe.transpose(ps[0:n, w % 2, P:2 * P], rkh[:, 1, c0:c0 + n], ident[:, :]).then_inc(ret_blocks, 1)

                def scores(w):
                    c0, n = window(w)
                    if w >= 2:
                        pe.wait_ge(ret_decayed, w - 1)
                    for h in range(H):
                        r0 = 64 * (h % 2)
                        mm = pe.matmul(ps[0:n, 2 * (w % 2) + h % 2, h // 2 * n:(h // 2 + 1) * n], Z[r0:r0 + 64, RK + h // 2, c0:c0 + n],
                                       Z[r0:r0 + 64, RQ + h // 2, c0:c0 + n], start=True, stop=True)
                    mm.then_inc(ret_scores, 1)

                pe.wait_ge(ret_keys, WINDOWS)
                scores(0)
                for w in range(WINDOWS):
                    c0, n = window(w)
                    if w + 1 < WINDOWS:
                        scores(w + 1)
                    pe.wait_ge(ret_decayed, w + 1)
                    if w == 0:
                        pe.wait_ge(alpha_taken, 1)
                    if w >= 2:
                        pe.wait_ge(ret_evac, w - 1)
                    if w:
                        pe.wait_ge(ret_state, w)
                    for j in range(2):
                        out = ps[:, 4 + w % 2, P * j:P * j + n]
                        for i in range(2):
                            h = 2 * j + i
                            pe.matmul(out[64 * i:64 * i + 64, :], V[0:n, w, 64 * h:64 * h + 64], rsc[0:n, w % 2, h * n:(h + 1) * n],
                                      start=True, stop=True)
                        if w:
                            mm = pe.matmul(out, rst[:, j, :], rqh[:, j, c0:c0 + n], start=False, stop=True, skip_group_check=True)
                        else:
                            for b in range(NB):
                                mm = pe.matmul(out[:, NT * b:NT * b + NT], ss[:, j, b, :], rqh[:, j, NT * b:NT * b + NT],
                                               start=False, stop=True, skip_group_check=True)
                    mm.then_inc(ret_mixed, 1)
                    r0, rows = (64, META) if w == 0 else (0, P)
                    for j in range(2):
                        mm = pe.matmul(ps[:, 6 + w % 2, P * j:P * j + P], rkt[r0:r0 + rows, w, j, :], V[r0:r0 + rows, w, P * j:P * j + P],
                                       start=True, stop=True)
                    mm.then_inc(ret_update, 1)
                pe.wait_ge(ret_spread, 1)
                pe.wait_ge(ret_decayed, WINDOWS)
                for j in range(2):
                    for half in range(2):
                        mm = pe.matmul(ps[:, 2 * j + half, :], rkt[0:TS, 0, j, :], vm[0:TS, j, 4 * half:4 * half + 4, :], start=True, stop=True)
                mm.then_inc(ret_s_update, 1)

            def gla():
                pe.wait_ge(gla_scaled, 1)
                for w in range(WINDOWS):
                    c0, n = window(w)
                    if w == 0:
                        pe.wait_ge(ret_evac, WINDOWS)
                    if w >= 2:
                        pe.wait_ge(gla_keys, w - 1)
                    pe.transpose(ps[0:n, 4 + w % 2, 0:P], g_kh[:, c0:c0 + n], ident[:, :]).then_inc(gla_blocks, 1)
                pe.wait_ge(ret_s_state, 1)
                for idx, (n, w) in enumerate(level_items):
                    c0, cols = window(w)
                    pe.wait_ge(lvl_ready, n + 1)
                    if idx >= 2:
                        pe.wait_ge(lvl_taken, idx - 1)
                    if idx == 1:
                        pe.wait_ge(gla_keys, WINDOWS)
                    for h in range(H):
                        if n == 0:
                            k, q = Z[32 * h:32 * h + 32, GK, :], Z[32 * h:32 * h + 32, GQ, :]
                        else:
                            k, q = g_kl[32 * h:32 * h + 32, n % 2, :], g_ql[32 * h:32 * h + 32, n % 2, :]
                        mm = pe.matmul(ps[0:cols, 4 * (idx % 2) + h, 0:cols], k[:, c0:c0 + cols], q[:, c0:c0 + cols], start=True, stop=True)
                    mm.then_inc(lvl_scores, 1)
                pe.wait_ge(lvl_taken, len(level_items))
                pe.wait_ge(gla_tables_loaded, 16 * 2)
                for w in range(WINDOWS):
                    c0, n = window(w)
                    if w >= 2:
                        pe.wait_ge(gla_evac, w - 1)
                    if w:
                        pe.wait_ge(gla_state, w)
                    for j in range(2):
                        out = ps[:, 6 + w % 2, P * j:P * j + n]
                        for i in range(2):
                            h = 2 * j + i
                            pe.matmul(out[64 * i:64 * i + 64, :], V[0:n, w, 256 + 64 * h:320 + 64 * h], g_sc[0:n, w, h * n:(h + 1) * n],
                                      start=True, stop=True)
                        if w:
                            mm = pe.matmul(out, g_st[:, P * j:P * j + P], g_qh[:, c0:c0 + n], start=False, stop=True, skip_group_check=True)
                        else:
                            for b in range(NB):
                                mm = pe.matmul(out[:, NT * b:NT * b + NT], g_ss[:, b, P * j:P * j + P], g_qh[:, NT * b:NT * b + NT],
                                               start=False, stop=True, skip_group_check=True)
                    mm.then_inc(gla_mixed, 1)
                    r0, rows = (64, META) if w == 0 else (0, P)
                    pe.matmul(ps[:, 4 + w % 2, 0:256], g_kt[r0:r0 + rows, w, :], V[r0:r0 + rows, w, 256:512], start=True, stop=True).then_inc(gla_update, 1)
                pe.wait_ge(gla_spread, 1)
                for q in range(4):
                    mm = pe.matmul(ps[:, q, :], g_kt[0:TS, 0, :], g_vm[0:TS, 2 * q:2 * q + 2, :], start=True, stop=True)
                mm.then_inc(gla_s_update, 1)

            def head_norms():
                pe.wait_ge(gla_s_state, 1)
                pe.wait_ge(gla_evac, WINDOWS)
                pe.wait_ge(conv_done, 1)
                for j in range(2):
                    sum_tile(j, ones[:, 1, :], branch_tiles[2 + j]).then_inc(hn_summed, 1)
                for j in range(2):
                    mm = sum_tile(2, ones[:, 0, :], branch_tiles[j], start=j == 0, stop=j == 1)
                mm.then_inc(hn_summed, 1)
                for i, (banks, width, tiles) in enumerate(HEAD_NORMS):
                    pe.wait_ge(hn_squared, i + len(tiles))
                    if 1 <= i < 4:
                        pe.wait_ge(hn_centered, (1, 2, 4)[i - 1])
                    if i >= 4:
                        pe.wait_ge(hn_log_ready, i - 3)
                    for n in range(len(tiles)):
                        mm = sum_tile(banks, ones[:, 0 if width == 256 else 1, :], hn_sq[:, (i + n) % 4, :], start=n == 0, stop=n == len(tiles) - 1)
                    mm.then_inc(hn_totalled, 1)

            def gates(l):
                pe.wait_ge(hn_log_ready, 7)
                pe.sem_inc(phases_entered, 1)
                with pe.Fori(0, 2) as i:
                    for mm_ in range(4):
                        m = i * 4 + mm_
                        for n in range(5):
                            pos = mm_ * 5 + n
                            quad, slot = l * QUADS + U_GATES // RING + i * 5 + pos // RING, pos % RING
                            unit_ready(quad, slot)
                            if n < 4:
                                pe.wait_ge(branch_taken, m * 4 + n + 1)
                                products(n, slot, (0, 8), 0, x_hi, x_lo).then_inc(units_multiplied, 1)
                            else:
                                pe.wait_ge(br_split, 8)
                                for b in range(4):
                                    pe.wait_ge(gate_tanh, m * 4 + b + 1)
                                    last = products(b, slot, (2 * b, 2 * b + 2), 2 * b, br_hi, br_lo)
                                    last.then_inc(*((branch_products, 1) if b < 3 else (units_multiplied, 1)))
                pe.wait_ge(branch_taken, 4 * KD + 1)
                pe.drain().then_inc(mixers_left, 1)

            pe.sem_inc(units_multiplied, RING)
            pe.wait_ge(consts_loaded, 16 * CONSTS)
            pe.wait_ge(bias_row_made, 1)
            for n, c in enumerate(range(0, RL, 512)):
                mm = pe.matmul(ps[0:16, 4 + n, 0:min(512, RL - c)], rb[0:33, :], bucket[0:33, c:min(c + 512, RL)], start=True, stop=True)
            mm.then_inc(bias_row_made, 1)
            pe.wait_ge(bias_row_made, 3)
            with pe.Fori(0, DEPTH) as l:
                gate_up(l, 0, U_FFN1)
                residual(l, 0, U_DOWN1, DOWN_BLOCKS, hid_hi, hid_lo, l * 2 * KF)
                norm(l, 1)
                project(l)
                attention_sample(l)
                attention_prompt()
                retention()
                gla()
                head_norms()
                gates(l)
                residual(l, 8, U_OUT, (8,), m_hi, m_lo)
                gate_up(l, 1, U_FFN2)
                residual(l, 16, U_DOWN2, DOWN_BLOCKS, hid_hi, hid_lo, l * 2 * KF + KF)

        @block.vector
        def _(v):
            def split_low(quad, slot):
                v.wait_ge(weights_high, 4 * quad + slot + 1)
                v.tensor_tensor(w_lo[:, slot, :, :], w_raw[:, slot, :, :], w_hi[:, slot, :, :].bitcast(F32), ALU.subtract).then_inc(weights_low, 1)

            def unit_done(quad, slot):
                v.wait_ge(units_multiplied, 4 * quad + slot + 1 + RING)

            def clear_sum(count):
                v.memset(ssum, 0.0).then_inc(sum_cleared, 1)
                v.wait_ge(sum_cleared, count)
                v.sem_inc(phases_entered, 1)

            def norm(l):
                w = l * 3 + 1
                v.wait_ge(inverse_ready, w + 1)

                def low(k):
                    v.wait_ge(x_high, 24 * l + 8 + k + 1)
                    v.wait_ge(normed, 8 * l + k + 1)
                    v.tensor_tensor(x_lo[:, k, :], fresh[k % 3], x_hi[:, k, :].bitcast(F32), ALU.subtract).then_inc(x_ready, 1)

                for k in range(KD):
                    c = P_GAIN + 8 + k
                    if k >= 3:
                        v.wait_ge(x_ready, 24 * l + 8 + k - 2)
                    v.scalar_tensor_tensor(fresh[k % 3], hT[:, k, :], prm[:, c:c + 1], tmp[:, 0, :], ALU.mult, ALU.mult).then_inc(normed, 1)
                    if k:
                        low(k - 1)
                low(KD - 1)

            def gate_up(l, f, first):
                v.wait_ge(inverse_ready, l * 3 + 2 * f + 1)
                v.sem_inc(phases_entered, 1)
                with v.Fori(0, KF // 2) as i:
                    for j in range(2):
                        q = l * 2 * KF + f * KF + i * 2 + j
                        quad = l * QUADS + first // RING + i
                        unit_done(quad, 2 * j)
                        v.tensor_tensor(split_cols(tmp[:, j, :]), pair(2 * j), split_cols(ssum), ALU.mult).then_inc(gate_scaled, 1)
                        split_low(quad + 1, 2 * j)
                        v.wait_ge(tanh_ready, q + 1)
                        v.scalar_tensor_tensor(gu[:, j, :], gu[:, j, :], 1.0, tmp[:, j, :], ALU.add, ALU.mult).then_inc(gated, 1)
                        v.wait_ge(gated, 2 * q + 1)
                        v.tensor_tensor(gu[:, j, :], gu[:, j, :], ssum, ALU.mult).then_inc(gated, 1)
                        unit_done(quad, 2 * j + 1)
                        v.wait_ge(gated, 2 * q + 2)
                        v.tensor_tensor(split_cols(gu[:, j, :]), split_cols(gu[:, j, :]), pair(2 * j + 1), ALU.mult).then_inc(hidden_made, 1)
                        split_low(quad + 1, 2 * j + 1)
                        v.wait_ge(hidden_made, q + 3)
                        v.wait_ge(hidden_high, q + 1)
                        v.tensor_tensor(hid_lo[:, ds(i * 2 + j, 1), :], gu[:, j:j + 1, :], hid_hi[:, ds(i * 2 + j, 1), :].bitcast(F32), ALU.subtract).then_inc(hidden_ready, 1)
                clear_sum(3 * l + 2 * f + 2)

            def sum_and_split(square, tile, gain, high, low):
                v.tensor_tensor(ssum, ssum, square, ALU.add).then_inc(squares_summed, 1)
                if gain is not None:
                    v.scalar_tensor_tensor(low, tile, gain, high.bitcast(F32), ALU.mult, ALU.subtract).then_inc(x_ready, 1)

            def residual(l, r0, first, units, scale, gain):
                with v.Fori(0, 2) as i:
                    for j in range(4):
                        r = l * 24 + r0 + i * 4 + j
                        m = i * 4 + j
                        for u in range(units):
                            pos = j * units + u
                            quad, slot = l * QUADS + first // RING + i * units + pos // RING, pos % RING
                            if u == units - 1:
                                unit_done(quad, slot)
                                tile = hT[:, ds(m, 1), :].rearrange("p a (h t) -> p (a h) t", h=2)
                                v.scalar_tensor_tensor(tile, pair(j), scale, tile, ALU.mult, ALU.add).then_inc(residual_added, 1)
                            split_low(quad + 1, slot)
                        v.wait_ge(squared, 9 + r)
                        v.wait_ge(squares_summed, 8 + r)
                        if gain is not None:
                            v.wait_ge(residual_added, r + 5)
                            v.wait_ge(x_high, r + 9)
                        sum_and_split(tmp[:, j % 2, :], hT[:, ds(m, 1), :], None if gain is None else prm[:, ds(m + gain, 1)],
                                      x_hi[:, ds(m, 1), :], x_lo[:, ds(m, 1), :])

            chain = [0]

            def link(ins):
                chain[0] += 1
                ins.then_inc(vector_chain, 1)
                v.wait_ge(vector_chain, chain[0])

            def project(l):
                v.wait_ge(mixers_open, l + 1)
                v.sem_inc(phases_entered, 1)
                v.wait_ge(vb_loaded, 16)
                for g in range(3):
                    for w in range(WINDOWS):
                        n = window(w)[1]
                        idx = WINDOWS * g + w
                        quad = l * QUADS + U_MIX // RING + 2 * g // RING
                        if w < WINDOWS - 1:
                            v.wait_ge(v_products, 4 * g + w + 1)
                        else:
                            unit_done(quad, 2 * g % RING + 1)
                        v.tensor_tensor(V[0:n, w, 256 * g:256 * g + 256], ps[0:n, idx % 8, 0:256], vb[0:n, 256 * g:256 * g + 256], ALU.add).then_inc(v_ready, 1)
                    for s in range(2):
                        split_low(quad + 1, 2 * g % RING + s)
                v.wait_ge(low_high, 1)
                v.tensor_tensor(low_lo[:, :, :], low_raw[:, :, :], low_hi[:, :, :].bitcast(F32), ALU.subtract).then_inc(low_split, 1)
                for c in range(Z_FIRST):
                    tile(l, c)

            def tile(l, c):
                pos = c + 6
                split_low(l * QUADS + U_MIX // RING + pos // RING + 1, pos % RING)

            def attention_sample(l):
                v.tensor_tensor(coef[0:32, 2:4], prm[0:32, P_LAM:P_LAM + 2], prm[0:32, P_LAM + 2:P_LAM + 4], ALU.mult).then_inc(lam_products, 1)
                v.tensor_scalar(hb[:, :], prm[:, P_GB:P_GB + 32], 0.5, None, ALU.mult)
                for t in range(4):
                    v.wait_ge(qk_root, t + 1)
                    c = P_QN if t < 2 else P_KN
                    v.scalar_tensor_tensor(Z[:, t, :], Z[:, t, :], prm[:, c:c + 1], n_room[:, t, :], ALU.mult, ALU.mult).then_inc(qk_normed, 1)
                v.wait_ge(lam_exps, 1)
                link(v.tensor_tensor(coef[:, 4:5], coef[:, 3:4], coef[:, 2:3], ALU.subtract))
                link(v.tensor_tensor(coef[:, 4:5], coef[:, 4:5], prm[:, P_LI:P_LI + 1], ALU.subtract))
                v.scalar_tensor_tensor(coef[:, 5:6], coef[:, 1:2], coef[:, 4:5], coef[:, 0:1], ALU.mult, ALU.add)
                link(v.memset(qbd[:, :, :, :], 0.0))
                v.wait_ge(qk_normed, 4)
                for j in range(2):
                    for g in range(4):
                        ins = v.tensor_copy(qbd[32 * g:32 * g + 32, j, :, 8 * g:8 * g + 8],
                                            Z[32 * g:32 * g + 32, DQ + j, 0:TS].rearrange("p (b t) -> p b t", b=NB))
                ins.then_inc(queries_placed, 1)
                for c in range(Z_FIRST, Z_BEFORE):
                    tile(l, c)
                v.wait_ge(attn_tables_loaded, 16 * 9)
                link(v.tensor_tensor(new_bias[:, :, :].rearrange("p a (b s) -> p a b s", s=NT),
                                     new_mask[:, :, :].rearrange("p a (b s) -> p a b s", s=NT),
                                     s_bias[:, None, None, PAST:PAST + NT].to_broadcast([P, 4, NB, NT]), ALU.add))
                part = early_taps // 9
                for p in range(4):
                    n = 3 * part * (p - 1)
                    if p:
                        conv_taps(n, n + part)
                    tile(l, Z_BEFORE + 3 * p)
                    v.wait_ge(sample_scores, p + 1)
                    if p:
                        v.wait_ge(sample_turned, p)
                    link(v.tensor_tensor_reduce(out=s_prob[:, 0:PAST], in0=ps[:, 0:2, :].rearrange("p b c -> p (b c)"), in1=s_bias[:, 0:PAST],
                                                scale=ATT_SCALE, scalar=-3e38, op0=ALU.add, op1=ALU.max, accum_out=coef[:, 7:8]))
                    link(v.tensor_tensor_reduce(out=s_prob[:, PAST:PAST + TS], in0=ps[:, 2, 0:TS], in1=new_bias[:, p, :],
                                                scale=ATT_SCALE, scalar=coef[:, 7:8], op0=ALU.add, op1=ALU.max, accum_out=coef[:, 6:7]))
                    v.tensor_scalar(coef[:, 6:7], coef[:, 6:7], -1.0, None, ALU.mult).then_inc(sample_max, 1)
                    v.wait_ge(sample_exp, p + 1)
                    link(v.reciprocal(coef[:, 7:8], coef[:, 7:8]))
                    link(v.tensor_tensor(coef[:, 7:8], coef[:, 7:8], coef[:, 5:6], ALU.mult))
                    v.tensor_scalar(s_prob[:, :], s_prob[:, :], coef[:, 7:8], None, ALU.mult).then_inc(sample_scaled, 1)
                    if p:
                        conv_taps(n + part, n + 2 * part)
                    tile(l, Z_BEFORE + 3 * p + 1)
                    if p:
                        conv_taps(n + 2 * part, n + 3 * part if p < 3 else early_taps)
                    tile(l, Z_BEFORE + 3 * p + 2)
                    v.wait_ge(sample_back, p + 1)
                    for h2 in range(2):
                        for j in range(2):
                            rows = ps[64 * h2:64 * h2 + 64, 5, P * j:P * j + P].rearrange("p (b r) -> p b r", b=2)
                            c = 32 * j + 16 * h2
                            link(v.tensor_copy(s_half[64 * h2:64 * h2 + 64, j, :].rearrange("p (b t) -> p b t", b=2), rows[:, :, c:c + 8]))
                            ins = v.tensor_tensor(od[64 * h2:64 * h2 + 64, j, 2 * NT * p:2 * NT * (p + 1)].rearrange("p (b t) -> p b t", b=2),
                                                  s_half[64 * h2:64 * h2 + 64, j, :].rearrange("p (b t) -> p b t", b=2), rows[:, :, c + 8:c + 16], ALU.add)
                    ins.then_inc(sample_placed, 1)
                    if p == 0:
                        conv_inputs()
            taps = [(k, j, part) for k in range(CK) for j in range(2) for part in range(2)]
            steps_taps = 2
            early_taps = len(taps) - steps_taps * WINDOWS * H

            def conv_inputs():
                for j in range(2):
                    v.wait_ge(conv_tanh, j + 1)
                    v.scalar_tensor_tensor(glu[:, j, :], Z[:, CG + j, :], 1.0, Z[:, CA + j, :], ALU.add, ALU.mult).then_inc(conv_gated, 1)
                v.wait_ge(conv_gated, 2)
                v.memset(ue_p[:, :, 0:CK - 1], 0.0).then_inc(conv_gated, 1)

            def conv_taps(first, end):
                if first == 0:
                    v.wait_ge(conv_rows, 4)
                    v.wait_ge(conv_gated, 3)
                for n in range(first, end):
                    k, j, part = taps[n]
                    tap = prm[:, P_CW + CK * j + k:P_CW + CK * j + k + 1]
                    if part:
                        src = ue_p[:, j, k:k + LP]
                        dst = Z[:, CG + j, TS:T]
                    else:
                        src = ue_s[:, j, :, k:k + NT]
                        dst = Z[:, CG + j, 0:TS].rearrange("p (b t) -> p b t", b=NB)
                    if k == 0:
                        v.tensor_scalar(dst, src, tap, prm[:, P_CB + j:P_CB + j + 1], ALU.mult, ALU.add).then_inc(conv_steps, 1)
                    else:
                        v.wait_ge(conv_steps, n - 3)
                        v.scalar_tensor_tensor(dst, src, tap, dst, ALU.mult, ALU.add).then_inc(conv_steps, 1)

            def attention_prompt():
                steps = [(j, h) for j in range(WINDOWS) for h in range(H)]

                def biased(x):
                    j, h = steps[x]
                    n = META if j == 0 else P
                    ns = META + P * j
                    t0 = 0 if j == 0 else META + P * (j - 1)
                    v.wait_ge(prompt_scores, x + 1)
                    if x >= 2:
                        v.wait_ge(prompt_turned, x - 1)
                    for i in range(2):
                        src = ps[0:n, 2 * i:2 * i + 2, :].rearrange("p b c -> p (b c)")[:, 0:ns]
                        ins = v.tensor_tensor_reduce(out=p_prob[0:n, x % 2, i, 0:ns], in0=src, in1=p_bias[0:n, h, LP - P - t0:LP - P - t0 + ns],
                                                     scale=ATT_SCALE, scalar=-3e38, op0=ALU.add, op1=ALU.max, accum_out=small[0:n, x % 2, 4 + i:5 + i])
                    link(ins)
                    v.tensor_scalar(small[0:n, x % 2, 0:2], small[0:n, x % 2, 4:6], -1.0, None, ALU.mult).then_inc(prompt_max, 1)

                v.wait_ge(z_ready, NZ + 1)
                v.wait_ge(prompt_bias_loaded, 16)
                v.wait_ge(sample_turned, 4)
                biased(0)
                for x, (j, h) in enumerate(steps):
                    n = META if j == 0 else P
                    ns = META + P * j
                    v.wait_ge(prompt_exp, 2 * (x + 1))
                    sums = small[0:n, x % 2, 2:4]
                    link(v.reciprocal(sums, sums))
                    link(v.tensor_tensor(sums[:, 1:2], sums[:, 1:2], coef[0:n, 4:5], ALU.mult))
                    one, two = p_prob[0:n, x % 2, 0, 0:ns], p_prob[0:n, x % 2, 1, 0:ns]
                    link(v.tensor_scalar(one, one, sums[:, 0:1], None, ALU.mult))
                    v.scalar_tensor_tensor(one, two, sums[:, 1:2], one, ALU.mult, ALU.add).then_inc(prompt_attn, 1)
                    if x + 1 < len(steps):
                        biased(x + 1)
                    conv_taps(early_taps + steps_taps * x, early_taps + steps_taps * (x + 1))
                v.wait_ge(conv_steps, len(taps))
                v.sem_inc(conv_done, 1)

            def by_window(ap, j=None):
                return ap[:, TS + META:T].rearrange("p (w t) -> p w t", t=P)

            def retention():
                v.wait_ge(ret_tables_loaded, 16 * 8)
                v.wait_ge(prompt_pt, 20)
                v.wait_ge(prompt_pv, 20)
                for t in range(4):
                    a, b = rtmp[:, t % 2, 0, :], rtmp[:, t % 2, 1, :]
                    scale = 1.0 if t < 2 else 64 ** -0.5
                    v.scalar_tensor_tensor(a, Z[:, RQ + t, :], scale, rope[:, 0, :], ALU.mult, ALU.mult)
                    v.wait_ge(rope_swapped, t + 1)
                    link(v.scalar_tensor_tensor(split_cols(b), pair(t % 2), scale, split_cols(rope[:, 1, :]), ALU.mult, ALU.mult))
                    v.tensor_tensor(Z[:, RQ + t, :], a, b, ALU.add).then_inc(rope_turned, 1)
                v.wait_ge(rope_turned, 4)
                v.memset(rst[:, :, :], 0.0)
                for src, table, dst in ((RQ, gq, rqh), (RK, gk, rkh)):
                    for j in range(2):
                        v.tensor_tensor(dst[:, j, 0:80], Z[:, src + j, 0:80], table[:, j, 0:80], ALU.mult)
                        ins = v.tensor_tensor(by_window(dst[:, j, :]), by_window(Z[:, src + j, :]),
                                              table[:, j:j + 1, 80:208].to_broadcast([P, 4, P]), ALU.mult)
                ins.then_inc(ret_scaled, 1)

                def decayed(w):
                    n = window(w)[1]
                    v.wait_ge(ret_scores, w + 1)
                    if w >= 2:
                        v.wait_ge(ret_mixed, w - 1)
                    table = dec[:, :, :] if w else dec0[0:80, :, :]
                    src = ps[0:n, 2 * (w % 2):2 * (w % 2) + 2, 0:2 * n].rearrange("p i (j t) -> p i j t", j=2)
                    v.tensor_tensor(rsc[0:n, w % 2, 0:H * n].rearrange("p (j i t) -> p i j t", j=2, i=2), src,
                                    table.rearrange("p (j i) t -> p i j t", j=2), ALU.mult).then_inc(ret_decayed, 1)

                v.wait_ge(decay_tables_loaded, 16 * 2)
                v.wait_ge(alpha_log, 1)
                link(v.scalar_tensor_tensor(g_eb, g_eb, 0.0, g_b, ALU.min, ALU.subtract))
                link(v.tensor_scalar(g_eb, g_eb, 1.0 / 16, None, ALU.mult))
                v.tensor_tensor_scan(g_b, reset, g_eb, 0.0, ALU.mult, ALU.add).then_inc(gla_summed, 1)
                v.wait_ge(gla_summed, 1)
                for c0, n, size in ((0, NB, NT), (TS, 1, META), (TS + META, 4, P)):
                    src = g_b[:, c0:c0 + n * size].rearrange("p (n t) -> p n t", n=n)
                    ins = v.tensor_tensor(g_rest[:, c0:c0 + n * size].rearrange("p (n t) -> p n t", n=n),
                                          src[:, :, size - 1:size].to_broadcast([P, n, size]), src, ALU.subtract)
                ins.then_inc(gla_diff, 1)
                link(v.tensor_scalar(Z[:, GQ, :], Z[:, GQ, :], 32 ** -0.5, None, ALU.mult))
                decayed(0)
                for w in range(WINDOWS):
                    if w + 1 < WINDOWS:
                        decayed(w + 1)
                    v.wait_ge(ret_mixed, w + 1)
                    v.wait_ge(ret_update, w + 1)
                    if w == 2:
                        v.wait_ge(gla_exp_b, 1)
                        v.tensor_tensor(g_qh[:, :], Z[:, GQ, :], g_eb, ALU.mult)
                        v.wait_ge(gla_exp_last, 1)
                        v.tensor_tensor(g_kh[:, :], Z[:, GK, :], g_rest, ALU.mult).then_inc(gla_scaled, 1)
                    if w:
                        v.wait_ge(ret_state, w)
                    for h in range(H):
                        j, r = h // 2, 64 * (h % 2)
                        block_ = rst[r:r + 64, j, r:r + 64]
                        ins = v.scalar_tensor_tensor(block_, block_, float(GAMMA[h] ** P), ps[r:r + 64, 6 + w % 2, P * j + r:P * j + r + 64], ALU.mult, ALU.add)
                    ins.then_inc(ret_state, 1)
                for j in range(2):
                    ins = v.tensor_tensor(vm[0:TS, j, :, :], V[0:TS, 0:1, P * j:P * j + P].to_broadcast([TS, NB, P]),
                                          seqs[0:TS, :, None].to_broadcast([TS, NB, P]), ALU.mult)
                ins.then_inc(ret_spread, 1)
                v.wait_ge(ret_s_update, 1)
                for h in range(H):
                    j, r = h // 2, 64 * (h % 2)
                    block_ = ss[r:r + 64, j, :, r:r + 64]
                    new = ps[r:r + 64, 2 * j:2 * j + 2, :].rearrange("p q (b n) -> p (q b) n", b=4)[:, :, r:r + 64]
                    ins = v.scalar_tensor_tensor(block_, block_, float(GAMMA[h] ** NT), new, ALU.mult, ALU.add)
                ins.then_inc(ret_s_state, 1)

            def gla():
                link(v.memset(g_st[:, :], 0.0))
                v.memset(Z[:, 0:4, :], 0.0).then_inc(lvl_ready, 1)

                v.wait_ge(masks_loaded, 16 * 2)
                v.wait_ge(mixers_stored, 16 * (MIXER_STORES - 2))

                def difference(n):
                    size = LEVELS[n]
                    c0 = level_start(size)
                    src = g_b[:, c0:T].rearrange("p (n b) -> p n b", b=size)
                    if n == 1:
                        v.wait_ge(gla_scaled, 1)
                    if n >= 2:
                        v.wait_ge(lvl_ready, n)
                    v.tensor_tensor(g_e[:, n % 2, c0:T].rearrange("p (n b) -> p n b", b=size), src,
                                    src[:, :, size // 2 - 1:size // 2].to_broadcast([P, (T - c0) // size, size]), ALU.subtract).then_inc(lvl_diff, 1)

                def take(n):
                    for idx, (m, w) in enumerate(level_items):
                        if m != n:
                            continue
                        cols = window(w)[1]
                        v.wait_ge(lvl_scores, idx + 1)
                        src = ps[0:cols, 4 * (idx % 2):4 * (idx % 2) + 4, 0:cols]
                        dst = g_sc[0:cols, w, 0:H * cols].rearrange("p (h t) -> p h t", h=H)
                        m0 = max(n - 3, 0)
                        mask = (lvl[:, n:n + 1, :] if w else lvl0[0:80, m0:m0 + 1, :]).to_broadcast([cols, H, cols])
                        if n == 0:
                            v.tensor_tensor(dst, src, mask, ALU.mult).then_inc(lvl_taken, 1)
                        else:
                            v.copy_predicated(dst, mask.bitcast(U32), src).then_inc(lvl_taken, 1)

                difference(0)
                for n, size in enumerate(LEVELS):
                    c0 = level_start(size)

                    def half(ap, part):
                        view = ap[:, c0:T].rearrange("p (n b) -> p n b", b=size)
                        return view[:, :, size // 2:size] if part else view[:, :, 0:size // 2]

                    if n + 1 < len(LEVELS):
                        difference(n + 1)
                    v.wait_ge(lvl_exp, 2 * (n + 1))
                    if n >= 2:
                        v.wait_ge(lvl_scores, items_through(n - 1))
                    v.tensor_tensor(half(g_kl[:, (n + 1) % 2, :], 0), half(Z[:, GK, :], 0), half(g_e[:, n % 2, :], 0), ALU.mult)
                    v.tensor_tensor(half(g_ql[:, (n + 1) % 2, :], 1), half(Z[:, GQ, :], 1), half(g_e[:, n % 2, :], 1), ALU.mult).then_inc(lvl_ready, 1)
                    if n:
                        v.wait_ge(lvl_taken, items_through(n - 1))
                    take(n)
                v.wait_ge(lvl_taken, items_through(len(LEVELS) - 1))
                take(len(LEVELS))
                for w in range(WINDOWS):
                    v.wait_ge(gla_mixed, w + 1)
                    v.wait_ge(gla_update, w + 1)
                    if w:
                        v.wait_ge(gla_state, w)
                    last = window(w)[0] + window(w)[1] - 1
                    for h in range(H):
                        block_ = g_st[32 * h:32 * h + 32, 64 * h:64 * h + 64]
                        ins = v.scalar_tensor_tensor(block_, block_, g_eb[32 * h:32 * h + 32, last:last + 1],
                                                     ps[32 * h:32 * h + 32, 4 + w % 2, 64 * h:64 * h + 64], ALU.mult, ALU.add)
                    ins.then_inc(gla_state, 1)
                v.tensor_tensor(g_vm[0:TS, :, :], V[0:TS, 0:1, 256:512].to_broadcast([TS, NB, 256]),
                                g_seqs[0:TS, :, None].to_broadcast([TS, NB, 256]), ALU.mult).then_inc(gla_spread, 1)
                for h in range(H):
                    block_ = g_ss[32 * h:32 * h + 32, :, 64 * h:64 * h + 64]
                    decay = g_eb[32 * h:32 * h + 32, 0:TS].rearrange("p (b t) -> p b t", b=NB)[:, :, NT - 1:NT].to_broadcast([32, NB, 64])
                    ins = v.tensor_tensor(block_, block_, decay, ALU.mult)
                link(ins)
                v.wait_ge(gla_s_update, 1)
                for h in range(H):
                    block_ = g_ss[32 * h:32 * h + 32, :, 64 * h:64 * h + 64]
                    new = ps[32 * h:32 * h + 32, 0:4, :].rearrange("p q (b n) -> p (q b) n", b=2)[:, :, 64 * h:64 * h + 64]
                    ins = v.tensor_tensor(block_, block_, new, ALU.add)
                ins.then_inc(gla_s_state, 1)

            def head_norms():
                v.sem_inc(branch_taken, 4)
                v.wait_ge(conv_steps, len(taps))
                for i, (tile, banks, width) in enumerate(((2, 0, 64), (3, 1, 64), (0, 2, 256), (1, 2, 256))):
                    v.wait_ge(hn_summed, min(i, 2) + 1)
                    x = split_cols(branch_tiles[tile])
                    v.scalar_tensor_tensor(x, pair(banks), -1.0 / width, x, ALU.mult, ALU.add).then_inc(hn_centered, 1)
                for n, c in enumerate((RG, RG + 1, GR, GR + 1)):
                    v.wait_ge(act_tanh, n + 1)
                    v.scalar_tensor_tensor(Z[:, c, :], Z[:, TG + n, :], 1.0, Z[:, c, :], ALU.add, ALU.mult).then_inc(silu_ready, 1)
                v.tensor_tensor(coef[:, 6:7], prm[:, P_SUB:P_SUB + 1], prm[:, P_LI1:P_LI1 + 1], ALU.mult).then_inc(silu_ready, 1)
                v.wait_ge(silu_ready, 5)
                v.wait_ge(hn_centered, 4)

                def normed(i):
                    v.wait_ge(hn_root_ready, i + 1)
                    for tile, c in HEAD_NORMS[i][2]:
                        gain = coef[:, 6:7] if i < 2 else prm[:, c:c + 1]
                        ins = v.scalar_tensor_tensor(tile, tile, gain, hn_root[:, i % 4, :], ALU.mult, ALU.mult)
                    ins.then_inc(hn_normed, 1)

                for i in range(7):
                    normed(i)
                v.wait_ge(hn_normed, 7)
                for j in range(2):
                    ins = v.tensor_scalar(Z[:, CG + j, :], Z[:, CG + j, :], prm[:, P_LB + j:P_LB + j + 1], None, ALU.add)
                ins.then_inc(conv_done, 1)
                v.sem_inc(br_ready, 2)
                for b, c in ((4, GR), (5, GR + 1), (2, RG), (3, RG + 1)):
                    v.scalar_tensor_tensor(branch_tiles[b], Z[:, c, :], 0.5, branch_tiles[b], ALU.mult, ALU.mult).then_inc(br_ready, 1)

            def branches():
                def low(n):
                    b = FINISHED[n]
                    v.wait_ge(br_high, n + 1)
                    v.tensor_tensor(br_lo[:, b, :], branch_tiles[b], br_hi[:, b, :].bitcast(F32), ALU.subtract).then_inc(br_split, 1)

                v.wait_ge(br_ready, 6)
                for n in range(4):
                    low(n)
                for n in range(2):
                    v.wait_ge(act_tanh, 5 + n)
                    link(v.tensor_scalar(hn_root[:, n, :], hn_root[:, n, :], 1.0, 0.5, ALU.add, ALU.mult))
                    v.tensor_tensor(branch_tiles[n], branch_tiles[n], hn_root[:, n, :], ALU.mult).then_inc(br_ready, 1)
                v.wait_ge(br_ready, 8)
                for n in range(4, 8):
                    low(n)

            def gates(l):
                v.wait_ge(mixers_stored, 16 * MIXER_STORES)
                clear_sum(3 * l + 3)
                with v.Fori(0, 2) as i:
                    for mm in range(4):
                        m = i * 4 + mm
                        for n in range(4):
                            pos = mm * 5 + n
                            split_low(l * QUADS + U_GATES // RING + i * 5 + pos // RING + 1, pos % RING)
                        pos = mm * 5 + 4
                        quad, slot = l * QUADS + U_GATES // RING + i * 5 + pos // RING, pos % RING
                        for b in range(4):
                            if b < 3:
                                v.wait_ge(branch_products, m * 3 + b + 1)
                            else:
                                unit_done(quad, slot)
                            if b > 1:
                                v.wait_ge(merged_steps, m * 3 + b - 1)
                            v.scalar_tensor_tensor(split_cols(d_acc[:, min(b, 1), :]), split_cols(d_sg[:, b, :]), 1.0, pair(b), ALU.add, ALU.mult
                                                   ).then_inc(branch_taken, 1)
                            if b:
                                v.wait_ge(branch_taken, m * 4 + b + 1 + 4)
                                v.tensor_tensor(d_acc[:, 0, :], d_acc[:, 0, :], d_acc[:, 1, :], ALU.add).then_inc(merged_steps, 1)
                        split_low(quad + 1, slot)
                        v.wait_ge(merged_steps, m * 3 + 3)
                        v.wait_ge(merged_high, m + 1)
                        v.scalar_tensor_tensor(m_lo[:, ds(m, 1), :], d_acc[:, 0:1, :], 0.5, m_hi[:, ds(m, 1), :].bitcast(F32),
                                               ALU.mult, ALU.subtract).then_inc(merged_ready, 1)
                v.drain().then_inc(mixers_left, 1)

            v.sem_inc(weights_low, RING)
            v.sem_inc(hidden_made, 2)
            v.sem_inc(residual_added, 4)
            clear_sum(1)
            for m in range(KD):
                v.wait_ge(squared, m + 1)
                v.wait_ge(x_high, m + 1)
                if m:
                    v.wait_ge(squares_summed, m)
                sum_and_split(tmp[:, m % 2, :], hT[:, m, :], prm[:, P_GAIN + m:P_GAIN + m + 1], x_hi[:, m, :], x_lo[:, m, :])
                if m % 2:
                    s = m // 2
                    v.wait_ge(weights_high, s + 1)
                    v.tensor_tensor(w_lo[:, s, :, :], w_raw[:, s, :, :], w_hi[:, s, :, :].bitcast(F32), ALU.subtract).then_inc(weights_low, 1)
                if m == 5:
                    v.wait_ge(consts_loaded, 16 * CONSTS)
                    v.tensor_scalar(rb[0:32, :], rb[0:32, :], 1.0 / ATT_SCALE, None, ALU.mult).then_inc(bias_row_made, 1)
            v.wait_ge(bias_row_made, 2)
            v.tensor_copy(brow[:, :], ps[0:16, 4:7, :].rearrange("p b c -> p (b c)")[:, 0:RL]).then_inc(bias_row_made, 1)
            with v.Fori(0, DEPTH) as l:
                gate_up(l, 0, U_FFN1)
                residual(l, 0, U_DOWN1, 3, 0.25, None)
                norm(l)
                project(l)
                attention_sample(l)
                attention_prompt()
                retention()
                gla()
                head_norms()
                branches()
                gates(l)
                residual(l, 8, U_OUT, 1, 1.0, P_GAIN + 16)
                gate_up(l, 1, U_FFN2)
                residual(l, 16, U_DOWN2, 3, 0.25, P_GAIN)


def constants():
    f = np.float32
    col = np.arange(T)
    pos = np.where(col < TS, PAST + col % NT, col - TS).astype(np.int32)
    inv = f(10000.0) ** (-np.arange(32, dtype=f) / f(32))
    ang = (pos.astype(f)[None, :] * inv[np.arange(P) % 32][:, None]).astype(f)
    rope = np.stack([np.cos(ang), np.sin(ang)], axis=1).astype(f)
    perm = np.zeros((P, P), f)
    for m in range(P):
        if m % 64 < 32:
            perm[m + 32, m] = -1
        else:
            perm[m - 32, m] = 1
    gam = np.array(GAMMA, np.float64)
    a = np.arange(P)
    d = a[None, :] - a[:, None]
    dec = np.where(d[:, None, :] >= 0, gam[None, :, None] ** np.maximum(d, 0)[:, None, :], 0).astype(f)
    a = np.arange(80)
    d = a[None, :] - a[:, None]
    chunk = np.where(a < TS, a // NT, NB)
    ok = (d >= 0) & (chunk[:, None] == chunk[None, :])
    dec0 = np.where(ok[:, None, :], gam[None, :, None] ** np.maximum(d, 0)[:, None, :], 0).astype(f)
    c = np.arange(208)
    step = np.where(c < TS, c % NT, np.where(c < 80, c - TS, c - 80))
    size = np.where(c < TS, NT, np.where(c < 80, META, P))
    head = 2 * np.arange(2)[None, :] + np.arange(P)[:, None] // 64
    gq = (gam[head][:, :, None] ** (step + 1)).astype(f)
    gk = (gam[head][:, :, None] ** (size - 1 - step)).astype(f)
    seq = (np.arange(TS)[:, None] // NT == np.arange(NB)[None, :]).astype(f)
    starts = (col < TS) & (col % NT == 0) | (col == TS) | (col >= 80) & ((col - 80) % P == 0)
    reset = np.broadcast_to(np.where(starts, 0, 1).astype(f), (P, T)).copy()

    def level(n, b, rows):
        s, t = np.arange(rows)[:, None], np.arange(rows)[None, :]
        if n == 0:
            return s == t
        m = (s // b == t // b) & (s % b < b // 2) & (t % b >= b // 2)
        return m & (s >= TS) if b == META and rows == 80 else m

    lvl = np.stack([level(n, LEVELS[n - 1], P) for n in range(8)], axis=1).astype(f)
    lvl0 = np.stack([level(n, LEVELS[n - 1], 80) for n in (0, 4, 5, 6, 7)], axis=1).astype(f)
    rel = REL - 1 - np.arange(RL)
    n = np.maximum(rel, 0)
    nf = np.maximum(n, 1).astype(f)
    large = 16 + (np.log(nf / f(16)) / f(math.log(8)) * f(16)).astype(np.int32)
    bucket = np.where(n < 16, n, np.minimum(large, 31))
    bucket = np.where(rel < 0, 32, bucket)
    onehot = (np.arange(33)[:, None] == bucket[None, :]).astype(f)
    block_of = [np.arange(P) // b for b in (128, 64, 32)]
    ones = np.stack([(b[:, None] == b[None, :]) for b in block_of], axis=1).astype(f)
    row = np.arange(P)
    seq_of = 2 * np.arange(4)[None, :] + row[:, None] // 64
    newmask = np.where(seq_of[:, :, None] == (np.arange(TS) // NT)[None, None, :], 0, NEG).astype(f)
    part = row // 8 % 2
    coef = np.stack([part == 0, part == 1], axis=1).astype(f)
    return dict(c_bucket=onehot, c_ones=ones, c_ident=np.eye(P, dtype=f), c_newmask=newmask, c_coef=coef,
                c_rope=rope, c_perm=perm, c_dec=dec, c_dec0=dec0, c_gq=gq, c_gk=gk, c_seq=seq,
                c_reset=reset, c_lvl=lvl, c_lvl0=lvl0)


def tiles_of(w, c0=0, n=None):
    n = w.shape[1] if n is None else n
    w = w[:, c0:c0 + n]
    return w.reshape(w.shape[0] // P, P, n // P, P).transpose(2, 1, 0, 3)


def down_units(w):
    t = tiles_of(w)
    out = np.zeros((KD, 3, P, 8, P), w.dtype)
    for u, k in enumerate(DOWN_BLOCKS):
        out[:, u, :, 0:k, :] = t[:, :, 8 * u:8 * u + k, :]
    return out.reshape(KD * 3, P, 8, P)


def per_tile(v):
    return v.reshape(-1, P).T


def layouts(a):
    f = np.float32
    out = {}
    h = np.concatenate([a["x_sample"].reshape(TS, D), a["meta_tokens"], a["x_prompt"].reshape(SEQ, D)], axis=0)
    out["h_in"] = h.T.reshape(KD, P, T).transpose(1, 0, 2)
    units = []
    low = np.zeros((DEPTH, P, 8, P), f)
    prm = np.zeros((DEPTH + 1, P, NP_), f)
    vb = np.zeros((DEPTH, 768), f)
    for l in range(DEPTH):
        w_in = a["w_in"][l]
        for f_ in (1, 2):
            pair_ = np.stack([tiles_of(a[f"ffn{f_}_gate"][l]), tiles_of(a[f"ffn{f_}_up"][l])], axis=1)
            ffn = [pair_.reshape(2 * KF, P, 8, P), down_units(a[f"ffn{f_}_down"][l])]
            if f_ == 1:
                units += ffn
                units += [tiles_of(w_in, c, 256) for c in V_COLS]
                units += [tiles_of(w_in, Z_COLS[z], P) for z in Z_ORDER]
                branch = a["w_branch"][l].reshape(8, P, KD, P).transpose(2, 1, 0, 3)
                gate = tiles_of(w_in, GATE_COL, 4 * D).reshape(4, KD, P, 8, P)
                units.append(np.concatenate([gate, branch[None]], axis=0).transpose(1, 0, 2, 3, 4).reshape(40, P, 8, P))
                units.append(tiles_of(a["w_out"][l]))
            else:
                units += ffn
        low[l, :, :, 0:16] = w_in[:, LOW_COL:LOW_COL + 16].reshape(8, P, 16).transpose(1, 0, 2)
        b = a["b_in"][l]
        vb[l] = np.concatenate([b[c:c + 256] for c in V_COLS])
        p = prm[l]
        for i, name in enumerate(("norm_ffn1", "norm_mix", "norm_ffn2")):
            p[:, P_GAIN + 8 * i:P_GAIN + 8 * i + 8] = per_tile(a[name][l])
        for i, c in enumerate(Z_COLS):
            p[:, P_ZB + i] = b[c:c + P]
        p[0:16, P_ZB + NZ] = b[LOW_COL:LOW_COL + 16]
        p[:, P_GB:P_GB + 32] = per_tile(b[GATE_COL:])
        for j in range(2):
            p[:, P_CW + CK * j:P_CW + CK * j + CK] = a["conv_w"][l][:, P * j:P * j + P].T
        for c, name in ((P_CB, "conv_b"), (P_LG, "conv_ln_g"), (P_LB, "conv_ln_b"), (P_RGN, "ret_gn"), (P_GGN, "gla_gn")):
            p[:, c:c + 2] = per_tile(a[name][l].reshape(-1))
        p[:, P_AB] = a["gla_alpha_b"][l]
        p[:, P_SUB] = np.tile(a["diff_subln"][l], 2)
        p[:, P_QN] = np.tile(a["q_norm"][l], 4)
        p[:, P_KN] = np.tile(a["k_norm"][l], 4)
        lam_init = 0.8 - 0.6 * math.exp(-0.3 * l)
        p[:, P_LI] = lam_init
        p[:, P_LI1] = 1.0 - lam_init
        for i, name in enumerate(("lam_q1", "lam_q2", "lam_k1", "lam_k2")):
            p[0:32, P_LAM + i] = a[name][l]
        p[0:16, P_AW:P_AW + P] = a["gla_alpha_w"][l]
    units.append(np.zeros((RING, P, 8, P), f))
    out["wstream"] = np.concatenate(units, axis=0).reshape(DEPTH * UNITS + RING, P, 8 * P)
    out["wlow"] = low.reshape(DEPTH, P, 8 * P)
    out["params"] = prm
    out["vbias"] = vb
    out["cache_k"] = a["cache_k"].reshape(DEPTH * POOL, PAGE, 2, P).transpose(0, 3, 2, 1).reshape(DEPTH * POOL, P, 2 * PAGE)
    out["cache_v"] = a["cache_v"].reshape(DEPTH * POOL, PAGE, 256)
    out["page_table"] = a["page_table"].reshape(1, NB * PAGES)
    sr = np.zeros((DEPTH, P, 2, NB, P), f)
    sg = np.zeros((DEPTH, P, NB, 256), f)
    for h in range(H):
        j, r = h // 2, 64 * (h % 2)
        sr[:, r:r + 64, j, :, r:r + 64] = a["state_ret"][:, :, h].transpose(0, 2, 1, 3)
        sg[:, 32 * h:32 * h + 32, :, 64 * h:64 * h + 64] = a["state_gla"][:, :, h].transpose(0, 2, 1, 3)
    out["st_ret"], out["st_gla"] = sr, sg
    out["st_conv"] = a["state_conv"].reshape(DEPTH, NB, CK - 1, 2, P).transpose(0, 4, 3, 1, 2)
    out["rel_bias"] = np.tile(np.repeat(np.concatenate([a["rel_bias"], np.full((1, H), NEG, f)], axis=0), 2, axis=1), (1, 2))
    return out


_ORDER = ["h_in", "wstream", "wlow", "params", "vbias", "cache_k", "cache_v", "page_table", "st_ret", "st_gla",
          "st_conv", "rel_bias", "c_bucket", "c_ones", "c_ident", "c_newmask", "c_coef", "c_rope", "c_perm",
          "c_dec", "c_dec0", "c_gq", "c_gk", "c_seq", "c_reset", "c_lvl", "c_lvl0"]
_OUTS = [("y_out", (P, KD, T)), ("k_out", (DEPTH, P, 2, T)), ("v_out", (DEPTH, P, WINDOWS, 256)),
         ("ret_out", (DEPTH, P, 2, P)), ("rets_out", (DEPTH, P, 2, NB, P)), ("gla_out", (DEPTH, P, 256)),
         ("glas_out", (DEPTH, P, NB, 256)), ("conv_out", (DEPTH, P, 2, CK - 1)), ("convs_out", (DEPTH, P, 2, NB, CK - 1))]


def kernel(**inputs):
    import concourse.bacc as _bacc
    from concourse.bass_utils import run_bass_kernel_spmd as _run

    nc = _bacc.Bacc("TRN2", target_bir_lowering=False, num_devices=1, dynamic_dma_scratch_size=2048)
    arrays = layouts({k: np.asarray(v) for k, v in inputs.items()})
    arrays.update(constants())
    arrays = {k: np.ascontiguousarray(v) for k, v in arrays.items()}
    args = [nc.dram_tensor(k, arrays[k].shape, mybir.dt.from_np(arrays[k].dtype), kind="ExternalInput").ap() for k in _ORDER]
    args += [nc.dram_tensor(k, shape, F32, kind="ExternalOutput").ap() for k, shape in _OUTS]
    build(nc, *args)
    r = _run(nc, [arrays], core_ids=[0]).results[0]

    y = r["y_out"].transpose(2, 1, 0).reshape(T, D)
    k = r["k_out"].transpose(0, 3, 2, 1).reshape(DEPTH, T, H, 64)
    v = r["v_out"]
    v_prompt = np.concatenate([v[:, TS:TS + META, 0], v[:, :, 1:].transpose(0, 2, 1, 3).reshape(DEPTH, SEQ, 256)], axis=1)
    ret_p = np.stack([r["ret_out"][:, 64 * (h % 2):64 * (h % 2) + 64, h // 2, 64 * (h % 2):64 * (h % 2) + 64] for h in range(H)], axis=1)
    ret_s = np.stack([r["rets_out"][:, 64 * (h % 2):64 * (h % 2) + 64, h // 2, :, 64 * (h % 2):64 * (h % 2) + 64].transpose(0, 2, 1, 3)
                      for h in range(H)], axis=2)
    gla_p = np.stack([r["gla_out"][:, 32 * h:32 * h + 32, 64 * h:64 * h + 64] for h in range(H)], axis=1)
    gla_s = np.stack([r["glas_out"][:, 32 * h:32 * h + 32, :, 64 * h:64 * h + 64].transpose(0, 2, 1, 3) for h in range(H)], axis=2)
    return (y[TS + META:].reshape(1, SEQ, D), y[:TS].reshape(NB, NT, D),
            k[:, TS:].reshape(DEPTH, 1, LP, H, 64), v_prompt.reshape(DEPTH, 1, LP, H, 64),
            k[:, :TS].reshape(DEPTH, NB, NT, H, 64), v[:, :TS, 0].reshape(DEPTH, NB, NT, H, 64),
            ret_p[:, None], ret_s, gla_p[:, None], gla_s,
            r["conv_out"].transpose(0, 3, 2, 1).reshape(DEPTH, 1, CK - 1, 256),
            r["convs_out"].transpose(0, 3, 4, 2, 1).reshape(DEPTH, NB, CK - 1, 256))
```
